# Optimizing a Trainium2 kernel written in Bass

```python
import jax, jax.numpy as jnp
from jax import lax
import numpy as np

D_MODEL = 1024
BATCH = 1
SEQ = 1024
DEPTH = 1
DEC_BATCH = 8
DEC_SEQ = 4
PAST_LEN = 8192
PAGE_SIZE = 128

D_CONV = D_MODEL // 2
D_POOL = D_MODEL - D_CONV
D_MIX = D_CONV + D_POOL
CONV_WIDTH = 31
CONV_CTX = CONV_WIDTH - 1
CONV_HEADS = 8
POOL_WINDOWS = (2, 4, 8, 16)
N_POOL_GROUPS = len(POOL_WINDOWS)
POOL_GROUP = D_POOL // N_POOL_GROUPS
POOL_CTX = max(POOL_WINDOWS) - 1
N_MEM = 256
X_HEADS = 4
X_HEAD_DIM = D_MODEL // X_HEADS
D_FF = 4 * D_MODEL
LN_EPS = 1e-5
DN_ALPHA = (2.0 * DEPTH) ** 0.25
DN_BETA = (8.0 * DEPTH) ** -0.25

kernel_name = "hybrid_conv_pool_xattn_decoder_step"

def layer_norm(x, g, b):
    xf = x.astype(jnp.float32)
    mu = jnp.mean(xf, axis=-1, keepdims=True)
    var = jnp.mean(jnp.square(xf - mu), axis=-1, keepdims=True)
    y = (xf - mu) * lax.rsqrt(var + LN_EPS)
    return (y * g.astype(jnp.float32) + b.astype(jnp.float32)).astype(x.dtype)

def group_norm_tokens(x, g, b):
    B, T, C = x.shape
    xf = x.astype(jnp.float32).reshape(B, T, CONV_HEADS, C // CONV_HEADS)
    mu = jnp.mean(xf, axis=-1, keepdims=True)
    var = jnp.mean(jnp.square(xf - mu), axis=-1, keepdims=True)
    y = ((xf - mu) * lax.rsqrt(var + LN_EPS)).reshape(B, T, C)
    return (y * g.astype(jnp.float32) + b.astype(jnp.float32)).astype(x.dtype)

def conv_branch(u, ctx, conv_w, conv_b, gn_g, gn_b):
    u_ext = jnp.concatenate([ctx.astype(u.dtype), u], axis=1)
    y = lax.conv_general_dilated(
        u_ext, conv_w[:, None, :].astype(u.dtype), window_strides=(1,), padding="VALID",
        dimension_numbers=("NWC", "WIO", "NWC"), feature_group_count=D_CONV)
    y = group_norm_tokens(y + conv_b, gn_g, gn_b)
    return jax.nn.silu(y), u_ext[:, -CONV_CTX:]

def pool_branch(p, ctx, pos0, pool_w, pool_scale):
    B, T, _ = p.shape
    p_ext = jnp.concatenate([ctx.astype(p.dtype), p], axis=1)
    L = p_ext.shape[1]
    pf = p_ext.astype(jnp.float32).reshape(B, L, N_POOL_GROUPS, POOL_GROUP)
    csum = jnp.cumsum(pf, axis=1)
    pos = pos0 + jnp.arange(T)
    means = []
    for gi, w in enumerate(POOL_WINDOWS):
        c = csum[:, :, gi]
        c_shift = jnp.pad(c, ((0, 0), (w, 0), (0, 0)))[:, :L]
        win_sum = (c - c_shift)[:, POOL_CTX:]
        count = jnp.minimum(pos + 1, w).astype(jnp.float32)[None, :, None]
        means.append(win_sum / count)
    mean = jnp.stack(means, axis=2)
    delta = (mean - pf[:, POOL_CTX:]).astype(p.dtype)
    mixed = jnp.einsum("btgc,gcd->btgd", delta, pool_w).reshape(B, T, D_POOL)
    return mixed * pool_scale, p_ext[:, -POOL_CTX:]

def mem_kv(mem, xk_w, xv_w):
    B, M, _ = mem.shape
    k = (mem @ xk_w).reshape(B, M, X_HEADS, X_HEAD_DIM)
    v = (mem @ xv_w).reshape(B, M, X_HEADS, X_HEAD_DIM)
    return k, v

def cross_attn(x, k, v, xq_w, xo_w):
    B, T, _ = x.shape
    q = (x @ xq_w).reshape(B, T, X_HEADS, X_HEAD_DIM)
    s = jnp.einsum("bthd,bmhd->bhtm", q, k.astype(q.dtype)).astype(jnp.float32) * (X_HEAD_DIM ** -0.5)
    a = jax.nn.softmax(s, axis=-1).astype(x.dtype)
    o = jnp.einsum("bhtm,bmhd->bthd", a, v.astype(x.dtype)).reshape(B, T, D_MODEL)
    return o @ xo_w

def decoder_layer(x, conv_ctx, pool_ctx, mem_k, mem_v, pos0,
                  w_in, b_in, conv_w, conv_b, gn_g, gn_b, pool_w, pool_scale, w_out,
                  ln1_g, ln1_b, xq_w, xo_w, ln2_g, ln2_b, w1, b1, w2, b2, ln3_g, ln3_b):
    h = x @ w_in + b_in
    a, g, p = jnp.split(h, [D_CONV, 2 * D_CONV], axis=-1)
    u = a * jax.nn.sigmoid(g)
    o_conv, conv_new = conv_branch(u, conv_ctx, conv_w, conv_b, gn_g, gn_b)
    o_pool, pool_new = pool_branch(p, pool_ctx, pos0, pool_w, pool_scale)
    mix = jnp.concatenate([o_conv, o_pool], axis=-1) @ w_out
    x = layer_norm(DN_ALPHA * x + mix, ln1_g, ln1_b)
    x = layer_norm(DN_ALPHA * x + cross_attn(x, mem_k, mem_v, xq_w, xo_w), ln2_g, ln2_b)
    f = jnp.square(jax.nn.relu(x @ w1 + b1)) @ w2 + b2
    x = layer_norm(DN_ALPHA * x + f, ln3_g, ln3_b)
    return x, conv_new, pool_new

def setup_inputs(seed: int = 0) -> dict:
    key = jax.random.key(seed)
    ks = iter(jax.random.split(key, 40))
    nrm = lambda shape, scale: jax.random.normal(next(ks), shape, jnp.float32) * scale
    d_in = 2 * D_CONV + D_POOL
    return {
        "x_prompt": nrm((BATCH, SEQ, D_MODEL), 1.0),
        "x_sample": nrm((DEC_BATCH, DEC_SEQ, D_MODEL), 1.0),
        "mem_prompt": nrm((BATCH, N_MEM, D_MODEL), 1.0),
        "cache_mem_k": nrm((DEPTH, DEC_BATCH, N_MEM, X_HEADS, X_HEAD_DIM), 1.0),
        "cache_mem_v": nrm((DEPTH, DEC_BATCH, N_MEM, X_HEADS, X_HEAD_DIM), DN_BETA),
        "state_conv": nrm((DEPTH, DEC_BATCH, CONV_CTX, D_CONV), 0.5),
        "state_pool": nrm((DEPTH, DEC_BATCH, POOL_CTX, D_POOL), 1.0),
        "w_in": nrm((DEPTH, D_MODEL, d_in), D_MODEL ** -0.5),
        "b_in": nrm((DEPTH, d_in), 0.02),
        "conv_w": nrm((DEPTH, CONV_WIDTH, D_CONV), CONV_WIDTH ** -0.5),
        "conv_b": nrm((DEPTH, D_CONV), 0.02),
        "gn_g": 1.0 + nrm((DEPTH, D_CONV), 0.02),
        "gn_b": nrm((DEPTH, D_CONV), 0.02),
        "pool_w": nrm((DEPTH, N_POOL_GROUPS, POOL_GROUP, POOL_GROUP), POOL_GROUP ** -0.5),
        "pool_scale": 1.0 + nrm((DEPTH, D_POOL), 0.1),
        "w_out": nrm((DEPTH, D_MIX, D_MODEL), D_MIX ** -0.5 * DN_BETA),
        "ln1_g": 1.0 + nrm((DEPTH, D_MODEL), 0.02),
        "ln1_b": nrm((DEPTH, D_MODEL), 0.02),
        "xq_w": nrm((DEPTH, D_MODEL, D_MODEL), D_MODEL ** -0.5),
        "xk_w": nrm((DEPTH, D_MODEL, D_MODEL), D_MODEL ** -0.5),
        "xv_w": nrm((DEPTH, D_MODEL, D_MODEL), D_MODEL ** -0.5 * DN_BETA),
        "xo_w": nrm((DEPTH, D_MODEL, D_MODEL), D_MODEL ** -0.5 * DN_BETA),
        "ln2_g": 1.0 + nrm((DEPTH, D_MODEL), 0.02),
        "ln2_b": nrm((DEPTH, D_MODEL), 0.02),
        "w1": nrm((DEPTH, D_MODEL, D_FF), D_MODEL ** -0.5),
        "b1": nrm((DEPTH, D_FF), 0.02),
        "w2": nrm((DEPTH, D_FF, D_MODEL), D_FF ** -0.5 * DN_BETA),
        "b2": nrm((DEPTH, D_MODEL), 0.02),
        "ln3_g": 1.0 + nrm((DEPTH, D_MODEL), 0.02),
        "ln3_b": nrm((DEPTH, D_MODEL), 0.02),
    }

def reference(x_prompt, x_sample, mem_prompt, cache_mem_k, cache_mem_v, state_conv, state_pool,
              w_in, b_in, conv_w, conv_b, gn_g, gn_b, pool_w, pool_scale, w_out,
              ln1_g, ln1_b, xq_w, xk_w, xv_w, xo_w, ln2_g, ln2_b, w1, b1, w2, b2, ln3_g, ln3_b):
    n_prompt = x_prompt.shape[0]
    hp, hs = x_prompt, x_sample
    mk_p, mv_p, conv_p, conv_s, pool_p, pool_s = [], [], [], [], [], []
    for l in range(DEPTH):
        lw = (w_in[l], b_in[l], conv_w[l], conv_b[l], gn_g[l], gn_b[l], pool_w[l], pool_scale[l],
              w_out[l], ln1_g[l], ln1_b[l], xq_w[l], xo_w[l], ln2_g[l], ln2_b[l],
              w1[l], b1[l], w2[l], b2[l], ln3_g[l], ln3_b[l])
        k_p, v_p = mem_kv(mem_prompt, xk_w[l], xv_w[l])
        hp, c_p, q_p = decoder_layer(
            hp, jnp.zeros((n_prompt, CONV_CTX, D_CONV), hp.dtype),
            jnp.zeros((n_prompt, POOL_CTX, D_POOL), hp.dtype), k_p, v_p, 0, *lw)
        hs, c_s, q_s = decoder_layer(
            hs, state_conv[l], state_pool[l], cache_mem_k[l], cache_mem_v[l], PAST_LEN, *lw)
        mk_p.append(k_p)
        mv_p.append(v_p)
        conv_p.append(c_p)
        conv_s.append(c_s)
        pool_p.append(q_p)
        pool_s.append(q_s)
    return (hp, hs, jnp.stack(mk_p), jnp.stack(mv_p), jnp.stack(conv_p), jnp.stack(conv_s),
            jnp.stack(pool_p), jnp.stack(pool_s))


_drawn_inputs = setup_inputs


def setup_inputs(seed=0):
    import zlib

    import numpy as np

    out = dict(_drawn_inputs(seed))
    spreads = {}
    factors = {'b_in': 2.689,
     'conv_b': 6.293,
     'gn_g': 21.4,
     'gn_b': 22.128,
     'ln1_g': 2.729,
     'ln1_b': 2.741,
     'ln2_g': 2.706,
     'ln2_b': 2.747,
     'b1': 4.62,
     'b2': 18.826,
     'ln3_g': 7.581,
     'ln3_b': 8.015,
     'pool_scale': 3.84}
    for name, (base, spread) in spreads.items():
        noise = np.random.default_rng([zlib.crc32(name.encode()), seed]).standard_normal(out[name].shape)
        drawn = base * np.exp(spread * noise) if base else spread * noise
        out[name] = __import__('jax').numpy.asarray(drawn.astype(out[name].dtype))
    for name, factor in factors.items():
        out[name] = (out[name] * factor).astype(out[name].dtype)
    return out
```

```python
from contextlib import ExitStack

import concourse.bass as bass
from concourse import mybir

P = 128
D = 1024
NB = D // P
TP = 1024
SB, ST = 8, 4
TS = SB * ST
T = TP + TS
D_CONV = 512
CB = D_CONV // P
PB = 4
TAPS = 31
CTX = TAPS - 1
WINDOWS = (2, 4, 8, 16)
PCTX = 15
NMEM = 256
HEADS = 4
FF = 4096
FFG = 4
GB = FF // P // FFG
ALPHA = 2.0 ** 0.25
SCALE = 256.0 ** -0.5
EPS = 1e-5
CHUNKS = ((0, 384), (384, 768), (768, 1056))
TILES = tuple(128 * t for t in range(8)) + (T - P,)
NT = len(TILES)
SLAB = NB * P

EXT = TP + CTX
DEXT = ST + CTX
PEXT = TP + PCTX
DPEXT = ST + PCTX
BLK = 2 * T

S_K, S_A, S_P0, S_V, S_P2, S_E1, S_E2, S_XQ, S_XO, S_FF = 0, 8, 16, 18, 26, 28, 32, 36, 44, 52
NSLAB = S_FF + FFG * 2 * GB

COLS = {}
_at = 0
for _name, _n in (("conv_w", CB * TAPS), ("b_in", 12), ("conv_b", 4), ("gn_g", 4), ("gn_b", 4), ("pool_scale", 4),
                  ("ln1_g", 8), ("ln1_b", 8), ("ln2_g", 8), ("ln2_b", 8), ("ln3_g", 8), ("ln3_b", 8),
                  ("b1", 32), ("b2", 8), ("ramp", 4 * 16), ("eps", 1), ("inv_d", 1), ("half", 2)):
    COLS[_name] = _at
    _at += _n
NPAR = _at
NCONST = 3 * P


SIX = {b: 1 for b in range(6)}
LN_MEAN = {6: 2, 7: 1}


def times(n, banks):
    return {b: n * k for b, k in banks.items()}


LINEAR = (times(4, SIX), (2, 5))
ONE_BANK = ({0: 4, 3: 4}, (0, 3))
ONE_PAIR = (SIX, (2, 5))
HALVES = (times(4, SIX), (5,))
STAGES = [("K", *ONE_BANK), ("A", *LINEAR), ("P0", *ONE_PAIR), ("V", *ONE_BANK), ("P2", *ONE_PAIR),
          ("PM", times(2, SIX), ()), ("E1", *HALVES), ("GM", times(2, SIX), ()), ("GS", {6: 1}, ()),
          ("GT", times(2, SIX), ()), ("E2", *HALVES), ("C1", LN_MEAN, ()), ("S1", {6: 1}, ()), ("T1", SIX, ()),
          ("XQ", *LINEAR), ("ATT", {0: 4, 1: 4, 2: 4, 3: 4, 4: 8, 5: 8, 6: 8, 7: 8}, ()),
          ("DEC", {0: 1, 1: 1, 2: 1, 3: 1}, (0, 3)), ("XO", *LINEAR), ("C2", LN_MEAN, ()), ("S2", {6: 1}, ()),
          ("T2", SIX, ())]
for _g in range(FFG):
    STAGES += [(f"W1{_g}", *LINEAR), (f"W2{_g}", *LINEAR)]
STAGES += [("C3", LN_MEAN, ()), ("S3", {6: 1}, ()), ("T3", SIX, ())]
FREED, FILLED = {}, {}
_n, _f = {b: 0 for b in range(8)}, {b: 0 for b in range(8)}
for _name, _uses, _silent in STAGES:
    FREED[_name], FILLED[_name] = dict(_n), dict(_f)
    for _b, _k in _uses.items():
        _n[_b] += _k
        _f[_b] += 0 if _b in _silent else _k


def decoder_step(nc, xT, memT, slabs, pool_w, params, consts, conv_state, pool_state, dec_kv,
                 yT, kT, v_out, conv_p, conv_s, pool_p, pool_s):
    f32, f32r = mybir.dt.float32, mybir.dt.float32r
    ALU = mybir.AluOpType
    ACT = mybir.ActivationFunctionType
    AX = mybir.AxisListType.X
    ctx = ExitStack()

    BASE = 16512
    O_XH = BASE
    O_XL = O_XH + NB * T * 4
    O_Q = O_XL + NB * T * 4
    O_W = O_Q + NB * BLK * 4
    O_KV = O_W + 6 * SLAB * 4
    O_S = O_KV + 32768
    O_PAR = O_S + 4 * T * 4
    O_CON = O_PAR + -(-NPAR // 8) * 32
    O_SMALL = O_CON + NCONST * 4

    def at(name, shape, dt, offset):
        return nc.alloc_sbuf_tensor_at(name, shape, dt, offset=offset)

    xh = at("x_high", [P, NB, T], f32r, O_XH)
    xl = at("x_low", [P, NB, T], f32r, O_XL)
    xf = at("x_full", [P, NB, T], f32, O_XL)
    q = at("mix", [P, NB, 2, T], f32r, O_Q)
    qf = at("mix_full", [P, NB, BLK], f32, O_Q)
    mem = at("mem", [P, 2, NB, NMEM], f32r, O_Q + 6 * BLK * 4)
    memf = at("mem_full", [P, 2, NB, NMEM], f32, O_Q + 6 * BLK * 4)
    raw = at("w_raw", [P, 2, SLAB], f32, O_W)
    wh = at("w_high", [P, 2, SLAB], f32r, O_W + 2 * SLAB * 4)
    wl = at("w_low", [P, 2, SLAB], f32r, O_W + 4 * SLAB * 4)
    kh = at("k_high", [P, NB, NMEM], f32r, O_KV)
    kl = at("k_low", [P, NB, NMEM], f32r, O_KV + 8192)
    kf = at("k_full", [P, NB, NMEM], f32, O_KV + 8192)
    vh = at("v_high", [P, 2, D], f32r, O_KV + 16384)
    vl = at("v_low", [P, 2, D], f32r, O_KV + 24576)
    vf = at("v_full", [P, 2, D], f32, O_KV + 24576)
    s = at("scratch", [P, 4, T], f32, O_S)
    prob = at("prob", [P, 2, HEADS * NMEM], f32, O_S)
    pth = at("prob_t_high", [P, 8, P], f32r, O_S + 8192)
    ptl = at("prob_t_low", [P, 8, P], f32r, O_S + 12288)
    spread = at("gn_spread", [P, 3, NT, P], f32, O_S)
    lnspread = at("ln_spread", [P, 2, NT, P], f32, O_Q)
    dkv = at("dec_kv", [P, 4, 2048], f32, O_XH)
    qd = at("dec_q", [P, NB, TS], f32, O_XH + 4 * 8192)
    acc = at("ffn_sum", [P, NB, T], f32, O_KV)
    relu = at("relu", [P, 2, T], f32, O_KV + NB * T * 4)
    s3 = at("ln3_scratch", [P, 4, T], f32, O_XH)
    par = at("params", [P, NPAR], f32, O_PAR)
    con = at("consts", [P, NCONST], f32, O_CON)
    small = at("small", [P, 80], f32, O_SMALL)
    poolw = qf[:, CB - 1, BLK - PB * P:BLK]

    inv128, inv64, ident = con[:, 0:P], con[:, P:2 * P], con[:, 2 * P:3 * P]

    def col(name, i=0, n=1):
        c = COLS[name] + i
        return par[:, c:c + n] if isinstance(c, int) else par[:, bass.ds(c, n)]

    ps = [ctx.enter_context(nc.psum_tensor(f"bank{b}", [P, 512], f32)) for b in range(8)]
    ps_pair = None

    sems = {}

    def sem(name):
        if name not in sems:
            sems[name] = ctx.enter_context(nc.semaphore(name))
        return sems[name]

    full = [sem(f"bank_full{b}") for b in range(8)]
    free = [sem(f"bank_free{b}") for b in range(8)]
    split_done, used = sem("split_done"), sem("slab_used")

    class Own:

        def __init__(self, eng, name):
            self.eng, self.sem, self.n = eng, sem(name), 0

        def done(self, ins):
            ins.then_inc(self.sem, 1)
            self.n += 1
            return self.n

        def wait(self, n=None):
            self.eng.wait_ge(self.sem, self.n if n is None else n)

        def link(self, ins):
            self.done(ins)
            self.wait()

    def conv_dec(i):
        return qf[:, i, EXT:EXT + SB * DEXT].rearrange("p (b n) -> p b n", b=SB)

    def pool_dec(g):
        return qf[:, CB + g, PEXT:PEXT + SB * DPEXT].rearrange("p (b n) -> p b n", b=SB)

    def by_request(ap):
        return ap.rearrange("p (b n) -> p b n", b=SB)

    def over_blocks(ap, n=NB):
        return ap.unsqueeze(1).broadcast_to([P, n, ap.shape[-1]])

    def slab_arrived(eng, stage, n, p, c, i, last=2):
        b = 3 * p + c
        if c == last:
            eng.wait_ge(used, n + 1)
        else:
            eng.wait_ge(full[b], FILLED[stage][b] + i + 1)
        return b

    ctx.enter_context(nc.allow_non_contiguous_dma(reason="the state's rows are short"))
    block = ctx.enter_context(nc.Block())

    @block.sync
    def _(sp):
        def load(n, p):
            sp.dma_start(raw[:, p, :], slabs[bass.ds(n, 1)].rearrange("a p n -> p (a n)")).then_inc(sem(f"raw_in{p}"), 16)

        load(0, 0)
        load(1, 1)
        with sp.Fori(1, (S_XO + 4) // 2) as i:
            for p in range(2):
                sp.wait_ge(split_done, 2 * i + p - 1)
                load(2 * i + p, p)
        sp.wait_ge(sem("x_restored"), 2 * NB)
        for n in range(16):
            if n >= 4:
                sp.wait_ge(sem("dec_used"), n - 3)
            sp.dma_start(dkv[:, n % 4, :], dec_kv[n]).then_inc(sem(f"dec_in{n % 4}"), 16)
        with sp.Fori((S_XO + 4) // 2, NSLAB // 2) as i:
            for p in range(2):
                sp.wait_ge(split_done, 2 * i + p - 1)
                load(2 * i + p, p)
        for c, (a, z) in enumerate(CHUNKS):
            sp.wait_ge(sem("y_ready"), c + 1)
            sp.dma_start(yT[:, :, a:z], xf[:, :, a:z]).then_inc(sem("y_out"), 16)
        sp.wait_ge(sem("y_out"), 48)
        sp.wait_ge(sem("k_out"), 16)
        sp.wait_ge(sem("v_out"), 16)
        sp.wait_ge(sem("conv_out"), 32 * CB)
        for g in range(PB):
            sp.wait_ge(sem(f"pool_out{g}"), 32)

    @block.gpsimd
    def _(pool):
        high_done = sem("high_done")

        def split(n, p, turn):
            pool.wait_ge(sem(f"raw_in{p}"), 16 * (turn + 1))
            if not (isinstance(n, int) and n < 2):
                pool.wait_ge(used, n - 1)
                pool.sem_inc(sem("slot_turned"), 1)
            pool.tensor_copy(wh[:, p, :], raw[:, p, :]).then_inc(high_done, 1)
            pool.wait_ge(high_done, n + 1)
            pool.tensor_tensor(wl[:, p, :], raw[:, p, :], wh[:, p, :].bitcast(f32), ALU.subtract).then_inc(split_done, 1)

        def splits(lo, hi):
            with pool.Fori(lo // 2, hi // 2) as i:
                for p in range(2):
                    split(2 * i + p, p, i)

        def restore(b):
            pool.tensor_tensor(xf[:, b, :], xh[:, b, :].bitcast(f32), xl[:, b, :].bitcast(f32), ALU.add)\
                .then_inc(sem("x_restored"), 1)

        split(0, 0, 0)
        split(1, 1, 0)
        pool.memset(qf[:, 0:CB, 0:CTX], 0.0).then_inc(sem("pad_done"), 1)
        pool.memset(qf[:, CB:CB + 2, 0:PCTX], 0.0).then_inc(sem("pad_done"), 1)
        splits(2, 10)
        for i in range(CB):
            split(10 + 2 * i, 0, 5 + i)
            for b in range(6):
                pool.wait_ge(free[b], FREED["A"][b] + i + 1)
            pool.tensor_tensor(qf[:, i, CTX:EXT], s[:, 3, 0:TP], s[:, 2, 0:TP], ALU.mult).then_inc(sem("u_done"), 1)
            pool.tensor_tensor(conv_dec(i)[:, :, CTX:DEXT], by_request(s[:, 3, TP:T]), by_request(s[:, 2, TP:T]),
                               ALU.mult).then_inc(sem("u_done"), 1)
            split(11 + 2 * i, 1, 5 + i)
        splits(18, 28)
        pool.memset(qf[:, CB + 2:CB + 4, 0:PCTX], 0.0).then_inc(sem("pad_done"), 1)
        pool.wait_ge(used, S_E1)
        restore(0)
        restore(1)
        split(28, 0, 14)
        split(29, 1, 14)
        for b in range(2, NB):
            restore(b)
        splits(30, 46)
        pool.wait_ge(used, S_XQ + 8)
        for b in range(NB):
            restore(b)
        splits(46, NSLAB)

    @block.tensor
    def _(pe):
        def take(b, n):
            if not (isinstance(n, int) and n == 0):
                pe.wait_ge(free[b], n)

        def product(out, w_high, w_low, x_high, x_low, first, last):
            pe.matmul(out, w_high, x_high, start=first, stop=False)
            pe.matmul(out, w_high, x_low, start=False, stop=False)
            return pe.matmul(out, w_low, x_high, start=False, stop=last)

        def slab(stage, n, p, i, parts, chunks=CHUNKS, ready=None):
            pe.wait_ge(split_done, n + 1)
            for c, (a, z) in enumerate(chunks):
                b = 3 * p + c
                take(b, FREED[stage][b] + i)
                for k in range(NB):
                    if ready:
                        ready(c, k)
                    w = slice(k * P, (k + 1) * P)
                    high, low = parts(k, a, z)
                    last = product(ps[b][:, 0:z - a], wh[:, p, w], wl[:, p, w], high, low, k == 0, k == NB - 1)
                last.then_inc(used if c == len(chunks) - 1 else full[b], 1)

        def x_parts(k, a, z):
            return xh[:, k, a:z], xl[:, k, a:z]

        def q_parts(k, a, z):
            return q[:, k, 0, a:z], q[:, k, 1, a:z]

        def mem_parts(k, a, z):
            return mem[:, 0, k, a:z], mem[:, 1, k, a:z]

        def pairs(stage, n0, lo, hi, parts, chunks=CHUNKS, ready=None):
            with pe.Fori(lo, hi) as i:
                for p in range(2):
                    slab(stage, n0 + 2 * i + p, p, i, parts, chunks, ready)

        def first_pair(stage, n0, parts, chunks=CHUNKS, ready=None):
            for p in range(2):
                slab(stage, n0 + p, p, 0, parts, chunks, ready if p == 0 else None)

        MEM = ((0, NMEM),)
        pe.wait_ge(sem("mem_low"), 1)
        first_pair("K", S_K, mem_parts, MEM)
        pairs("K", S_K, 1, 4, mem_parts, MEM)

        def x_ready(c, k):
            if c == 0:
                pe.wait_ge(sem("x_low"), k + 1)

        first_pair("A", S_A, x_parts, ready=x_ready)
        pairs("A", S_A, 1, 4, x_parts)
        first_pair("P0", S_P0, x_parts)

        with pe.Fori(0, 4) as i:
            for p in range(2):
                pe.wait_ge(split_done, S_V + 2 * i + p + 1)
                b = 3 * p
                take(b, FREED["V"][b] + i)
                for mt in range(2):
                    m = slice(mt * P, (mt + 1) * P)
                    for k in range(NB):
                        w = slice(k * P, (k + 1) * P)
                        last = product(ps[b][:, m], mem[:, 0, k, m], mem[:, 1, k, m], wh[:, p, w], wl[:, p, w],
                                       k == 0, k == NB - 1)
                last.then_inc(used, 1)
        first_pair("P2", S_P2, x_parts)

        pe.wait_ge(sem("pool_w_in"), 16)
        for g in range(PB):
            pe.wait_ge(sem("delta_done"), 2 * (g + 1))
            for c, (a, z) in enumerate(CHUNKS):
                b = 3 * (g % 2) + c
                take(b, FREED["PM"][b] + g // 2)
                w = poolw[:, g * P:(g + 1) * P]
                zp = min(z, TP)
                last = pe.matmul(ps[b][:, 0:zp - a], w, qf[:, CB + g, PCTX + a:PCTX + zp], start=True, stop=True)
                if z > TP:
                    last = pe.matmul(ps[b][:, zp - a:z - a], w, pool_dec(g)[:, :, PCTX:DPEXT], start=True, stop=True)
                last.then_inc(full[b], 1)

        def half(stage, n0, k0):
            with pe.Fori(0, 2) as i:
                for p in range(2):
                    pe.wait_ge(split_done, n0 + 2 * i + p + 1)
                    for m in range(2):
                        for c, (a, z) in enumerate(CHUNKS):
                            b = 3 * m + c
                            take(b, FREED[stage][b] + 2 * i + p)
                            for k in range(4):
                                w = slice((m * 4 + k) * P, (m * 4 + k + 1) * P)
                                last = product(ps[b][:, 0:z - a], wh[:, p, w], wl[:, p, w],
                                               *q_parts(k0 + k, a, z), k == 0, k == 3)
                            last.then_inc(used if b == 5 else full[b], 1)

        pe.wait_ge(sem("mix_low"), PB)
        half("E1", S_E1, CB)

        def spread_back(stage, bank, i, c, tiles):
            take(bank, FREED[stage][bank] + i)
            for t in range(3 * c, min(3 * c + 3, NT)):
                o = TILES[t] - CHUNKS[c][0]
                last = pe.transpose(ps[bank][:, o:o + P], tiles[:, t, :], ident)
            last.then_inc(full[bank], 1)

        for i in range(CB):
            pe.wait_ge(sem("conv_kept"), i + 1)
            for c, (a, z) in enumerate(CHUNKS):
                b = 3 * (i % 2) + c
                take(b, FREED["GM"][b] + i // 2)
                pe.matmul(ps[b][:, 0:z - a], inv64, qf[:, i, a:z], start=True, stop=True).then_inc(full[b], 1)
        take(6, FREED["GS"][6])
        for i in range(CB):
            pe.wait_ge(sem("gn_sq"), i + 1)
            for t, t0 in enumerate(TILES):
                o = (i * NT + t) * 2
                last = pe.matmul(ps[6][:, o:o + 2], qf[:, i, T + t0:T + t0 + P], col("half", 0, 2), start=True, stop=True)
        last.then_inc(full[6], 1)
        for i in range(CB):
            pe.wait_ge(sem("gn_spread"), i + 1)
            for c in range(3):
                spread_back("GT", 3 * (i % 2) + c, i // 2, c, spread[:, i % 3])
        pe.wait_ge(sem("mix_low"), PB + CB)
        half("E2", S_E2, 0)

        def ln_first_mean(n, x0):
            for c, (a, z) in enumerate(CHUNKS):
                b = 6 + c % 2
                take(b, FREED[f"C{n}"][b] + c // 2)
                pe.matmul(ps[b][:, 0:z - a], inv128, x0(a, z), start=True, stop=True).then_inc(full[b], 1)

        def ln_stats(n, sums, squares):
            pe.wait_ge(sem("ln_sums"), n)
            take(6, FREED[f"S{n}"][6])
            for j, src in enumerate((sums, squares)):
                for t, t0 in enumerate(TILES):
                    last = pe.matmul(ps[6][:, j * NT + t:j * NT + t + 1], src[:, t0:t0 + P], col("inv_d"),
                                     start=True, stop=True)
            last.then_inc(full[6], 1)
            pe.wait_ge(sem("ln_spread"), 2 * n)
            for c in range(3):
                for j in range(2):
                    spread_back(f"T{n}", 3 * j + c, 0, c, lnspread[:, j])

        pe.wait_ge(sem("ln_y"), 8)
        ln_first_mean(1, lambda a, z: xf[:, 0, a:z])
        ln_stats(1, s[:, 0, :], s[:, 1, :])

        def x_normed(n):
            def ready(c, k):
                if k == 0:
                    pe.wait_ge(sem("x_norm_low"), 3 * (n - 1) + c + 1)
            return ready

        first_pair("XQ", S_XQ, x_parts, ready=x_normed(1))
        pairs("XQ", S_XQ, 1, 4, x_parts)

        def scores(t):
            for h in range(HEADS):
                b = 2 * (t % 2) + h // 2
                if h % 2 == 0:
                    take(b, FREED["ATT"][b] + t // 2)
                o = (h % 2) * NMEM
                for k in range(2):
                    f = 2 * h + k
                    tok = slice(t * P, (t + 1) * P)
                    last = product(ps[b][:, o:o + NMEM], q[:, f, 0, tok], q[:, f, 1, tok], kh[:, f, :], kl[:, f, :],
                                   k == 0, k == 1)
                if h % 2 == 1:
                    last.then_inc(full[b], 1)

        def prob_transposes(t):
            pe.wait_ge(sem("prob_done"), t + 1)
            for j in range(8):
                b = 4 + j // 4
                if j % 4 == 0:
                    take(b, FREED["ATT"][b] + t)
                last = pe.transpose(ps[b][:, (j % 4) * P:(j % 4 + 1) * P], prob[:, t % 2, j * P:(j + 1) * P], ident)
                if j % 4 == 3:
                    last.then_inc(full[b], 1)

        def values(t):
            pe.wait_ge(sem("prob_t_low"), 2 * (t + 1))
            for f in range(NB):
                b = 6 + f // 4
                if f % 4 == 0:
                    take(b, FREED["ATT"][b] + t)
                for mt in range(2):
                    w = slice(f * P, (f + 1) * P)
                    j = 2 * (f // 2) + mt
                    last = product(ps[b][:, (f % 4) * P:(f % 4 + 1) * P], vh[:, mt, w], vl[:, mt, w],
                                   pth[:, j, :], ptl[:, j, :], mt == 0, mt == 1)
                if f % 4 == 3:
                    last.then_inc(full[b], 1)

        pe.wait_ge(sem("q_low"), 24)
        pe.wait_ge(sem("kv_low"), 2)
        scores(0)
        for t in range(8):
            if t + 1 < 8:
                scores(t + 1)
            prob_transposes(t)
            if t >= 1:
                values(t - 1)
        values(7)

        pe.wait_ge(sem("dec_q"), 1)
        take(0, FREED["DEC"][0])
        for n in range(SB):
            pe.wait_ge(sem(f"dec_in{n % 4}"), 16 * (n // 4 + 1))
            for h in range(HEADS):
                for mt in range(2):
                    o = mt * P + h * TS + n * ST
                    for k in range(2):
                        f = 2 * h + k
                        m0 = f * NMEM + mt * P
                        last = pe.matmul(ps[0][:, o:o + ST], dkv[:, n % 4, m0:m0 + P], qd[:, f, n * ST:(n + 1) * ST],
                                         start=(k == 0), stop=(k == 1))
            last.then_inc(sem("dec_used"), 1)
        take(1, FREED["DEC"][1])
        pe.wait_ge(sem("dec_s"), 1)
        for mt in range(2):
            last = pe.transpose(ps[1][:, mt * P:(mt + 1) * P], prob[:, 0, mt * P:(mt + 1) * P], ident)
        last.then_inc(full[1], 1)
        take(2, FREED["DEC"][2])
        pe.wait_ge(sem("prob_done"), 9)
        for mt in range(2):
            last = pe.transpose(ps[2][:, mt * P:(mt + 1) * P], prob[:, 1, mt * P:(mt + 1) * P], ident)
        last.then_inc(full[2], 1)
        take(3, FREED["DEC"][3])
        pe.wait_ge(sem("dec_p"), 1)
        for n in range(SB):
            c = SB + n
            pe.wait_ge(sem(f"dec_in{c % 4}"), 16 * (c // 4 + 1))
            for f in range(NB):
                for mt in range(2):
                    m0 = mt * D + f * P
                    o = mt * P + (f // 2) * TS + n * ST
                    last = pe.matmul(ps[3][:, f * TS + n * ST:f * TS + (n + 1) * ST], dkv[:, c % 4, m0:m0 + P],
                                     prob[:, 0, 512 + o:512 + o + ST], start=(mt == 0), stop=(mt == 1))
            last.then_inc(sem("dec_used"), 1)

        pe.wait_ge(sem("o_low"), 2 * 8 + 1)
        first_pair("XO", S_XO, q_parts)
        pe.wait_ge(sem("ln_y"), 9)
        ln_first_mean(2, lambda a, z: xf[:, 0, a:z])
        pairs("XO", S_XO, 1, 4, q_parts)
        ln_stats(2, s[:, 0, :], s[:, 1, :])

        for g in range(FFG):
            n0 = S_FF + g * 2 * GB
            first_pair(f"W1{g}", n0, x_parts, ready=x_normed(2) if g == 0 else None)
            pairs(f"W1{g}", n0, 1, 4, x_parts)

            def hidden_ready(c, k, g=g):
                if k == 0:
                    pe.wait_ge(sem("hidden_low"), 24 * g + 21)
                if k == NB - 1:
                    pe.wait_ge(sem("hidden_low"), 24 * g + 21 + c + 1)

            first_pair(f"W2{g}", n0 + GB, q_parts, ready=hidden_ready)
            if g == FFG - 1:
                pe.wait_ge(sem("ln_y"), 10)
                ln_first_mean(3, lambda a, z: xf[:, 0, a:z])
            pairs(f"W2{g}", n0 + GB, 1, 4, q_parts)
        ln_stats(3, s3[:, 0, :], s3[:, 1, :])

    @block.scalar
    def _(act):
        own = Own(act, "act_own")

        def load(out, in_, name):
            act.dma_start(out, in_).then_inc(sem(name), 16)

        load(memf[:, 1], memT, "mem_in")
        load(par[:], params, "const_in")
        load(con[:], consts, "const_in")
        for b in range(NB):
            load(xf[:, b, :], xT[:, b, :], f"x_in{b}")
        for i in range(CB):
            load(conv_dec(i)[:, :, 0:CTX], conv_state[:, i], "conv_state_in")
        for g in range(2):
            load(pool_dec(g)[:, :, 0:PCTX], pool_state[:, g], "pool_state_in")
        load(poolw, pool_w, "pool_w_in")

        act.wait_ge(sem("mem_in"), 16)
        act.copy(mem[:, 0], memf[:, 1]).then_inc(sem("mem_high"), 1)
        for j in range(NB):
            b = slab_arrived(act, "K", S_K + j, j % 2, 0, j // 2, last=0)
            act.copy(kf[:, j, :], ps[b][:, 0:NMEM]).then_inc(sem("k_full"), 1)
            act.copy(kh[:, j, :], ps[b][:, 0:NMEM]).then_inc(free[b], 1)
            act.wait_ge(sem(f"x_in{j}"), 16)
            act.copy(xh[:, j, :], xf[:, j, :]).then_inc(sem("x_high"), 1)
        act.wait_ge(sem("k_full"), NB)
        act.dma_start(kT, kf[:]).then_inc(sem("k_out"), 16)

        act.wait_ge(sem("const_in"), 32)
        for i in range(CB):
            if i >= 1:
                act.wait_ge(sem("u_done"), 2 * i)
            for c, (a, z) in enumerate(CHUNKS):
                b = slab_arrived(act, "A", S_A + 2 * i, 0, c, i)
                act.wait_ge(full[b], 0) if False else None
                act.activation(s[:, 3, a:z], ps[b][:, 0:z - a], ACT.Identity, bias=col("b_in", i)).then_inc(free[b], 1)
            for c, (a, z) in enumerate(CHUNKS):
                b = slab_arrived(act, "A", S_A + 2 * i + 1, 1, c, i)
                act.activation(s[:, 2, a:z], ps[b][:, 0:z - a], ACT.Sigmoid, bias=col("b_in", CB + i)).then_inc(free[b], 1)
            act.wait_ge(free[2], 0) if False else None
            act.wait_ge(sem("u_done"), 2 * (i + 1))
            act.dma_start(conv_p[:, i], qf[:, i, EXT - CTX:EXT]).then_inc(sem("conv_out"), 16)
            act.wait_ge(sem("conv_state_in"), 16 * CB)
            act.dma_start(conv_s[:, i], conv_dec(i)[:, :, ST:DEXT]).then_inc(sem("conv_out"), 16)

        def keep_conv(i):
            act.wait_ge(sem("conv_done"), i + 1)
            if i == 0:
                act.wait_ge(sem("conv_out"), 16 * 2 * CB)
            act.copy(qf[:, i, 0:T], s[:, i % 2, :]).then_inc(sem("conv_kept"), 1)

        def pool_inputs(stage, n0, g0):
            for p in range(2):
                g = g0 + p
                for c, (a, z) in enumerate(CHUNKS):
                    b = slab_arrived(act, stage, n0 + p, p, c, 0)
                    zp = min(z, TP)
                    ins = act.activation(qf[:, CB + g, PCTX + a:PCTX + zp], ps[b][:, 0:zp - a], ACT.Identity,
                                         bias=col("b_in", 2 * CB + g))
                    if z > TP:
                        own.done(ins)
                        ins = act.activation(pool_dec(g)[:, :, PCTX:DPEXT], by_request(ps[b][:, zp - a:z - a]),
                                             ACT.Identity, bias=col("b_in", 2 * CB + g))
                    ins.then_inc(free[b], 1)
                    if z > TP:
                        own.wait()
                        act.wait_ge(free[b], FREED[stage][b] + 1)
                act.wait_ge(free[3 * p], FREED[stage][3 * p] + 1)
                act.wait_ge(free[3 * p + 1], FREED[stage][3 * p + 1] + 1)
                act.wait_ge(sem("pool_state_in"), 16 * (2 if g < 2 else 4))
                act.dma_start(pool_p[:, g], qf[:, CB + g, PEXT - PCTX:PEXT]).then_inc(sem(f"pool_out{g}"), 16)
                act.dma_start(pool_s[:, g], pool_dec(g)[:, :, ST:DPEXT]).then_inc(sem(f"pool_out{g}"), 16)

        keep_conv(0)
        pool_inputs("P0", S_P0, 0)
        keep_conv(1)
        for j in range(NB):
            b = slab_arrived(act, "V", S_V + j, j % 2, 0, j // 2, last=0)
            src = ps[b][:, 0:NMEM].rearrange("p (m d) -> p m d", m=2)
            w = slice(j * P, (j + 1) * P)
            act.copy(vf[:, :, w], src).then_inc(sem("v_full"), 1)
            act.copy(vh[:, :, w], src).then_inc(free[b], 1)
        act.wait_ge(sem("v_full"), NB)
        act.dma_start(v_out, vf[:]).then_inc(sem("v_out"), 16)
        for g in range(2, PB):
            load(pool_dec(g)[:, :, 0:PCTX], pool_state[:, g], "pool_state_in")
        pool_inputs("P2", S_P2, 2)
        keep_conv(2)

        for g in range(PB):
            banks = [3 * (g % 2) + c for c in range(3)]
            act.wait_ge(full[banks[2]], FILLED["PM"][banks[2]] + g // 2 + 1)
            for c, (a, z) in enumerate(CHUNKS):
                b = banks[c]
                act.wait_ge(full[b], FILLED["PM"][b] + g // 2 + 1)
                act.activation(qf[:, CB + g, T + a:T + z], ps[b][:, 0:z - a], ACT.Copy, scale=col("pool_scale", g))\
                    .then_inc(free[b], 1)
            for b in banks:
                act.wait_ge(free[b], FREED["PM"][b] + g // 2 + 1)
            act.copy(q[:, CB + g, 0, :], qf[:, CB + g, T:2 * T]).then_inc(sem("mix_high"), 1)
        keep_conv(3)

        for i in range(CB):
            act.wait_ge(sem("gn_d"), 3 * (i + 1))
            act.activation(qf[:, i, T:2 * T], qf[:, i, 0:T], ACT.Square).then_inc(sem("gn_sq"), 1)
        act.wait_ge(full[6], FILLED["GS"][6] + 1)
        act.activation(small[:, 0:72], ps[6][:, 0:72], ACT.Sqrt, bias=col("eps")).then_inc(free[6], 1)
        act.wait_ge(sem("gn_rstd"), 1)
        for i in range(CB):
            if i == 3:
                act.wait_ge(full[2], FILLED["GT"][2] + 1)
            src = small[:, 18 * i:18 * (i + 1)].rearrange("p (t g) -> p t g", g=2)
            for g in range(2):
                ins = act.copy(spread[:, i % 3, :, 64 * g:64 * (g + 1)],
                               src[:, :, g:g + 1].broadcast_to([P, NT, 64]))
                if g == 0:
                    own.done(ins)
                else:
                    own.wait()
                    ins.then_inc(sem("gn_spread_half"), 1)
                    act.wait_ge(sem("gn_spread_half"), i + 1)
                    act.sem_inc(sem("gn_spread"), 1)
        for i in range(CB):
            act.wait_ge(sem("gn_n"), 3 * (i + 1))
            act.activation(qf[:, i, T:2 * T], qf[:, i, 0:T], ACT.Silu, scale=col("gn_g", i), bias=col("gn_b", i))\
                .then_inc(sem("gn_out"), 1)
            act.wait_ge(sem("gn_out"), i + 1)
            act.copy(q[:, i, 0, :], qf[:, i, T:2 * T]).then_inc(sem("mix_high"), 1)

        def ln(n, scr):
            for c, (a, z) in enumerate(CHUNKS):
                b = 6 + c % 2
                act.wait_ge(full[b], FILLED[f"C{n}"][b] + c // 2 + 1)
                act.copy(scr[:, 2, a:z], ps[b][:, 0:z - a]).then_inc(free[b], 1)
            for j in range(NB):
                act.wait_ge(sem("ln_d"), NB * (n - 1) + j + 1)
                if j:
                    act.wait_ge(sem("ln_sq_used"), NB * (n - 1) + j)
                act.activation(scr[:, 3, :], xf[:, j, :], ACT.Square).then_inc(sem("ln_sq"), 1)
            act.wait_ge(sem("ln_var"), n)
            act.activation(small[:, 0:NT], small[:, 32:32 + NT], ACT.Sqrt, bias=col("eps")).then_inc(sem("ln_std"), 1)
            act.wait_ge(sem("ln_e"), n)
            for j in range(2):
                act.copy(lnspread[:, j], small[:, 16 * j + 48:16 * j + 48 + NT].unsqueeze(2).broadcast_to([P, NT, P]))\
                    .then_inc(sem("ln_spread"), 1)

        def x_high(n):
            for c, (a, z) in enumerate(CHUNKS):
                act.wait_ge(sem("x_norm"), NB * (3 * (n - 1) + c + 1))
                act.copy(xh[:, :, a:z], xf[:, :, a:z]).then_inc(sem("x_norm_high"), 1)

        ln(1, s)
        x_high(1)

        with act.Fori(0, 4) as i:
            for p in range(2):
                for c, (a, z) in enumerate(CHUNKS):
                    b = slab_arrived(act, "XQ", S_XQ + 2 * i + p, p, c, i)
                    act.copy(q[:, bass.ds(2 * i + p, 1), 0, a:z], ps[b][:, 0:z - a].unsqueeze(1)).then_inc(sem("q_high"), 1)

        def prob_exp(t):
            act.wait_ge(sem("neg_max"), t + 1)
            for h in range(HEADS):
                b = 2 * (t % 2) + h // 2
                if t >= 2 and h == 0:
                    act.wait_ge(full[5], FILLED["ATT"][5] + t - 1)
                ins = act.activation(prob[:, t % 2, h * NMEM:(h + 1) * NMEM], ps[b][:, (h % 2) * NMEM:(h % 2 + 1) * NMEM],
                                     ACT.Exp, bias=small[:, 8 * (t % 2) + h:8 * (t % 2) + h + 1], scale=SCALE,
                                     accum_out=small[:, 16 + 8 * (t % 2) + h:16 + 8 * (t % 2) + h + 1])
                ins.then_inc(sem("exp_done"), 1)
                if h % 2:
                    act.wait_ge(sem("exp_done"), 4 * t + h + 1)
                    act.sem_inc(free[b], 1)

        def prob_t_high(t):
            for j in range(2):
                b = 4 + j
                act.wait_ge(full[b], FILLED["ATT"][b] + t + 1)
                if t:
                    act.wait_ge(full[7], FILLED["ATT"][7] + t)
                act.copy(pth[:, 4 * j:4 * j + 4, :], ps[b][:].rearrange("p (j n) -> p j n", j=4))\
                    .then_inc(sem("prob_t_high"), 1)

        def o_high(t):
            for j in range(2):
                b = 6 + j
                act.wait_ge(full[b], FILLED["ATT"][b] + t + 1)
                act.copy(q[:, 4 * j:4 * j + 4, 0, t * P:(t + 1) * P], ps[b][:].rearrange("p (j n) -> p j n", j=4))\
                    .then_inc(sem("o_high"), 1)

        prob_exp(0)
        for t in range(8):
            if t + 1 < 8:
                prob_exp(t + 1)
            prob_t_high(t)
            if t >= 1:
                o_high(t - 1)
        o_high(7)

        act.wait_ge(sem("dec_used"), SB)
        act.copy(prob[:, 0, 0:NMEM], ps[0][:, 0:NMEM]).then_inc(sem("dec_s"), 1)
        act.wait_ge(sem("neg_max"), 9)
        act.activation(prob[:, 1, 0:NMEM], ps[1][:, 0:NMEM], ACT.Exp, bias=small[:, 0:1], scale=SCALE,
                       accum_out=small[:, 16:17]).then_inc(sem("exp_done"), 1)
        act.wait_ge(full[2], FILLED["DEC"][2] + 1)
        act.copy(prob[:, 0, 512:512 + NMEM], ps[2][:, 0:NMEM]).then_inc(sem("dec_p"), 1)
        act.wait_ge(sem("dec_used"), 2 * SB)
        act.copy(q[:, :, 0, TP:T], ps[3][:, 0:NMEM].rearrange("p (f n) -> p f n", n=TS)).then_inc(sem("o_high"), 1)
        for b in range(3):
            act.sem_inc(free[b], 1)

        ln(2, s)
        x_high(2)

        for g in range(FFG):
            stage, n0 = f"W1{g}", S_FF + g * 2 * GB
            for i in range(GB // 2):
                for p in range(2):
                    j = 2 * i + p
                    for c, (a, z) in enumerate(CHUNKS):
                        done = 24 * g + 3 * j + c
                        b = slab_arrived(act, stage, n0 + j, p, c, i)
                        if done >= 6:
                            act.wait_ge(sem("square"), done - 5)
                        act.activation(relu[:, p, a:z], ps[b][:, 0:z - a], ACT.Relu, bias=col("b1", GB * g + j))\
                            .then_inc(free[b], 1)
                        act.wait_ge(sem("square"), done + 1)
                        act.copy(q[:, j, 0, a:z], qf[:, j, T + a:T + z]).then_inc(sem("hidden_high"), 1)
        ln(3, s3)

    @block.vector
    def _(dve):
        own = Own(dve, "dve_own")
        stt, tt, ts = dve.scalar_tensor_tensor, dve.tensor_tensor, dve.tensor_scalar

        dve.wait_ge(sem("mem_high"), 1)
        tt(mem[:, 1], memf[:, 1], mem[:, 0].bitcast(f32), ALU.subtract).then_inc(sem("mem_low"), 1)
        for j in range(NB):
            dve.wait_ge(sem("x_high"), j + 1)
            tt(xl[:, j, :], xf[:, j, :], xh[:, j, :].bitcast(f32), ALU.subtract).then_inc(sem("x_low"), 1)
        dve.wait_ge(sem("k_out"), 16)
        dve.wait_ge(free[0], 4)
        dve.wait_ge(free[3], 4)
        tt(kl[:], kf[:], kh[:].bitcast(f32), ALU.subtract).then_inc(sem("kv_low"), 1)
        dve.wait_ge(sem("const_in"), 32)
        dve.wait_ge(sem("pad_done"), 2)

        def conv(i, lo=0, hi=TAPS):
            out = s[:, i % 2, 0:TP]
            if lo == 0:
                dve.wait_ge(sem("u_done"), 2 * (i + 1))
                if i >= 2:
                    dve.wait_ge(sem("conv_kept"), i - 1)
                own.link(ts(out, qf[:, i, 0:TP], col("conv_w", TAPS * i), col("conv_b", i), ALU.mult, ALU.add))
            for k in range(max(lo, 1), hi):
                own.link(stt(out, qf[:, i, k:k + TP], col("conv_w", TAPS * i + k), out, ALU.mult, ALU.add))
            if hi == TAPS:
                dve.wait_ge(sem("conv_state_in"), 16 * CB)
                w = col("conv_w", TAPS * i, TAPS).unsqueeze(1).broadcast_to([P, SB, TAPS])
                tmp = qf[:, i, EXT + SB * DEXT:EXT + SB * DEXT + SB * TAPS].rearrange("p (b n) -> p b n", b=SB)
                dst = by_request(s[:, i % 2, TP:T])
                for t in range(ST):
                    own.link(tt(tmp, conv_dec(i)[:, :, t:t + TAPS], w, ALU.mult))
                    own.link(dve.tensor_reduce(dst[:, :, t:t + 1], tmp, AX, ALU.add))
                ts(s[:, i % 2, TP:T], s[:, i % 2, TP:T], col("conv_b", i), None, ALU.add).then_inc(sem("conv_done"), 1)

        def window(g):
            dve.wait_ge(sem("pool_out%d" % g), 32)
            if g >= 2:
                dve.wait_ge(sem("pad_done"), 3)
            src, sdec = qf[:, CB + g, 0:PEXT], pool_dec(g)
            n, nd, w = PEXT, DPEXT, 1
            cur, cdec = src, sdec
            base = CB + g
            while w < WINDOWS[g]:
                j = 2 + (w.bit_length() - 1) % 2
                n, nd = n - w, nd - w
                nxt = s[:, j, 0:n]
                o = 1200 + 160 * (j - 2)
                ndec = qf[:, base, o:o + SB * nd].rearrange("p (b n) -> p b n", b=SB)
                tt(nxt, cur[:, w:w + n], cur[:, 0:n], ALU.add).then_inc(own.sem, 1)
                tt(ndec, cdec[:, :, w:w + nd], cdec[:, :, 0:nd], ALU.add).then_inc(own.sem, 1)
                own.n += 2
                own.wait()
                cur, cdec, w = nxt, ndec, 2 * w
            wn = WINDOWS[g]
            tok = qf[:, base, PCTX:PEXT]
            lead = PCTX - (wn - 1)
            head = small[:, 64:80]
            own.link(tt(head, cur[:, lead:lead + 16], col("ramp", 16 * g, 16), ALU.mult))
            own.link(tt(head, head, tok[:, 0:16], ALU.subtract))
            own.link(stt(tok, cur[:, lead:lead + TP], 1.0 / wn, tok, ALU.mult, ALU.subtract))
            own.link(dve.tensor_copy(tok[:, 0:16], head))
            dve.sem_inc(sem("delta_done"), 1)
            stt(sdec[:, :, PCTX:DPEXT], cdec[:, :, lead:lead + ST], 1.0 / wn, sdec[:, :, PCTX:DPEXT],
                ALU.mult, ALU.subtract).then_inc(sem("delta_done"), 1)

        conv(0)
        conv(1)
        window(0)
        window(1)
        conv(2)
        dve.wait_ge(sem("v_out"), 16)
        dve.wait_ge(free[0], FREED["V"][0] + 4)
        dve.wait_ge(free[3], FREED["V"][3] + 4)
        tt(vl[:], vf[:], vh[:].bitcast(f32), ALU.subtract).then_inc(sem("kv_low"), 1)
        window(2)
        window(3)
        for g in range(PB):
            dve.wait_ge(sem("mix_high"), g + 1)
            tt(q[:, CB + g, 1, :], qf[:, CB + g, T:2 * T], q[:, CB + g, 0, :].bitcast(f32), ALU.subtract)\
                .then_inc(sem("mix_low"), 1)

        e1 = Own(dve, "e1_sum")
        for j in range(NB):
            lo = 4 * j
            conv(3, lo, min(lo + 4, TAPS))
            dve.wait_ge(sem("x_restored"), j + 1)
            m, turn = j % 2, j // 2
            for c, (a, z) in enumerate(CHUNKS):
                b = 3 * m + c
                if b == 5:
                    dve.wait_ge(used, S_E1 + turn + 1)
                else:
                    dve.wait_ge(full[b], FILLED["E1"][b] + turn + 1)
                stt(xf[:, j, a:z], xf[:, j, a:z], ALPHA, ps[b][:, 0:z - a], ALU.mult, ALU.add).then_inc(free[b], 1)

        for i in range(CB):
            for c, (a, z) in enumerate(CHUNKS):
                b = 3 * (i % 2) + c
                dve.wait_ge(full[b], FILLED["GM"][b] + i // 2 + 1)
                tt(qf[:, i, a:z], qf[:, i, a:z], ps[b][:, 0:z - a], ALU.subtract).then_inc(free[b], 1)
            for c in range(3):
                b = 3 * (i % 2) + c
                dve.wait_ge(free[b], FREED["GM"][b] + i // 2 + 1)
                dve.sem_inc(sem("gn_d"), 1)
        dve.wait_ge(free[6], FREED["GS"][6] + 1)
        dve.reciprocal(small[:, 0:72], small[:, 0:72]).then_inc(sem("gn_rstd"), 1)
        for i in range(CB):
            for c, (a, z) in enumerate(CHUNKS):
                b = 3 * (i % 2) + c
                dve.wait_ge(full[b], FILLED["GT"][b] + i // 2 + 1)
                tt(qf[:, i, a:z], qf[:, i, a:z], ps[b][:, 0:z - a], ALU.mult).then_inc(free[b], 1)
            for c in range(3):
                b = 3 * (i % 2) + c
                dve.wait_ge(free[b], FREED["GT"][b] + i // 2 + 1)
                dve.sem_inc(sem("gn_n"), 1)
        for i in range(CB):
            dve.wait_ge(sem("mix_high"), PB + i + 1)
            tt(q[:, i, 1, :], qf[:, i, T:2 * T], q[:, i, 0, :].bitcast(f32), ALU.subtract).then_inc(sem("mix_low"), 1)

        def ln_block(n, scr, j):
            if j == 0:
                for b, k in LN_MEAN.items():
                    dve.wait_ge(free[b], FREED[f"C{n}"][b] + k)
            tt(xf[:, j, :], xf[:, j, :], scr[:, 2, :], ALU.subtract).then_inc(sem("ln_d"), 1)
            dve.wait_ge(sem("ln_d"), NB * (n - 1) + j + 1)
            if j == 0:
                own.done(dve.tensor_copy(scr[:, 0, :], xf[:, j, :]))
            else:
                own.done(tt(scr[:, 0, :], scr[:, 0, :], xf[:, j, :], ALU.add))
            dve.wait_ge(sem("ln_sq"), NB * (n - 1) + j + 1)
            own.wait()
            if j == 0:
                ins = dve.tensor_copy(scr[:, 1, :], scr[:, 3, :])
            else:
                ins = tt(scr[:, 1, :], scr[:, 1, :], scr[:, 3, :], ALU.add)
            ins.then_inc(sem("ln_sq_used"), 1)
            dve.wait_ge(sem("ln_sq_used"), NB * (n - 1) + j + 1)

        def ln_finish(n, out=None):
            dve.sem_inc(sem("ln_sums"), 1)
            dve.wait_ge(full[6], FILLED[f"S{n}"][6] + 1)
            mean, var, rstd, shift = (small[:, o:o + NT] for o in (16, 32, 48, 64))
            own.link(dve.tensor_copy(mean, ps[6][:, 0:NT]))
            own.link(tt(var, mean, mean, ALU.mult))
            tt(var, ps[6][:, NT:2 * NT], var, ALU.subtract).then_inc(free[6], 1)
            dve.wait_ge(free[6], FREED[f"S{n}"][6] + 1)
            dve.sem_inc(sem("ln_var"), 1)
            dve.wait_ge(sem("ln_std"), n)
            own.link(dve.reciprocal(rstd, small[:, 0:NT]))
            stt(shift, mean, -1.0, rstd, ALU.mult, ALU.mult).then_inc(sem("ln_e"), 1)
            for c, (a, z) in enumerate(CHUNKS):
                for j, op in enumerate((ALU.mult, ALU.add)):
                    b = 3 * j + c
                    dve.wait_ge(full[b], FILLED[f"T{n}"][b] + 1)
                    tt(xf[:, :, a:z], xf[:, :, a:z], over_blocks(ps[b][:, 0:z - a]), op).then_inc(free[b], 1)
                    dve.wait_ge(free[b], FREED[f"T{n}"][b] + 1)
                for j in range(NB):
                    ts(xf[:, j, a:z], xf[:, j, a:z], col(f"ln{n}_g", j), col(f"ln{n}_b", j), ALU.mult, ALU.add)\
                        .then_inc(sem("x_norm"), 1)
                if out:
                    dve.wait_ge(sem("x_norm"), NB * (3 * (n - 1) + c + 1))
                    dve.sem_inc(sem("y_ready"), 1)
                else:
                    dve.wait_ge(sem("x_norm_high"), 3 * (n - 1) + c + 1)
                    tt(xl[:, :, a:z], xf[:, :, a:z], xh[:, :, a:z].bitcast(f32), ALU.subtract).then_inc(sem("x_norm_low"), 1)

        for j in range(NB):
            m, turn = j % 2, j // 2
            for c, (a, z) in enumerate(CHUNKS):
                b = 3 * m + c
                if b == 5:
                    dve.wait_ge(used, S_E2 + turn + 1)
                else:
                    dve.wait_ge(full[b], FILLED["E2"][b] + turn + 1)
                tt(xf[:, j, a:z], xf[:, j, a:z], ps[b][:, 0:z - a], ALU.add).then_inc(free[b], 1)
            for c in range(3):
                dve.wait_ge(free[3 * m + c], FREED["E2"][3 * m + c] + turn + 1)
            dve.sem_inc(sem("ln_y"), 1)
        for j in range(NB):
            ln_block(1, s, j)
        ln_finish(1)

        with dve.Fori(0, 4) as i:
            for p in range(2):
                for c, (a, z) in enumerate(CHUNKS):
                    b = 3 * p + c
                    dve.wait_ge(sem("q_high"), 6 * i + 3 * p + c + 1)
                    f = bass.ds(2 * i + p, 1)
                    tt(q[:, f, 1, a:z], ps[b][:, 0:z - a].unsqueeze(1), q[:, f, 0, a:z].bitcast(f32), ALU.subtract)\
                        .then_inc(free[b], 1)
        for b in range(6):
            dve.wait_ge(free[b], FREED["XQ"][b] + 4)
        dve.sem_inc(sem("q_low"), 24)

        def neg_max(t, bank0, heads):
            o = 8 * (t % 2)
            for h in range(0, heads, 2):
                n = min(2, heads - h)
                own.done(dve.reduce_max(small[:, o + h:o + h + n], ps[bank0 + h // 2][:, 0:n * NMEM].rearrange("p (h m) -> p h m", h=n), AX))
            own.wait()
            ts(small[:, o:o + heads], small[:, o:o + heads], -SCALE, None, ALU.mult).then_inc(sem("neg_max"), 1)

        def normalise(t, heads):
            o = 8 * (t % 2)
            own.link(dve.reciprocal(small[:, 32 + o:32 + o + heads], small[:, 16 + o:16 + o + heads]))
            for h in range(heads):
                own.done(ts(prob[:, t % 2, h * NMEM:(h + 1) * NMEM], prob[:, t % 2, h * NMEM:(h + 1) * NMEM],
                            small[:, 32 + o + h:32 + o + h + 1], None, ALU.mult))
            own.wait()
            dve.sem_inc(sem("prob_done"), 1)

        def maxes(t):
            for j in range(2):
                b = 2 * (t % 2) + j
                dve.wait_ge(full[b], FILLED["ATT"][b] + t // 2 + 1)
            if t >= 2:
                dve.wait_ge(sem("exp_done"), 4 * (t - 1))
            neg_max(t, 2 * (t % 2), HEADS)

        def prob_t_low(t):
            for j in range(2):
                b = 4 + j
                dve.wait_ge(sem("prob_t_high"), 2 * t + j + 1)
                tt(ptl[:, 4 * j:4 * j + 4, :], ps[b][:].rearrange("p (j n) -> p j n", j=4),
                   pth[:, 4 * j:4 * j + 4, :].bitcast(f32), ALU.subtract).then_inc(free[b], 1)
                dve.wait_ge(free[b], FREED["ATT"][b] + t + 1)
                dve.sem_inc(sem("prob_t_low"), 1)

        def o_low(t):
            for j in range(2):
                b = 6 + j
                dve.wait_ge(sem("o_high"), 2 * t + j + 1)
                tok = slice(t * P, (t + 1) * P)
                tt(q[:, 4 * j:4 * j + 4, 1, tok], ps[b][:].rearrange("p (j n) -> p j n", j=4),
                   q[:, 4 * j:4 * j + 4, 0, tok].bitcast(f32), ALU.subtract).then_inc(free[b], 1)
                dve.wait_ge(free[b], FREED["ATT"][b] + t + 1)
                dve.sem_inc(sem("o_low"), 1)

        maxes(0)
        for t in range(8):
            if t + 1 < 8:
                maxes(t + 1)
            dve.wait_ge(sem("exp_done"), 4 * (t + 1))
            normalise(t, HEADS)
            prob_t_low(t)
            if t >= 1:
                o_low(t - 1)
        o_low(7)

        dve.wait_ge(sem("x_restored"), 2 * NB)
        tt(qd[:], q[:, :, 0, TP:T].bitcast(f32), q[:, :, 1, TP:T].bitcast(f32), ALU.add).then_inc(sem("dec_q"), 1)
        dve.wait_ge(full[1], FILLED["DEC"][1] + 1)
        neg_max(0, 1, 1)
        dve.wait_ge(sem("exp_done"), 33)
        own.link(dve.reciprocal(small[:, 32:33], small[:, 16:17]))
        own.link(ts(prob[:, 1, 0:NMEM], prob[:, 1, 0:NMEM], small[:, 32:33], None, ALU.mult))
        dve.sem_inc(sem("prob_done"), 1)
        dve.wait_ge(sem("o_high"), 17)
        tt(q[:, :, 1, TP:T], ps[3][:, 0:NMEM].rearrange("p (f n) -> p f n", n=TS), q[:, :, 0, TP:T].bitcast(f32),
           ALU.subtract).then_inc(free[3], 1)
        dve.wait_ge(free[3], FREED["DEC"][3] + 1)
        dve.sem_inc(sem("o_low"), 1)

        def joins(stage, n0, j, add):
            p, i = j % 2, j // 2
            for c, (a, z) in enumerate(CHUNKS):
                b = slab_arrived(dve, stage, n0 + j, p, c, i)
                add(j, c, a, z, ps[b][:, 0:z - a]).then_inc(free[b], 1)
            for c in range(3):
                dve.wait_ge(free[3 * p + c], FREED[stage][3 * p + c] + i + 1)
            if j == 0:
                dve.sem_inc(sem("ln_y"), 1)

        def joins_with_norm(stage, n0, n, scr, add):
            for j in range(NB):
                joins(stage, n0, j, add)
                if j == 2:
                    ln_block(n, scr, 0)
                    ln_block(n, scr, 1)
                if j >= 2:
                    ln_block(n, scr, j)

        joins_with_norm("XO", S_XO, 2, s, lambda j, c, a, z, y: stt(xf[:, j, a:z], xf[:, j, a:z], ALPHA, y, ALU.mult, ALU.add))
        ln_finish(2)

        for g in range(FFG):
            n0 = S_FF + g * 2 * GB
            for j in range(GB):
                p = j % 2
                for c, (a, z) in enumerate(CHUNKS):
                    done = 24 * g + 3 * j + c
                    dve.wait_ge(free[3 * p + c], FREED[f"W1{g}"][3 * p + c] + j // 2 + 1)
                    full_part = qf[:, j, T + a:T + z]
                    tt(full_part, relu[:, p, a:z], relu[:, p, a:z], ALU.mult).then_inc(sem("square"), 1)
                    dve.wait_ge(sem("hidden_high"), done + 1)
                    tt(q[:, j, 1, a:z], full_part, q[:, j, 0, a:z].bitcast(f32), ALU.subtract).then_inc(sem("hidden_low"), 1)
                if g == 0:
                    own.link(ts(acc[:, j, :], xh[:, j, :].bitcast(f32), ALPHA, col("b2", j), ALU.mult, ALU.add))
                    own.link(stt(acc[:, j, :], xl[:, j, :].bitcast(f32), ALPHA, acc[:, j, :], ALU.mult, ALU.add))
            if g < FFG - 1:
                for j in range(NB):
                    joins_plain = lambda j, c, a, z, y: tt(acc[:, j, a:z], acc[:, j, a:z], y, ALU.add)
                    p, i = j % 2, j // 2
                    for c, (a, z) in enumerate(CHUNKS):
                        b = slab_arrived(dve, f"W2{g}", n0 + GB + j, p, c, i)
                        joins_plain(j, c, a, z, ps[b][:, 0:z - a]).then_inc(free[b], 1)
                for b in range(6):
                    dve.wait_ge(free[b], FREED[f"W2{g}"][b] + 4)
            else:
                joins_with_norm(f"W2{g}", n0 + GB, 3, s3, lambda j, c, a, z, y: tt(xf[:, j, a:z], acc[:, j, a:z], y, ALU.add))
        ln_finish(3, True)

    ctx.close()


def kernel(x_prompt, x_sample, mem_prompt, cache_mem_k, cache_mem_v, state_conv, state_pool,
           w_in, b_in, conv_w, conv_b, gn_g, gn_b, pool_w, pool_scale, w_out,
           ln1_g, ln1_b, xq_w, xk_w, xv_w, xo_w, ln2_g, ln2_b, w1, b1, w2, b2, ln3_g, ln3_b):
    import numpy as np
    import concourse.bacc as bacc
    from concourse import mybir as mb
    from concourse.bass_utils import run_bass_kernel_spmd as run

    def feature_major(a):
        a = np.asarray(a)
        return a.reshape(a.shape[0], -1, P).transpose(2, 1, 0)

    def blocks(w, k=NB):
        w = np.asarray(w)
        return w.reshape(k, P, -1, P).transpose(2, 1, 0, 3).reshape(-1, P, k * P)

    def paired(w):
        return blocks(w, 4).reshape(4, 2, P, 4 * P).transpose(0, 2, 1, 3).reshape(4, P, SLAB)

    x = np.concatenate([np.asarray(x_prompt).reshape(TP, D), np.asarray(x_sample).reshape(TS, D)])
    win = blocks(w_in[0])
    order = [n for i in range(CB) for n in (i, CB + i)]
    ff = []
    up, down = blocks(w1[0]), np.asarray(w2[0]).reshape(FFG, D, D)
    for g in range(FFG):
        ff += [up[g * GB:(g + 1) * GB], blocks(down[g])]
    wo = np.asarray(w_out[0])
    slabs = np.concatenate([blocks(xk_w[0]), win[order], win[8:10], blocks(xv_w[0]), win[10:12],
                            paired(wo[D_CONV:]), paired(wo[:D_CONV]), blocks(xq_w[0]), blocks(xo_w[0])] + ff)
    cols = [np.asarray(conv_w[0]).reshape(TAPS, CB, P).transpose(2, 1, 0).reshape(P, -1)]
    for v in (b_in, conv_b, gn_g, gn_b, pool_scale, ln1_g, ln1_b, ln2_g, ln2_b, ln3_g, ln3_b, b1, b2):
        cols.append(np.asarray(v[0]).reshape(-1, P).T)
    ramp = np.array([[1.0 / min(t + 1, w) for t in range(16)] for w in WINDOWS], np.float32).reshape(1, -1)
    fixed = [np.repeat(ramp, P, 0), np.full((P, 1), EPS, np.float32), np.full((P, 1), 1.0 / D, np.float32),
             np.repeat(np.eye(2, dtype=np.float32) / 64, 64, 0)]
    params = np.concatenate(cols + fixed, axis=1)
    consts = np.concatenate([np.full((P, P), 1.0 / P, np.float32),
                             np.kron(np.eye(2, dtype=np.float32), np.full((64, 64), 1.0 / 64, np.float32)),
                             np.eye(P, dtype=np.float32)], axis=1)
    ck = np.asarray(cache_mem_k[0]).transpose(0, 2, 3, 1).reshape(SB, NB, P, NMEM).transpose(0, 2, 1, 3)
    cv = np.asarray(cache_mem_v[0]).reshape(SB, 2, P, D).transpose(0, 2, 1, 3)
    state = lambda a, n: np.asarray(a[0]).transpose(2, 0, 1).reshape(-1, P, SB, n).transpose(1, 0, 2, 3)
    arrays = {
        "xT": feature_major(x), "memT": feature_major(np.asarray(mem_prompt)[0]), "slabs": slabs,
        "pool_w": np.asarray(pool_w[0]).transpose(1, 0, 2).reshape(P, -1), "params": params, "consts": consts,
        "conv_state": state(state_conv, CTX), "pool_state": state(state_pool, PCTX),
        "dec_kv": np.concatenate([ck.reshape(SB, P, 2048), cv.reshape(SB, P, 2048)]),
    }
    outs = {"yT": (P, NB, T), "kT": (P, NB, NMEM), "v_out": (P, 2, D), "conv_p": (P, CB, CTX),
            "conv_s": (P, CB, SB, CTX), "pool_p": (P, PB, PCTX), "pool_s": (P, PB, SB, PCTX)}
    nc = bacc.Bacc("TRN2", target_bir_lowering=False, num_devices=1)
    args, fed = {}, {}
    for name, a in arrays.items():
        fed[name + "_in"] = np.ascontiguousarray(a)
        args[name] = nc.dram_tensor(name + "_in", a.shape, mb.dt.float32, kind="ExternalInput").ap()
    for name, shape in outs.items():
        args[name] = nc.dram_tensor(name + "_res", shape, mb.dt.float32, kind="ExternalOutput").ap()
    decoder_step(nc, **args)
    r = run(nc, [fed], core_ids=[0]).results[0]
    got = {name: np.asarray(r[name + "_res"]) for name in outs}

    y = got["yT"].transpose(2, 1, 0).reshape(T, D)
    k = got["kT"].transpose(2, 1, 0).reshape(1, 1, NMEM, HEADS, D // HEADS)
    v = got["v_out"].transpose(1, 0, 2).reshape(1, 1, NMEM, HEADS, D // HEADS)
    cp = got["conv_p"].transpose(2, 1, 0).reshape(1, 1, CTX, D_CONV)
    cs = got["conv_s"].transpose(2, 3, 1, 0).reshape(1, SB, CTX, D_CONV)
    pp = got["pool_p"].transpose(2, 1, 0).reshape(1, 1, PCTX, D - D_CONV)
    pss = got["pool_s"].transpose(2, 3, 1, 0).reshape(1, SB, PCTX, D - D_CONV)
    return (y[:TP].reshape(1, TP, D), y[TP:].reshape(SB, ST, D), k, v, cp, cs, pp, pss)
```

```python
from contextlib import ExitStack

import concourse.bass as bass
from concourse import mybir

P = 128
D = 1024
NB = D // P
TP = 1024
SB, ST = 8, 4
TS = SB * ST
T = TP + TS
D_CONV = 512
CB = D_CONV // P
PB = 4
TAPS = 31
CTX = TAPS - 1
WINDOWS = (2, 4, 8, 16)
PCTX = 15
NMEM = 256
HEADS = 4
FF = 4096
FFG = 4
GB = FF // P // FFG
ALPHA = 2.0 ** 0.25
SCALE = 256.0 ** -0.5
EPS = 1e-5
CHUNKS = ((0, 384), (384, 768), (768, 1056))
TILES = tuple(128 * t for t in range(8)) + (T - P,)
NT = len(TILES)
SLAB = NB * P

EXT = TP + CTX
DEXT = ST + CTX
PEXT = TP + PCTX
DPEXT = ST + PCTX
BLK = 2 * T

S_K, S_A, S_P0, S_V, S_P2, S_E1, S_E2, S_XQ, S_XO, S_FF = 0, 8, 16, 18, 26, 28, 32, 36, 44, 52
NSLAB = S_FF + FFG * 2 * GB

COLS = {}
_at = 0
for _name, _n in (("conv_w", CB * TAPS), ("b_in", 12), ("conv_b", 4), ("gn_g", 4), ("gn_b", 4), ("pool_scale", 4),
                  ("ln1_g", 8), ("ln1_b", 8), ("ln2_g", 8), ("ln2_b", 8), ("ln3_g", 8), ("ln3_b", 8),
                  ("b1", 32), ("b2", 8), ("ramp", 4 * 16), ("eps", 1), ("inv_d", 1), ("half", 2)):
    COLS[_name] = _at
    _at += _n
NPAR = _at
RING = 5
NCONST = 3 * P


SIX = {b: 1 for b in range(6)}
LN_MEAN = {6: 2, 7: 1}


def times(n, banks):
    return {b: n * k for b, k in banks.items()}


LINEAR = (times(4, SIX), (2, 5))
ONE_BANK = ({0: 4, 3: 4}, (0, 3))
ONE_PAIR = (SIX, (2, 5))
HALVES = (times(4, SIX), (5,))
STAGES = [("K", *ONE_BANK), ("A", *LINEAR), ("P0", *ONE_PAIR), ("V", {0: 4, 3: 4}, (3,)), ("P2", *ONE_PAIR),
          ("PM", times(2, SIX), ()), ("E1", *HALVES), ("GM", times(2, SIX), ()), ("GS", {6: 1}, ()),
          ("GT", times(2, SIX), ()), ("E2", *HALVES), ("C1", LN_MEAN, ()), ("S1", {6: 1}, ()), ("T1", SIX, ()),
          ("XQ", *LINEAR), ("ATT", {0: 4, 1: 4, 2: 4, 3: 4, 4: 8, 5: 8, 6: 8, 7: 8}, ()),
          ("DEC", {0: 6, 1: 6, 2: 3, 3: 2, 4: 4, 5: 4, 6: 4, 7: 4}, tuple(range(8))), ("XO", *LINEAR), ("C2", LN_MEAN, ()), ("S2", {6: 1}, ()),
          ("T2", SIX, ())]
for _g in range(FFG):
    STAGES += [(f"W1{_g}", *LINEAR), (f"W2{_g}", *LINEAR)]
STAGES += [("C3", LN_MEAN, ()), ("S3", {6: 1}, ()), ("T3", SIX, ())]
FREED, FILLED = {}, {}
_n, _f = {b: 0 for b in range(8)}, {b: 0 for b in range(8)}
for _name, _uses, _silent in STAGES:
    FREED[_name], FILLED[_name] = dict(_n), dict(_f)
    for _b, _k in _uses.items():
        _n[_b] += _k
        _f[_b] += 0 if _b in _silent else _k


def decoder_step(nc, xT, memT, slabs, pool_w, params, consts, conv_state, pool_state, dec_kv,
                 yT, kT, v_out, conv_p, conv_s, pool_p, pool_s):
    f32, f32r = mybir.dt.float32, mybir.dt.float32r
    ALU = mybir.AluOpType
    ACT = mybir.ActivationFunctionType
    AX = mybir.AxisListType.X
    ctx = ExitStack()

    BASE = 16512
    O_XH = BASE
    O_XL = O_XH + NB * T * 4
    O_Q = O_XL + NB * T * 4
    O_W = O_Q + NB * BLK * 4
    O_KV = O_W + 6 * SLAB * 4
    O_S = O_KV + 32768
    O_PAR = O_S + 4 * T * 4
    O_CON = O_PAR + -(-NPAR // 8) * 32
    O_SMALL = O_CON + NCONST * 4

    def at(name, shape, dt, offset):
        return nc.alloc_sbuf_tensor_at(name, shape, dt, offset=offset)

    xh = at("x_high", [P, NB, T], f32r, O_XH)
    xl = at("x_low", [P, NB, T], f32r, O_XL)
    xf = at("x_full", [P, NB, T], f32, O_XL)
    q = at("mix", [P, NB, 2, T], f32r, O_Q)
    qf = at("mix_full", [P, NB, BLK], f32, O_Q)
    mem = at("mem", [P, 2, NB, NMEM], f32r, O_Q + 6 * BLK * 4)
    memf = at("mem_full", [P, 2, NB, NMEM], f32, O_Q + 6 * BLK * 4)
    raw = at("w_raw", [P, 2, SLAB], f32, O_W)
    wh = at("w_high", [P, 2, SLAB], f32r, O_W + 2 * SLAB * 4)
    wl = at("w_low", [P, 2, SLAB], f32r, O_W + 4 * SLAB * 4)
    kh = at("k_high", [P, NB, NMEM], f32r, O_KV)
    kl = at("k_low", [P, NB, NMEM], f32r, O_KV + 8192)
    kf = at("k_full", [P, NB, NMEM], f32, O_KV + 8192)
    vh = at("v_high", [P, 2, D], f32r, O_KV + 16384)
    vl = at("v_low", [P, 2, D], f32r, O_KV + 24576)
    vf = at("v_full", [P, 2, D], f32, O_KV + 24576)
    s = at("scratch", [P, 4, T], f32, O_S)
    prob = at("prob", [P, 2, HEADS * NMEM], f32, O_S)
    pth = at("prob_t_high", [P, 2, 4, 2 * P], f32r, O_S + 8192)
    ptl = at("prob_t_low", [P, 2, 4, 2 * P], f32r, O_XH)
    qz = at("dec_q", [P, NB, SB, HEADS * ST], f32, O_XH + 2 * T * 4)
    dkv = at("dec_kv", [P, RING, D], f32, O_XH + 3 * T * 4)
    dprob = at("dec_prob", [HEADS * ST, SB, NMEM], f32, O_S)
    dpt = at("dec_prob_t", [P, SB, 2, HEADS * ST], f32, O_S + 8192)
    dout = at("dec_out", [HEADS * ST, 2, D], f32, O_XH)
    spread = at("gn_spread", [P, 3, NT, P], f32, O_S)
    lnspread = at("ln_spread", [P, 2, NT, P], f32, O_Q)
    acc = at("ffn_sum", [P, NB, T], f32, O_KV)
    relu = at("relu", [P, 2, T], f32, O_KV + NB * T * 4)
    s3 = at("ln3_scratch", [P, 4, T], f32, O_XH)
    par = at("params", [P, NPAR], f32, O_PAR)
    con = at("consts", [P, NCONST], f32, O_CON)
    small = at("small", [P, 80], f32, O_SMALL)
    ones = at("ones", [P, 1], f32, O_SMALL + 320)
    poolw = qf[:, CB - 1, BLK - PB * P:BLK]

    inv128, inv64, ident = con[:, 0:P], con[:, P:2 * P], con[:, 2 * P:3 * P]

    def col(name, i=0, n=1):
        c = COLS[name] + i
        return par[:, c:c + n] if isinstance(c, int) else par[:, bass.ds(c, n)]

    ps = [ctx.enter_context(nc.psum_tensor(f"bank{b}", [P, 512], f32)) for b in range(8)]

    sems = {}

    def sem(name):
        if name not in sems:
            sems[name] = ctx.enter_context(nc.semaphore(name))
        return sems[name]

    full = [sem(f"bank_full{b}") for b in range(8)]
    free = [sem(f"bank_free{b}") for b in range(8)]
    split_done, used = sem("split_done"), sem("slab_used")

    class Own:

        def __init__(self, eng, name):
            self.eng, self.sem, self.n = eng, sem(name), 0

        def done(self, ins):
            ins.then_inc(self.sem, 1)
            self.n += 1
            return self.n

        def wait(self, n=None):
            self.eng.wait_ge(self.sem, self.n if n is None else n)

        def link(self, ins):
            self.done(ins)
            self.wait()

    def conv_dec(i):
        return qf[:, i, EXT:EXT + SB * DEXT].rearrange("p (b n) -> p b n", b=SB)

    def pool_dec(g):
        return qf[:, CB + g, PEXT:PEXT + SB * DPEXT].rearrange("p (b n) -> p b n", b=SB)

    def by_request(ap):
        return ap.rearrange("p (b n) -> p b n", b=SB)

    def over_blocks(ap, n=NB):
        return ap.unsqueeze(1).broadcast_to([P, n, ap.shape[-1]])

    def slab_arrived(eng, stage, n, p, c, i, last=2):
        b = 3 * p + c
        if c == last:
            eng.wait_ge(used, n + 1)
        else:
            eng.wait_ge(full[b], FILLED[stage][b] + i + 1)
        return b

    ctx.enter_context(nc.allow_non_contiguous_dma(reason="the state's rows are short"))
    block = ctx.enter_context(nc.Block())

    @block.sync
    def _(sp):
        def load(n, p):
            sp.dma_start(raw[:, p, :], slabs[bass.ds(n, 1)].rearrange("a p n -> p (a n)")).then_inc(sem(f"raw_in{p}"), 16)

        load(0, 0)
        load(1, 1)
        with sp.Fori(1, (S_XO + 4) // 2) as i:
            for p in range(2):
                sp.wait_ge(split_done, 2 * i + p - 1)
                load(2 * i + p, p)
        sp.wait_ge(sem("x_restored"), 2 * NB)
        for n in range(4 * SB):
            if n >= RING:
                sp.wait_ge(sem("dec_used"), n - RING + 1)
            sp.dma_start(dkv[:, n % RING, :], dec_kv[n]).then_inc(sem(f"dec_in{n % RING}"), 16)
        with sp.Fori((S_XO + 4) // 2, NSLAB // 2) as i:
            for p in range(2):
                sp.wait_ge(split_done, 2 * i + p - 1)
                load(2 * i + p, p)
        for c, (a, z) in enumerate(CHUNKS):
            sp.wait_ge(sem("y_ready"), c + 1)
            sp.dma_start(yT[:, :, a:z], xf[:, :, a:z]).then_inc(sem("y_out"), 16)
        sp.wait_ge(sem("y_out"), 48)
        sp.wait_ge(sem("k_out"), 16)
        sp.wait_ge(sem("v_out"), 16)
        sp.wait_ge(sem("conv_out"), 32 * CB)
        for g in range(PB):
            sp.wait_ge(sem(f"pool_out{g}"), 32)

    @block.gpsimd
    def _(pool):
        high_done = sem("high_done")
        one = ones[:].broadcast_to([P, SLAB])
        pool.memset(ones[:], 1.0).then_inc(sem("one_set"), 1)
        pool.wait_ge(sem("one_set"), 1)

        def split(n, p, turn):
            pool.wait_ge(sem(f"raw_in{p}"), 16 * (turn + 1))
            if not (isinstance(n, int) and n < 2):
                pool.wait_ge(used, n - 1)
                pool.sem_inc(sem("slot_turned"), 1)
            pool.tensor_tensor(wh[:, p, :], raw[:, p, :], one, ALU.mult).then_inc(high_done, 1)
            pool.wait_ge(high_done, n + 1)
            pool.tensor_tensor(wl[:, p, :], raw[:, p, :], wh[:, p, :].bitcast(f32), ALU.subtract).then_inc(split_done, 1)

        def splits(lo, hi):
            with pool.Fori(lo // 2, hi // 2) as i:
                for p in range(2):
                    split(2 * i + p, p, i)

        def restore(b):
            pool.tensor_tensor(xf[:, b, :], xh[:, b, :].bitcast(f32), xl[:, b, :].bitcast(f32), ALU.add)\
                .then_inc(sem("x_restored"), 1)

        split(0, 0, 0)
        split(1, 1, 0)
        pool.memset(qf[:, 0:CB, 0:CTX], 0.0).then_inc(sem("pad_done"), 1)
        pool.memset(qf[:, CB:CB + 2, 0:PCTX], 0.0).then_inc(sem("pad_done"), 1)
        splits(2, 10)
        for i in range(CB):
            split(10 + 2 * i, 0, 5 + i)
            for b in range(6):
                pool.wait_ge(free[b], FREED["A"][b] + i + 1)
            pool.tensor_tensor(qf[:, i, CTX:EXT], s[:, 3, 0:TP], s[:, 2, 0:TP], ALU.mult).then_inc(sem("u_done"), 1)
            pool.tensor_tensor(conv_dec(i)[:, :, CTX:DEXT], by_request(s[:, 3, TP:T]), by_request(s[:, 2, TP:T]),
                               ALU.mult).then_inc(sem("u_done"), 1)
            split(11 + 2 * i, 1, 5 + i)
        splits(18, 28)
        pool.memset(qf[:, CB + 2:CB + 4, 0:PCTX], 0.0).then_inc(sem("pad_done"), 1)
        pool.wait_ge(used, S_E1)
        restore(0)
        restore(1)
        split(28, 0, 14)
        split(29, 1, 14)
        for b in range(2, NB):
            restore(b)
        splits(30, 46)
        pool.wait_ge(used, S_XQ + 8)
        for b in range(NB):
            restore(b)
        pool.wait_ge(sem("x_restored"), NB + 3)
        pool.memset(qz[:], 0.0).then_inc(sem("dec_q_zero"), 1)
        pool.wait_ge(sem("dec_q_zero"), 1)
        pool.wait_ge(sem("q_low"), 24)
        for h in range(HEADS):
            part = [q[:, 2 * h:2 * h + 2, j, TP:T].bitcast(f32).rearrange("p f (n t) -> p f n t", n=SB) for j in range(2)]
            pool.tensor_tensor(qz[:, 2 * h:2 * h + 2, :, h * ST:(h + 1) * ST], part[0], part[1], ALU.add)\
                .then_inc(sem("dec_q"), 1)
        splits(46, NSLAB)

    @block.tensor
    def _(pe):
        def take(b, n):
            if not (isinstance(n, int) and n == 0):
                pe.wait_ge(free[b], n)

        def product(out, w_high, w_low, x_high, x_low, first, last):
            pe.matmul(out, w_high, x_high, start=first, stop=False)
            pe.matmul(out, w_high, x_low, start=False, stop=False)
            return pe.matmul(out, w_low, x_high, start=False, stop=last)

        def slab(stage, n, p, i, parts, chunks=CHUNKS, ready=None):
            pe.wait_ge(split_done, n + 1)
            for c, (a, z) in enumerate(chunks):
                b = 3 * p + c
                take(b, FREED[stage][b] + i)
                for k in range(NB):
                    if ready:
                        ready(c, k)
                    w = slice(k * P, (k + 1) * P)
                    high, low = parts(k, a, z)
                    last = product(ps[b][:, 0:z - a], wh[:, p, w], wl[:, p, w], high, low, k == 0, k == NB - 1)
                last.then_inc(used if c == len(chunks) - 1 else full[b], 1)

        def x_parts(k, a, z):
            return xh[:, k, a:z], xl[:, k, a:z]

        def q_parts(k, a, z):
            return q[:, k, 0, a:z], q[:, k, 1, a:z]

        def mem_parts(k, a, z):
            return mem[:, 0, k, a:z], mem[:, 1, k, a:z]

        def pairs(stage, n0, lo, hi, parts, chunks=CHUNKS, ready=None):
            with pe.Fori(lo, hi) as i:
                for p in range(2):
                    slab(stage, n0 + 2 * i + p, p, i, parts, chunks, ready)

        def first_pair(stage, n0, parts, chunks=CHUNKS, ready=None):
            for p in range(2):
                slab(stage, n0 + p, p, 0, parts, chunks, ready if p == 0 else None)

        MEM = ((0, NMEM),)
        pe.wait_ge(sem("mem_low"), 1)
        first_pair("K", S_K, mem_parts, MEM)
        pairs("K", S_K, 1, 4, mem_parts, MEM)

        def x_ready(c, k):
            if c == 0:
                pe.wait_ge(sem("x_low"), k + 1)

        first_pair("A", S_A, x_parts, ready=x_ready)
        pairs("A", S_A, 1, 4, x_parts)
        first_pair("P0", S_P0, x_parts)

        with pe.Fori(0, 4) as i:
            for p in range(2):
                pe.wait_ge(split_done, S_V + 2 * i + p + 1)
                for mt in range(2):
                    b = 3 * mt
                    if p == 0:
                        take(b, FREED["V"][b] + i)
                    m = slice(mt * P, (mt + 1) * P)
                    for k in range(4):
                        w = slice(k * 256, (k + 1) * 256)
                        last = product(ps[b][:, 0:256], mem[:, 0, 4 * p + k, m], mem[:, 1, 4 * p + k, m],
                                       wh[:, p, w], wl[:, p, w], p == 0 and k == 0, p == 1 and k == 3)
                    if mt == 1:
                        last.then_inc(used, 1)
                    elif p == 1:
                        last.then_inc(full[b], 1)
        first_pair("P2", S_P2, x_parts)

        pe.wait_ge(sem("pool_w_in"), 16)
        for g in range(PB):
            pe.wait_ge(sem("delta_done"), 2 * (g + 1))
            for c, (a, z) in enumerate(CHUNKS):
                b = 3 * (g % 2) + c
                take(b, FREED["PM"][b] + g // 2)
                w = poolw[:, g * P:(g + 1) * P]
                zp = min(z, TP)
                last = pe.matmul(ps[b][:, 0:zp - a], w, qf[:, CB + g, PCTX + a:PCTX + zp], start=True, stop=True)
                if z > TP:
                    last = pe.matmul(ps[b][:, zp - a:z - a], w, pool_dec(g)[:, :, PCTX:DPEXT], start=True, stop=True)
                last.then_inc(full[b], 1)

        def half(stage, n0, k0):
            with pe.Fori(0, 2) as i:
                for p in range(2):
                    pe.wait_ge(split_done, n0 + 2 * i + p + 1)
                    for m in range(2):
                        for c, (a, z) in enumerate(CHUNKS):
                            b = 3 * m + c
                            take(b, FREED[stage][b] + 2 * i + p)
                            for k in range(4):
                                w = slice((m * 4 + k) * P, (m * 4 + k + 1) * P)
                                last = product(ps[b][:, 0:z - a], wh[:, p, w], wl[:, p, w],
                                               *q_parts(k0 + k, a, z), k == 0, k == 3)
                            last.then_inc(used if b == 5 else full[b], 1)

        pe.wait_ge(sem("mix_low"), PB)
        half("E1", S_E1, CB)

        def spread_back(stage, bank, i, c, tiles):
            take(bank, FREED[stage][bank] + i)
            for t in range(3 * c, min(3 * c + 3, NT)):
                o = TILES[t] - CHUNKS[c][0]
                last = pe.transpose(ps[bank][:, o:o + P], tiles[:, t, :], ident)
            last.then_inc(full[bank], 1)

        for i in range(CB):
            pe.wait_ge(sem("conv_kept"), i + 1)
            for c, (a, z) in enumerate(CHUNKS):
                b = 3 * (i % 2) + c
                take(b, FREED["GM"][b] + i // 2)
                pe.matmul(ps[b][:, 0:z - a], inv64, qf[:, i, a:z], start=True, stop=True).then_inc(full[b], 1)
        take(6, FREED["GS"][6])
        for i in range(CB):
            pe.wait_ge(sem("gn_sq"), i + 1)
            for t, t0 in enumerate(TILES):
                o = (i * NT + t) * 2
                last = pe.matmul(ps[6][:, o:o + 2], qf[:, i, T + t0:T + t0 + P], col("half", 0, 2), start=True, stop=True)
        last.then_inc(full[6], 1)
        for i in range(CB):
            pe.wait_ge(sem("gn_spread"), i + 1)
            for c in range(3):
                spread_back("GT", 3 * (i % 2) + c, i // 2, c, spread[:, i % 3])
        pe.wait_ge(sem("mix_low"), PB + CB)
        half("E2", S_E2, 0)

        def ln_first_mean(n, x0):
            for c, (a, z) in enumerate(CHUNKS):
                b = 6 + c % 2
                take(b, FREED[f"C{n}"][b] + c // 2)
                pe.matmul(ps[b][:, 0:z - a], inv128, x0(a, z), start=True, stop=True).then_inc(full[b], 1)

        def ln_stats(n, sums, squares):
            pe.wait_ge(sem("ln_sums"), n)
            take(6, FREED[f"S{n}"][6])
            for j, src in enumerate((sums, squares)):
                for t, t0 in enumerate(TILES):
                    last = pe.matmul(ps[6][:, j * NT + t:j * NT + t + 1], src[:, t0:t0 + P], col("inv_d"),
                                     start=True, stop=True)
            last.then_inc(full[6], 1)
            pe.wait_ge(sem("ln_spread"), 2 * n)
            for c in range(3):
                for j in range(2):
                    spread_back(f"T{n}", 3 * j + c, 0, c, lnspread[:, j])

        pe.wait_ge(sem("ln_y"), 8)
        ln_first_mean(1, lambda a, z: xf[:, 0, a:z])
        ln_stats(1, s[:, 0, :], s[:, 1, :])

        def x_normed(n):
            def ready(c, k):
                if k == 0:
                    pe.wait_ge(sem("x_norm_low"), 3 * (n - 1) + c + 1)
            return ready

        first_pair("XQ", S_XQ, x_parts, ready=x_normed(1))
        pairs("XQ", S_XQ, 1, 4, x_parts)

        def scores(t):
            for h in range(HEADS):
                b = 2 * (t % 2) + h // 2
                if h % 2 == 0:
                    take(b, FREED["ATT"][b] + t // 2)
                o = (h % 2) * NMEM
                for k in range(2):
                    f = 2 * h + k
                    tok = slice(t * P, (t + 1) * P)
                    last = product(ps[b][:, o:o + NMEM], q[:, f, 0, tok], q[:, f, 1, tok], kh[:, f, :], kl[:, f, :],
                                   k == 0, k == 1)
                if h % 2 == 1:
                    last.then_inc(full[b], 1)

        def prob_transposes(i, hh):
            for t in range(2):
                pe.wait_ge(sem("prob_done"), 2 * i + t + 1)
                b = 4 + t
                take(b, FREED["ATT"][b] + 2 * i + hh)
                for j in range(4):
                    m = (4 * hh + j) * P
                    last = pe.transpose(ps[b][:, j * P:(j + 1) * P], prob[:, t, m:m + P], ident)
                last.then_inc(full[b], 1)

        def values(i, hh):
            pe.wait_ge(sem("prob_t_low"), 2 * (2 * i + hh) + 2)
            for f in range(4):
                b = 6 + f // 2
                if f % 2 == 0:
                    take(b, FREED["ATT"][b] + 2 * i + hh)
                for mt in range(2):
                    w = slice((4 * hh + f) * P, (4 * hh + f + 1) * P)
                    j = 2 * (f // 2) + mt
                    last = product(ps[b][:, (f % 2) * 2 * P:(f % 2 + 1) * 2 * P], vh[:, mt, w], vl[:, mt, w],
                                   pth[:, hh, j, :], ptl[:, hh, j, :], mt == 0, mt == 1)
                if f % 2 == 1:
                    last.then_inc(full[b], 1)

        pe.wait_ge(sem("q_low"), 24)
        pe.wait_ge(sem("kv_low"), 2)
        scores(0)
        scores(1)
        for i in range(4):
            prob_transposes(i, 0)
            if i < 3:
                scores(2 * i + 2)
            prob_transposes(i, 1)
            if i < 3:
                scores(2 * i + 3)
            values(i, 0)
            values(i, 1)

        ROWS = HEADS * ST

        def dec_chunk(c):
            pe.wait_ge(sem(f"dec_in{c % RING}"), 16 * (c // RING + 1))
            return dkv[:, c % RING]

        def dec_scores(n):
            b = n % 4
            take(b, FREED["DEC"][b] + n // 4)
            for k in range(2):
                keys = dec_chunk(2 * n + k)
                for f in range(4):
                    last = pe.matmul(ps[b][0:ROWS, 0:NMEM], qz[:, 4 * k + f, n, :], keys[:, f * NMEM:(f + 1) * NMEM],
                                     start=(k == 0 and f == 0), stop=(k == 1 and f == 3))
                last.then_inc(sem("dec_used"), 1)

        def dec_transposes(n):
            b = 4 + n % 2
            take(b, FREED["DEC"][b] + n // 2)
            pe.wait_ge(sem("dec_prob"), n + 1)
            for mt in range(2):
                last = pe.transpose(ps[b][:, mt * ROWS:(mt + 1) * ROWS], dprob[:, n, mt * P:(mt + 1) * P],
                                    ident[0:ROWS, 0:ROWS])
            last.then_inc(sem("dec_pt_full"), 1)

        def dec_values(n):
            b = 0 if n % 2 else 6
            for j in range(2):
                take(b + j, FREED["DEC"][b + j] + n // 2 + (2 if n % 2 else 0))
            pe.wait_ge(sem("dec_pt"), n + 1)
            for mt in range(2):
                vals = dec_chunk(2 * SB + 2 * n + mt)
                for j in range(2):
                    last = pe.matmul(ps[b + j][0:ROWS, :], dpt[:, n, mt, :], vals[:, j * 512:(j + 1) * 512],
                                     start=(mt == 0), stop=(mt == 1))
                last.then_inc(sem("dec_used"), 1)

        def dec_pick(n):
            pe.wait_ge(sem("dec_o"), 2 * (n + 1))
            for f in range(NB):
                h = f // 2
                last = pe.matmul(ps[2][:, f * TS + n * ST:f * TS + (n + 1) * ST], dout[:, n % 2, f * P:(f + 1) * P],
                                 ident[0:ROWS, h * ST:(h + 1) * ST], start=True, stop=True)
            last.then_inc(sem("dec_picked"), 1)

        pe.wait_ge(sem("dec_q"), HEADS)
        for n in range(SB):
            dec_scores(n)
            if n >= 2:
                dec_transposes(n - 2)
        dec_transposes(SB - 2)
        dec_values(0)
        dec_transposes(SB - 1)
        take(2, FREED["DEC"][2] + 2)
        for n in range(1, SB):
            dec_values(n)
            dec_pick(n - 1)
        dec_pick(SB - 1)

        pe.wait_ge(sem("o_low"), 2 * 8 + 1)
        first_pair("XO", S_XO, q_parts)
        pe.wait_ge(sem("ln_y"), 9)
        ln_first_mean(2, lambda a, z: xf[:, 0, a:z])
        pairs("XO", S_XO, 1, 4, q_parts)
        ln_stats(2, s[:, 0, :], s[:, 1, :])

        for g in range(FFG):
            n0 = S_FF + g * 2 * GB
            first_pair(f"W1{g}", n0, x_parts, ready=x_normed(2) if g == 0 else None)
            pairs(f"W1{g}", n0, 1, 4, x_parts)

            def hidden_ready(c, k, g=g):
                if k == 0:
                    pe.wait_ge(sem("hidden_low"), 24 * g + 21)
                if k == NB - 1:
                    pe.wait_ge(sem("hidden_low"), 24 * g + 21 + c + 1)

            first_pair(f"W2{g}", n0 + GB, q_parts, ready=hidden_ready)
            if g == FFG - 1:
                pe.wait_ge(sem("ln_y"), 10)
                ln_first_mean(3, lambda a, z: xf[:, 0, a:z])
            pairs(f"W2{g}", n0 + GB, 1, 4, q_parts)
        ln_stats(3, s3[:, 0, :], s3[:, 1, :])

    @block.scalar
    def _(act):
        own = Own(act, "act_own")

        def load(out, in_, name):
            act.dma_start(out, in_).then_inc(sem(name), 16)

        load(memf[:, 1], memT, "mem_in")
        load(par[:], params, "const_in")
        load(con[:], consts, "const_in")
        for b in range(NB):
            load(xf[:, b, :], xT[:, b, :], f"x_in{b}")
        for i in range(CB):
            load(conv_dec(i)[:, :, 0:CTX], conv_state[:, i], "conv_state_in")
        for g in range(2):
            load(pool_dec(g)[:, :, 0:PCTX], pool_state[:, g], "pool_state_in")
        load(poolw, pool_w, "pool_w_in")

        act.wait_ge(sem("mem_in"), 16)
        act.copy(mem[:, 0], memf[:, 1]).then_inc(sem("mem_high"), 1)
        for j in range(NB):
            b = slab_arrived(act, "K", S_K + j, j % 2, 0, j // 2, last=0)
            act.copy(kf[:, j, :], ps[b][:, 0:NMEM]).then_inc(sem("k_full"), 1)
            act.copy(kh[:, j, :], ps[b][:, 0:NMEM]).then_inc(free[b], 1)
            act.wait_ge(sem(f"x_in{j}"), 16)
            act.copy(xh[:, j, :], xf[:, j, :]).then_inc(sem("x_high"), 1)
        act.wait_ge(sem("k_full"), NB)
        act.dma_start(kT, kf[:]).then_inc(sem("k_out"), 16)

        act.wait_ge(sem("const_in"), 32)
        for i in range(CB):
            if i >= 1:
                act.wait_ge(sem("u_done"), 2 * i)
            for c, (a, z) in enumerate(CHUNKS):
                b = slab_arrived(act, "A", S_A + 2 * i, 0, c, i)
                act.activation(s[:, 3, a:z], ps[b][:, 0:z - a], ACT.Identity, bias=col("b_in", i)).then_inc(free[b], 1)
            for c, (a, z) in enumerate(CHUNKS):
                b = slab_arrived(act, "A", S_A + 2 * i + 1, 1, c, i)
                act.activation(s[:, 2, a:z], ps[b][:, 0:z - a], ACT.Sigmoid, bias=col("b_in", CB + i)).then_inc(free[b], 1)
            act.wait_ge(sem("u_done"), 2 * (i + 1))
            act.dma_start(conv_p[:, i], qf[:, i, EXT - CTX:EXT]).then_inc(sem("conv_out"), 16)
            act.wait_ge(sem("conv_state_in"), 16 * CB)
            act.dma_start(conv_s[:, i], conv_dec(i)[:, :, ST:DEXT]).then_inc(sem("conv_out"), 16)

        def keep_conv(i):
            act.wait_ge(sem("conv_done"), i + 1)
            if i == 0:
                act.wait_ge(sem("conv_out"), 16 * 2 * CB)
            act.copy(qf[:, i, 0:T], s[:, i % 2, :]).then_inc(sem("conv_kept"), 1)

        def pool_inputs(stage, n0, g0):
            for p in range(2):
                g = g0 + p
                for c, (a, z) in enumerate(CHUNKS):
                    b = slab_arrived(act, stage, n0 + p, p, c, 0)
                    zp = min(z, TP)
                    ins = act.activation(qf[:, CB + g, PCTX + a:PCTX + zp], ps[b][:, 0:zp - a], ACT.Identity,
                                         bias=col("b_in", 2 * CB + g))
                    if z > TP:
                        own.done(ins)
                        ins = act.activation(pool_dec(g)[:, :, PCTX:DPEXT], by_request(ps[b][:, zp - a:z - a]),
                                             ACT.Identity, bias=col("b_in", 2 * CB + g))
                    ins.then_inc(free[b], 1)
                    if z > TP:
                        own.wait()
                        act.wait_ge(free[b], FREED[stage][b] + 1)
                act.wait_ge(free[3 * p], FREED[stage][3 * p] + 1)
                act.wait_ge(free[3 * p + 1], FREED[stage][3 * p + 1] + 1)
                act.wait_ge(sem("pool_state_in"), 16 * (2 if g < 2 else 4))
                act.dma_start(pool_p[:, g], qf[:, CB + g, PEXT - PCTX:PEXT]).then_inc(sem(f"pool_out{g}"), 16)
                act.dma_start(pool_s[:, g], pool_dec(g)[:, :, ST:DPEXT]).then_inc(sem(f"pool_out{g}"), 16)

        keep_conv(0)
        pool_inputs("P0", S_P0, 0)
        keep_conv(1)
        for i in range(4):
            for mt in range(2):
                b = 3 * mt
                if mt == 0:
                    act.wait_ge(full[b], FILLED["V"][b] + i + 1)
                else:
                    act.wait_ge(used, S_V + 2 * i + 2)
                w = slice(i * 256, (i + 1) * 256)
                act.copy(vf[:, mt, w], ps[b][:, 0:256]).then_inc(sem("v_full"), 1)
                act.copy(vh[:, mt, w], ps[b][:, 0:256]).then_inc(free[b], 1)
        act.wait_ge(sem("v_full"), NB)
        act.dma_start(v_out, vf[:]).then_inc(sem("v_out"), 16)
        for g in range(2, PB):
            load(pool_dec(g)[:, :, 0:PCTX], pool_state[:, g], "pool_state_in")
        pool_inputs("P2", S_P2, 2)
        keep_conv(2)

        for g in range(PB):
            banks = [3 * (g % 2) + c for c in range(3)]
            act.wait_ge(full[banks[2]], FILLED["PM"][banks[2]] + g // 2 + 1)
            for c, (a, z) in enumerate(CHUNKS):
                b = banks[c]
                act.wait_ge(full[b], FILLED["PM"][b] + g // 2 + 1)
                act.activation(qf[:, CB + g, T + a:T + z], ps[b][:, 0:z - a], ACT.Copy, scale=col("pool_scale", g))\
                    .then_inc(free[b], 1)
            for b in banks:
                act.wait_ge(free[b], FREED["PM"][b] + g // 2 + 1)
            act.copy(q[:, CB + g, 0, :], qf[:, CB + g, T:2 * T]).then_inc(sem("mix_high"), 1)
        keep_conv(3)

        for i in range(CB):
            act.wait_ge(sem("gn_d"), 3 * (i + 1))
            act.activation(qf[:, i, T:2 * T], qf[:, i, 0:T], ACT.Square).then_inc(sem("gn_sq"), 1)
        act.wait_ge(full[6], FILLED["GS"][6] + 1)
        act.activation(small[:, 0:72], ps[6][:, 0:72], ACT.Sqrt, bias=col("eps")).then_inc(free[6], 1)
        act.wait_ge(sem("gn_rstd"), 1)
        for i in range(CB):
            if i == 3:
                act.wait_ge(full[2], FILLED["GT"][2] + 1)
            src = small[:, 18 * i:18 * (i + 1)].rearrange("p (t g) -> p t g", g=2)
            for g in range(2):
                ins = act.copy(spread[:, i % 3, :, 64 * g:64 * (g + 1)],
                               src[:, :, g:g + 1].broadcast_to([P, NT, 64]))
                if g == 0:
                    own.done(ins)
                else:
                    own.wait()
                    ins.then_inc(sem("gn_spread_half"), 1)
                    act.wait_ge(sem("gn_spread_half"), i + 1)
                    act.sem_inc(sem("gn_spread"), 1)
        for i in range(CB):
            act.wait_ge(sem("gn_n"), 3 * (i + 1))
            act.activation(qf[:, i, T:2 * T], qf[:, i, 0:T], ACT.Silu, scale=col("gn_g", i), bias=col("gn_b", i))\
                .then_inc(sem("gn_out"), 1)
            act.wait_ge(sem("gn_out"), i + 1)
            act.copy(q[:, i, 0, :], qf[:, i, T:2 * T]).then_inc(sem("mix_high"), 1)

        def ln(n, scr):
            for c, (a, z) in enumerate(CHUNKS):
                b = 6 + c % 2
                act.wait_ge(full[b], FILLED[f"C{n}"][b] + c // 2 + 1)
                act.copy(scr[:, 2, a:z], ps[b][:, 0:z - a]).then_inc(free[b], 1)
            for j in range(NB):
                act.wait_ge(sem("ln_d"), NB * (n - 1) + j + 1)
                if j:
                    act.wait_ge(sem("ln_sq_used"), NB * (n - 1) + j)
                act.activation(scr[:, 3, :], xf[:, j, :], ACT.Square).then_inc(sem("ln_sq"), 1)
            act.wait_ge(sem("ln_var"), n)
            act.activation(small[:, 0:NT], small[:, 32:32 + NT], ACT.Sqrt, bias=col("eps")).then_inc(sem("ln_std"), 1)
            act.wait_ge(sem("ln_e"), n)
            for j in range(2):
                act.copy(lnspread[:, j], small[:, 16 * j + 48:16 * j + 48 + NT].unsqueeze(2).broadcast_to([P, NT, P]))\
                    .then_inc(sem("ln_spread"), 1)

        def x_high(n):
            for c, (a, z) in enumerate(CHUNKS):
                act.wait_ge(sem("x_norm"), NB * (3 * (n - 1) + c + 1))
                act.copy(xh[:, :, a:z], xf[:, :, a:z]).then_inc(sem("x_norm_high"), 1)

        ln(1, s)
        x_high(1)

        with act.Fori(0, 4) as i:
            for p in range(2):
                for c, (a, z) in enumerate(CHUNKS):
                    b = slab_arrived(act, "XQ", S_XQ + 2 * i + p, p, c, i)
                    act.copy(q[:, bass.ds(2 * i + p, 1), 0, a:z], ps[b][:, 0:z - a].unsqueeze(1)).then_inc(sem("q_high"), 1)

        def prob_exp(t):
            act.wait_ge(sem("neg_max"), t + 1)
            for h in range(HEADS):
                b = 2 * (t % 2) + h // 2
                if t >= 2 and h == 0:
                    f = 4 + t % 2
                    act.wait_ge(full[f], FILLED["ATT"][f] + 2 * (t // 2))
                ins = act.activation(prob[:, t % 2, h * NMEM:(h + 1) * NMEM], ps[b][:, (h % 2) * NMEM:(h % 2 + 1) * NMEM],
                                     ACT.Exp, bias=small[:, 8 * (t % 2) + h:8 * (t % 2) + h + 1], scale=SCALE,
                                     accum_out=small[:, 16 + 8 * (t % 2) + h:16 + 8 * (t % 2) + h + 1])
                ins.then_inc(sem("exp_done"), 1)
                if h % 2:
                    act.wait_ge(sem("exp_done"), 4 * t + h + 1)
                    act.sem_inc(free[b], 1)

        def prob_t_high(i, hh):
            for t in range(2):
                b = 4 + t
                act.wait_ge(full[b], FILLED["ATT"][b] + 2 * i + hh + 1)
                if i:
                    act.wait_ge(full[7], FILLED["ATT"][7] + 2 * i + hh - 1)
                act.copy(pth[:, hh, :, t * P:(t + 1) * P], ps[b][:].rearrange("p (j n) -> p j n", j=4))\
                    .then_inc(sem("prob_t_high"), 1)

        def o_high(i, hh):
            for j in range(2):
                b = 6 + j
                act.wait_ge(full[b], FILLED["ATT"][b] + 2 * i + hh + 1)
                f = 4 * hh + 2 * j
                act.copy(q[:, f:f + 2, 0, 2 * P * i:2 * P * (i + 1)], ps[b][:].rearrange("p (j n) -> p j n", j=2))\
                    .then_inc(sem("o_high"), 1)

        prob_exp(0)
        prob_exp(1)
        for i in range(4):
            prob_t_high(i, 0)
            prob_t_high(i, 1)
            if i < 3:
                prob_exp(2 * i + 2)
                prob_exp(2 * i + 3)
            o_high(i, 0)
            o_high(i, 1)

        R = HEADS * ST

        def dec_prob_t(n):
            act.wait_ge(sem("dec_pt_full"), n + 1)
            b = 4 + n % 2
            act.copy(dpt[:, n], ps[b][:, 0:2 * R].rearrange("p (m r) -> p m r", m=2)).then_inc(sem("dec_pt"), 1)
            act.wait_ge(sem("dec_pt"), n + 1)
            act.sem_inc(free[b], 1)

        def dec_out(n):
            act.wait_ge(sem("dec_used"), 2 * SB + 2 * (n + 1))
            if n >= 2:
                act.wait_ge(sem("dec_picked"), n - 1)
            b = 0 if n % 2 else 6
            for j in range(2):
                act.copy(dout[:, n % 2, j * 512:(j + 1) * 512], ps[b + j][0:R, :]).then_inc(sem("dec_o"), 1)
            act.wait_ge(sem("dec_o"), 2 * (n + 1))
            for j in range(2):
                act.sem_inc(free[b + j], 1)

        for n in range(SB):
            act.wait_ge(sem("dec_max"), n + 1)
            act.activation(dprob[:, n, :], ps[n % 4][0:R, 0:NMEM], ACT.Exp, bias=small[0:R, 48 + n:49 + n], scale=SCALE,
                           accum_out=small[0:R, 56 + n:57 + n]).then_inc(free[n % 4], 1)
            if n >= 2:
                dec_prob_t(n - 2)
        dec_prob_t(SB - 2)
        dec_out(0)
        dec_prob_t(SB - 1)
        for n in range(1, SB):
            dec_out(n)
        act.wait_ge(sem("dec_picked"), SB)
        act.copy(q[:, :, 0, TP:T], ps[2][:, 0:NMEM].rearrange("p (f n) -> p f n", n=TS)).then_inc(sem("o_high"), 1)

        ln(2, s)
        x_high(2)

        for g in range(FFG):
            stage, n0 = f"W1{g}", S_FF + g * 2 * GB
            for i in range(GB // 2):
                for p in range(2):
                    j = 2 * i + p
                    for c, (a, z) in enumerate(CHUNKS):
                        done = 24 * g + 3 * j + c
                        b = slab_arrived(act, stage, n0 + j, p, c, i)
                        if done >= 6:
                            act.wait_ge(sem("square"), done - 5)
                        act.activation(relu[:, p, a:z], ps[b][:, 0:z - a], ACT.Relu, bias=col("b1", GB * g + j))\
                            .then_inc(free[b], 1)
                        act.wait_ge(sem("square"), done + 1)
                        act.copy(q[:, j, 0, a:z], qf[:, j, T + a:T + z]).then_inc(sem("hidden_high"), 1)
        ln(3, s3)

    @block.vector
    def _(dve):
        own = Own(dve, "dve_own")
        stt, tt, ts = dve.scalar_tensor_tensor, dve.tensor_tensor, dve.tensor_scalar

        dve.wait_ge(sem("mem_high"), 1)
        tt(mem[:, 1], memf[:, 1], mem[:, 0].bitcast(f32), ALU.subtract).then_inc(sem("mem_low"), 1)
        for j in range(NB):
            dve.wait_ge(sem("x_high"), j + 1)
            tt(xl[:, j, :], xf[:, j, :], xh[:, j, :].bitcast(f32), ALU.subtract).then_inc(sem("x_low"), 1)
        dve.wait_ge(sem("k_out"), 16)
        dve.wait_ge(free[0], 4)
        dve.wait_ge(free[3], 4)
        tt(kl[:], kf[:], kh[:].bitcast(f32), ALU.subtract).then_inc(sem("kv_low"), 1)
        dve.wait_ge(sem("const_in"), 32)
        dve.wait_ge(sem("pad_done"), 2)

        def conv(i, lo=0, hi=TAPS):
            out = s[:, i % 2, 0:TP]
            if lo == 0:
                dve.wait_ge(sem("u_done"), 2 * (i + 1))
                if i >= 2:
                    dve.wait_ge(sem("conv_kept"), i - 1)
                own.link(ts(out, qf[:, i, 0:TP], col("conv_w", TAPS * i), col("conv_b", i), ALU.mult, ALU.add))
            for k in range(max(lo, 1), hi):
                own.link(stt(out, qf[:, i, k:k + TP], col("conv_w", TAPS * i + k), out, ALU.mult, ALU.add))
            if hi == TAPS:
                dve.wait_ge(sem("conv_state_in"), 16 * CB)
                w = col("conv_w", TAPS * i, TAPS).unsqueeze(1).broadcast_to([P, SB, TAPS])
                tmp = qf[:, i, EXT + SB * DEXT:EXT + SB * DEXT + SB * TAPS].rearrange("p (b n) -> p b n", b=SB)
                dst = by_request(s[:, i % 2, TP:T])
                for t in range(ST):
                    own.link(tt(tmp, conv_dec(i)[:, :, t:t + TAPS], w, ALU.mult))
                    own.link(dve.tensor_reduce(dst[:, :, t:t + 1], tmp, AX, ALU.add))
                ts(s[:, i % 2, TP:T], s[:, i % 2, TP:T], col("conv_b", i), None, ALU.add).then_inc(sem("conv_done"), 1)

        def window(g):
            dve.wait_ge(sem("pool_out%d" % g), 32)
            if g >= 2:
                dve.wait_ge(sem("pad_done"), 3)
            src, sdec = qf[:, CB + g, 0:PEXT], pool_dec(g)
            n, nd, w = PEXT, DPEXT, 1
            cur, cdec = src, sdec
            base = CB + g
            while w < WINDOWS[g]:
                j = 2 + (w.bit_length() - 1) % 2
                n, nd = n - w, nd - w
                nxt = s[:, j, 0:n]
                o = 1200 + 160 * (j - 2)
                ndec = qf[:, base, o:o + SB * nd].rearrange("p (b n) -> p b n", b=SB)
                tt(nxt, cur[:, w:w + n], cur[:, 0:n], ALU.add).then_inc(own.sem, 1)
                tt(ndec, cdec[:, :, w:w + nd], cdec[:, :, 0:nd], ALU.add).then_inc(own.sem, 1)
                own.n += 2
                own.wait()
                cur, cdec, w = nxt, ndec, 2 * w
            wn = WINDOWS[g]
            tok = qf[:, base, PCTX:PEXT]
            lead = PCTX - (wn - 1)
            head = small[:, 64:80]
            own.link(tt(head, cur[:, lead:lead + 16], col("ramp", 16 * g, 16), ALU.mult))
            own.link(tt(head, head, tok[:, 0:16], ALU.subtract))
            own.link(stt(tok, cur[:, lead:lead + TP], 1.0 / wn, tok, ALU.mult, ALU.subtract))
            own.link(dve.tensor_copy(tok[:, 0:16], head))
            dve.sem_inc(sem("delta_done"), 1)
            stt(sdec[:, :, PCTX:DPEXT], cdec[:, :, lead:lead + ST], 1.0 / wn, sdec[:, :, PCTX:DPEXT],
                ALU.mult, ALU.subtract).then_inc(sem("delta_done"), 1)

        conv(0)
        conv(1)
        window(0)
        window(1)
        conv(2)
        dve.wait_ge(sem("v_out"), 16)
        dve.wait_ge(free[0], FREED["V"][0] + 4)
        dve.wait_ge(free[3], FREED["V"][3] + 4)
        tt(vl[:], vf[:], vh[:].bitcast(f32), ALU.subtract).then_inc(sem("kv_low"), 1)
        window(2)
        window(3)
        for g in range(PB):
            dve.wait_ge(sem("mix_high"), g + 1)
            tt(q[:, CB + g, 1, :], qf[:, CB + g, T:2 * T], q[:, CB + g, 0, :].bitcast(f32), ALU.subtract)\
                .then_inc(sem("mix_low"), 1)

        e1 = Own(dve, "e1_sum")
        for j in range(NB):
            lo = 4 * j
            conv(3, lo, min(lo + 4, TAPS))
            dve.wait_ge(sem("x_restored"), j + 1)
            m, turn = j % 2, j // 2
            for c, (a, z) in enumerate(CHUNKS):
                b = 3 * m + c
                if b == 5:
                    dve.wait_ge(used, S_E1 + turn + 1)
                else:
                    dve.wait_ge(full[b], FILLED["E1"][b] + turn + 1)
                stt(xf[:, j, a:z], xf[:, j, a:z], ALPHA, ps[b][:, 0:z - a], ALU.mult, ALU.add).then_inc(free[b], 1)

        for i in range(CB):
            for c, (a, z) in enumerate(CHUNKS):
                b = 3 * (i % 2) + c
                dve.wait_ge(full[b], FILLED["GM"][b] + i // 2 + 1)
                tt(qf[:, i, a:z], qf[:, i, a:z], ps[b][:, 0:z - a], ALU.subtract).then_inc(free[b], 1)
            for c in range(3):
                b = 3 * (i % 2) + c
                dve.wait_ge(free[b], FREED["GM"][b] + i // 2 + 1)
                dve.sem_inc(sem("gn_d"), 1)
        dve.wait_ge(free[6], FREED["GS"][6] + 1)
        dve.reciprocal(small[:, 0:72], small[:, 0:72]).then_inc(sem("gn_rstd"), 1)
        for i in range(CB):
            for c, (a, z) in enumerate(CHUNKS):
                b = 3 * (i % 2) + c
                dve.wait_ge(full[b], FILLED["GT"][b] + i // 2 + 1)
                tt(qf[:, i, a:z], qf[:, i, a:z], ps[b][:, 0:z - a], ALU.mult).then_inc(free[b], 1)
            for c in range(3):
                b = 3 * (i % 2) + c
                dve.wait_ge(free[b], FREED["GT"][b] + i // 2 + 1)
                dve.sem_inc(sem("gn_n"), 1)
        for i in range(CB):
            dve.wait_ge(sem("mix_high"), PB + i + 1)
            tt(q[:, i, 1, :], qf[:, i, T:2 * T], q[:, i, 0, :].bitcast(f32), ALU.subtract).then_inc(sem("mix_low"), 1)

        def ln_block(n, scr, j):
            if j == 0:
                for b, k in LN_MEAN.items():
                    dve.wait_ge(free[b], FREED[f"C{n}"][b] + k)
            tt(xf[:, j, :], xf[:, j, :], scr[:, 2, :], ALU.subtract).then_inc(sem("ln_d"), 1)
            dve.wait_ge(sem("ln_d"), NB * (n - 1) + j + 1)
            if j == 0:
                own.done(dve.tensor_copy(scr[:, 0, :], xf[:, j, :]))
            else:
                own.done(tt(scr[:, 0, :], scr[:, 0, :], xf[:, j, :], ALU.add))
            dve.wait_ge(sem("ln_sq"), NB * (n - 1) + j + 1)
            own.wait()
            if j == 0:
                ins = dve.tensor_copy(scr[:, 1, :], scr[:, 3, :])
            else:
                ins = tt(scr[:, 1, :], scr[:, 1, :], scr[:, 3, :], ALU.add)
            ins.then_inc(sem("ln_sq_used"), 1)
            dve.wait_ge(sem("ln_sq_used"), NB * (n - 1) + j + 1)

        def ln_finish(n, out=None):
            dve.sem_inc(sem("ln_sums"), 1)
            dve.wait_ge(full[6], FILLED[f"S{n}"][6] + 1)
            mean, var, rstd, shift = (small[:, o:o + NT] for o in (16, 32, 48, 64))
            own.link(dve.tensor_copy(mean, ps[6][:, 0:NT]))
            own.link(tt(var, mean, mean, ALU.mult))
            tt(var, ps[6][:, NT:2 * NT], var, ALU.subtract).then_inc(free[6], 1)
            dve.wait_ge(free[6], FREED[f"S{n}"][6] + 1)
            dve.sem_inc(sem("ln_var"), 1)
            dve.wait_ge(sem("ln_std"), n)
            own.link(dve.reciprocal(rstd, small[:, 0:NT]))
            stt(shift, mean, -1.0, rstd, ALU.mult, ALU.mult).then_inc(sem("ln_e"), 1)
            for c, (a, z) in enumerate(CHUNKS):
                for j, op in enumerate((ALU.mult, ALU.add)):
                    b = 3 * j + c
                    dve.wait_ge(full[b], FILLED[f"T{n}"][b] + 1)
                    tt(xf[:, :, a:z], xf[:, :, a:z], over_blocks(ps[b][:, 0:z - a]), op).then_inc(free[b], 1)
                    dve.wait_ge(free[b], FREED[f"T{n}"][b] + 1)
                for j in range(NB):
                    ts(xf[:, j, a:z], xf[:, j, a:z], col(f"ln{n}_g", j), col(f"ln{n}_b", j), ALU.mult, ALU.add)\
                        .then_inc(sem("x_norm"), 1)
                if out:
                    dve.wait_ge(sem("x_norm"), NB * (3 * (n - 1) + c + 1))
                    dve.sem_inc(sem("y_ready"), 1)
                else:
                    dve.wait_ge(sem("x_norm_high"), 3 * (n - 1) + c + 1)
                    tt(xl[:, :, a:z], xf[:, :, a:z], xh[:, :, a:z].bitcast(f32), ALU.subtract).then_inc(sem("x_norm_low"), 1)

        for j in range(NB):
            m, turn = j % 2, j // 2
            for c, (a, z) in enumerate(CHUNKS):
                b = 3 * m + c
                if b == 5:
                    dve.wait_ge(used, S_E2 + turn + 1)
                else:
                    dve.wait_ge(full[b], FILLED["E2"][b] + turn + 1)
                tt(xf[:, j, a:z], xf[:, j, a:z], ps[b][:, 0:z - a], ALU.add).then_inc(free[b], 1)
            for c in range(3):
                dve.wait_ge(free[3 * m + c], FREED["E2"][3 * m + c] + turn + 1)
            dve.sem_inc(sem("ln_y"), 1)
        for j in range(NB):
            ln_block(1, s, j)
        ln_finish(1)

        with dve.Fori(0, 4) as i:
            for p in range(2):
                for c, (a, z) in enumerate(CHUNKS):
                    b = 3 * p + c
                    dve.wait_ge(sem("q_high"), 6 * i + 3 * p + c + 1)
                    f = bass.ds(2 * i + p, 1)
                    tt(q[:, f, 1, a:z], ps[b][:, 0:z - a].unsqueeze(1), q[:, f, 0, a:z].bitcast(f32), ALU.subtract)\
                        .then_inc(free[b], 1)
        for b in range(6):
            dve.wait_ge(free[b], FREED["XQ"][b] + 4)
        dve.sem_inc(sem("q_low"), 24)

        def neg_max(t, bank0, heads):
            o = 8 * (t % 2)
            for h in range(0, heads, 2):
                n = min(2, heads - h)
                own.done(dve.reduce_max(small[:, o + h:o + h + n], ps[bank0 + h // 2][:, 0:n * NMEM].rearrange("p (h m) -> p h m", h=n), AX))
            own.wait()
            ts(small[:, o:o + heads], small[:, o:o + heads], -SCALE, None, ALU.mult).then_inc(sem("neg_max"), 1)

        def normalise(t, heads):
            o = 8 * (t % 2)
            own.link(dve.reciprocal(small[:, 32 + o:32 + o + heads], small[:, 16 + o:16 + o + heads]))
            for h in range(heads):
                own.done(ts(prob[:, t % 2, h * NMEM:(h + 1) * NMEM], prob[:, t % 2, h * NMEM:(h + 1) * NMEM],
                            small[:, 32 + o + h:32 + o + h + 1], None, ALU.mult))
            own.wait()
            dve.sem_inc(sem("prob_done"), 1)

        def maxes(t):
            for j in range(2):
                b = 2 * (t % 2) + j
                dve.wait_ge(full[b], FILLED["ATT"][b] + t // 2 + 1)
            if t >= 2:
                dve.wait_ge(sem("exp_done"), 4 * (t - 1))
            neg_max(t, 2 * (t % 2), HEADS)

        def prob_t_low(i, hh):
            for t in range(2):
                b = 4 + t
                dve.wait_ge(sem("prob_t_high"), 2 * (2 * i + hh) + t + 1)
                tt(ptl[:, hh, :, t * P:(t + 1) * P], ps[b][:].rearrange("p (j n) -> p j n", j=4),
                   pth[:, hh, :, t * P:(t + 1) * P].bitcast(f32), ALU.subtract).then_inc(free[b], 1)
                dve.wait_ge(free[b], FREED["ATT"][b] + 2 * i + hh + 1)
                dve.sem_inc(sem("prob_t_low"), 1)

        def o_low(i, hh):
            for j in range(2):
                b = 6 + j
                dve.wait_ge(sem("o_high"), 2 * (2 * i + hh) + j + 1)
                f, tok = 4 * hh + 2 * j, slice(2 * P * i, 2 * P * (i + 1))
                tt(q[:, f:f + 2, 1, tok], ps[b][:].rearrange("p (j n) -> p j n", j=2),
                   q[:, f:f + 2, 0, tok].bitcast(f32), ALU.subtract).then_inc(free[b], 1)
                dve.wait_ge(free[b], FREED["ATT"][b] + 2 * i + hh + 1)
                dve.sem_inc(sem("o_low"), 1)

        def finish_prob(t):
            dve.wait_ge(sem("exp_done"), 4 * (t + 1))
            normalise(t, HEADS)

        maxes(0)
        maxes(1)
        finish_prob(0)
        finish_prob(1)
        dve.wait_ge(sem("x_restored"), NB + 2)
        for i in range(4):
            prob_t_low(i, 0)
            if i < 3:
                maxes(2 * i + 2)
            prob_t_low(i, 1)
            if i < 3:
                maxes(2 * i + 3)
                finish_prob(2 * i + 2)
                finish_prob(2 * i + 3)
            o_low(i, 0)
            o_low(i, 1)

        R = HEADS * ST

        def dec_max(n):
            dve.wait_ge(sem("dec_used"), 2 * (n + 1))
            c = small[0:R, 48 + n:49 + n]
            own.link(dve.reduce_max(c, ps[n % 4][0:R, 0:NMEM], AX))
            ts(c, c, -SCALE, None, ALU.mult).then_inc(sem("dec_max"), 1)

        def dec_norm(n):
            b = n % 4
            dve.wait_ge(free[b], FREED["DEC"][b] + n // 4 + 1)
            own.link(dve.reciprocal(small[0:R, 64 + n:65 + n], small[0:R, 56 + n:57 + n]))
            ts(dprob[:, n, :], dprob[:, n, :], small[0:R, 64 + n:65 + n], None, ALU.mult).then_inc(sem("dec_prob"), 1)

        for n in range(SB):
            dec_max(n)
            if n:
                dec_norm(n - 1)
        dec_norm(SB - 1)
        dve.wait_ge(sem("o_high"), 17)
        tt(q[:, :, 1, TP:T], ps[2][:, 0:NMEM].rearrange("p (f n) -> p f n", n=TS), q[:, :, 0, TP:T].bitcast(f32),
           ALU.subtract).then_inc(free[2], 1)
        dve.wait_ge(free[2], FREED["DEC"][2] + 3)
        dve.sem_inc(sem("o_low"), 1)

        def joins(stage, n0, j, add):
            p, i = j % 2, j // 2
            for c, (a, z) in enumerate(CHUNKS):
                b = slab_arrived(dve, stage, n0 + j, p, c, i)
                add(j, c, a, z, ps[b][:, 0:z - a]).then_inc(free[b], 1)
            for c in range(3):
                dve.wait_ge(free[3 * p + c], FREED[stage][3 * p + c] + i + 1)
            if j == 0:
                dve.sem_inc(sem("ln_y"), 1)

        def joins_with_norm(stage, n0, n, scr, add):
            for j in range(NB):
                joins(stage, n0, j, add)
                if j == 2:
                    ln_block(n, scr, 0)
                    ln_block(n, scr, 1)
                if j >= 2:
                    ln_block(n, scr, j)

        joins_with_norm("XO", S_XO, 2, s, lambda j, c, a, z, y: stt(xf[:, j, a:z], xf[:, j, a:z], ALPHA, y, ALU.mult, ALU.add))
        ln_finish(2)

        for g in range(FFG):
            n0 = S_FF + g * 2 * GB
            for j in range(GB):
                p = j % 2
                for c, (a, z) in enumerate(CHUNKS):
                    done = 24 * g + 3 * j + c
                    dve.wait_ge(free[3 * p + c], FREED[f"W1{g}"][3 * p + c] + j // 2 + 1)
                    full_part = qf[:, j, T + a:T + z]
                    tt(full_part, relu[:, p, a:z], relu[:, p, a:z], ALU.mult).then_inc(sem("square"), 1)
                    dve.wait_ge(sem("hidden_high"), done + 1)
                    tt(q[:, j, 1, a:z], full_part, q[:, j, 0, a:z].bitcast(f32), ALU.subtract).then_inc(sem("hidden_low"), 1)
                if g == 0:
                    own.link(ts(acc[:, j, :], xh[:, j, :].bitcast(f32), ALPHA, col("b2", j), ALU.mult, ALU.add))
                    own.link(stt(acc[:, j, :], xl[:, j, :].bitcast(f32), ALPHA, acc[:, j, :], ALU.mult, ALU.add))
            if g < FFG - 1:
                for j in range(NB):
                    p, i = j % 2, j // 2
                    for c, (a, z) in enumerate(CHUNKS):
                        b = slab_arrived(dve, f"W2{g}", n0 + GB + j, p, c, i)
                        tt(acc[:, j, a:z], acc[:, j, a:z], ps[b][:, 0:z - a], ALU.add).then_inc(free[b], 1)
                for b in range(6):
                    dve.wait_ge(free[b], FREED[f"W2{g}"][b] + 4)
            else:
                joins_with_norm(f"W2{g}", n0 + GB, 3, s3, lambda j, c, a, z, y: tt(xf[:, j, a:z], acc[:, j, a:z], y, ALU.add))
        ln_finish(3, True)

    ctx.close()


def kernel(x_prompt, x_sample, mem_prompt, cache_mem_k, cache_mem_v, state_conv, state_pool,
           w_in, b_in, conv_w, conv_b, gn_g, gn_b, pool_w, pool_scale, w_out,
           ln1_g, ln1_b, xq_w, xk_w, xv_w, xo_w, ln2_g, ln2_b, w1, b1, w2, b2, ln3_g, ln3_b):
    import numpy as np
    import concourse.bacc as bacc
    from concourse import mybir as mb
    from concourse.bass_utils import run_bass_kernel_spmd as run

    def feature_major(a):
        a = np.asarray(a)
        return a.reshape(a.shape[0], -1, P).transpose(2, 1, 0)

    def blocks(w, k=NB):
        w = np.asarray(w)
        return w.reshape(k, P, -1, P).transpose(2, 1, 0, 3).reshape(-1, P, k * P)

    def paired(w):
        return blocks(w, 4).reshape(4, 2, P, 4 * P).transpose(0, 2, 1, 3).reshape(4, P, SLAB)

    x = np.concatenate([np.asarray(x_prompt).reshape(TP, D), np.asarray(x_sample).reshape(TS, D)])
    win = blocks(w_in[0])
    order = [n for i in range(CB) for n in (i, CB + i)]
    ff = []
    up, down = blocks(w1[0]), np.asarray(w2[0]).reshape(FFG, D, D)
    for g in range(FFG):
        ff += [up[g * GB:(g + 1) * GB], blocks(down[g])]
    wo = np.asarray(w_out[0])
    wv = np.asarray(xv_w[0]).reshape(2, 4, P, 4, 256).transpose(3, 0, 2, 1, 4).reshape(NB, P, SLAB)
    slabs = np.concatenate([blocks(xk_w[0]), win[order], win[8:10], wv, win[10:12],
                            paired(wo[D_CONV:]), paired(wo[:D_CONV]), blocks(xq_w[0]), blocks(xo_w[0])] + ff)
    cols = [np.asarray(conv_w[0]).reshape(TAPS, CB, P).transpose(2, 1, 0).reshape(P, -1)]
    for v in (b_in, conv_b, gn_g, gn_b, pool_scale, ln1_g, ln1_b, ln2_g, ln2_b, ln3_g, ln3_b, b1, b2):
        cols.append(np.asarray(v[0]).reshape(-1, P).T)
    ramp = np.array([[1.0 / min(t + 1, w) for t in range(16)] for w in WINDOWS], np.float32).reshape(1, -1)
    fixed = [np.repeat(ramp, P, 0), np.full((P, 1), EPS, np.float32), np.full((P, 1), 1.0 / D, np.float32),
             np.repeat(np.eye(2, dtype=np.float32) / 64, 64, 0)]
    params = np.concatenate(cols + fixed, axis=1)
    consts = np.concatenate([np.full((P, P), 1.0 / P, np.float32),
                             np.kron(np.eye(2, dtype=np.float32), np.full((64, 64), 1.0 / 64, np.float32)),
                             np.eye(P, dtype=np.float32)], axis=1)
    ck = np.asarray(cache_mem_k[0]).transpose(0, 2, 3, 1).reshape(SB, 2, 4, P, NMEM).transpose(0, 1, 3, 2, 4).reshape(-1, P, D)
    cv = np.asarray(cache_mem_v[0]).reshape(-1, P, D)
    state = lambda a, n: np.asarray(a[0]).transpose(2, 0, 1).reshape(-1, P, SB, n).transpose(1, 0, 2, 3)
    arrays = {
        "xT": feature_major(x), "memT": feature_major(np.asarray(mem_prompt)[0]), "slabs": slabs,
        "pool_w": np.asarray(pool_w[0]).transpose(1, 0, 2).reshape(P, -1), "params": params, "consts": consts,
        "conv_state": state(state_conv, CTX), "pool_state": state(state_pool, PCTX),
        "dec_kv": np.concatenate([ck, cv]),
    }
    outs = {"yT": (P, NB, T), "kT": (P, NB, NMEM), "v_out": (P, 2, D), "conv_p": (P, CB, CTX),
            "conv_s": (P, CB, SB, CTX), "pool_p": (P, PB, PCTX), "pool_s": (P, PB, SB, PCTX)}
    nc = bacc.Bacc("TRN2", target_bir_lowering=False, num_devices=1)
    args, fed = {}, {}
    for name, a in arrays.items():
        fed[name + "_in"] = np.ascontiguousarray(a)
        args[name] = nc.dram_tensor(name + "_in", a.shape, mb.dt.float32, kind="ExternalInput").ap()
    for name, shape in outs.items():
        args[name] = nc.dram_tensor(name + "_res", shape, mb.dt.float32, kind="ExternalOutput").ap()
    decoder_step(nc, **args)
    r = run(nc, [fed], core_ids=[0]).results[0]
    got = {name: np.asarray(r[name + "_res"]) for name in outs}

    y = got["yT"].transpose(2, 1, 0).reshape(T, D)
    k = got["kT"].transpose(2, 1, 0).reshape(1, 1, NMEM, HEADS, D // HEADS)
    v = got["v_out"].transpose(1, 0, 2).reshape(1, 1, NMEM, HEADS, D // HEADS)
    cp = got["conv_p"].transpose(2, 1, 0).reshape(1, 1, CTX, D_CONV)
    cs = got["conv_s"].transpose(2, 3, 1, 0).reshape(1, SB, CTX, D_CONV)
    pp = got["pool_p"].transpose(2, 1, 0).reshape(1, 1, PCTX, D - D_CONV)
    pss = got["pool_s"].transpose(2, 3, 1, 0).reshape(1, SB, PCTX, D - D_CONV)
    return (y[:TP].reshape(1, TP, D), y[TP:].reshape(SB, ST, D), k, v, cp, cs, pp, pss)
```

```python
from contextlib import ExitStack

import concourse.bass as bass
from concourse import mybir

P = 128
D = 1024
NB = D // P
TP = 1024
SB, ST = 8, 4
TS = SB * ST
T = TP + TS
D_CONV = 512
CB = D_CONV // P
PB = 4
TAPS = 31
CTX = TAPS - 1
WINDOWS = (2, 4, 8, 16)
PCTX = 15
NMEM = 256
HEADS = 4
FF = 4096
FFG = 4
GB = FF // P // FFG
ALPHA = 2.0 ** 0.25
SCALE = 256.0 ** -0.5
EPS = 1e-5
CHUNKS = ((0, 384), (384, 768), (768, 1056))
TILES = tuple(128 * t for t in range(8)) + (T - P,)
NT = len(TILES)
PIECES = [(slice(k, k + 2), *CHUNKS[0]) for k in range(0, NB, 2)]
PIECES += [(slice(k, k + 4), *c) for c in CHUNKS[1:] for k in range(0, NB, 4)]
SLAB = NB * P

EXT = TP + CTX
DEXT = ST + CTX
PEXT = TP + PCTX
DPEXT = ST + PCTX
BLK = 2 * T

S_A, S_P, S_K, S_V, S_E1, S_E2, S_XQ, S_XO, S_FF = 0, 8, 12, 20, 28, 32, 36, 44, 52
MEM_SLABS = S_E1 - S_K
NSLAB = S_FF + FFG * 2 * GB

GROWS = 3 * 2 * CB

COLS = {}
_at = 0
for _name, _n in (("conv_w", CB * TAPS), ("b_in", 12), ("conv_b", 4), ("gn_g", 4), ("gn_b", 4), ("pool_scale", 4),
                  ("ln1_g", 8), ("ln1_b", 8), ("ln2_g", 8), ("ln2_b", 8), ("ln3_g", 8), ("ln3_b", 8),
                  ("b1", 32), ("b2", 8), ("ramp", 4 * 16), ("eps", 1), ("half", 2 * GROWS - 2)):
    COLS[_name] = _at
    _at += _n
NPAR = _at
RING = 5
NCONST = 3 * P


SIX = {b: 1 for b in range(6)}
LN_MEAN = {6: 2, 7: 1}


def times(n, banks):
    return {b: n * k for b, k in banks.items()}


LINEAR = (times(4, SIX), (2, 5))
ONE_BANK = ({0: 4, 3: 4}, (0, 3))
HALVES = (times(4, SIX), (5,))
STAGES = [("A", *LINEAR), ("P", times(2, SIX), (2, 5)), ("K", *ONE_BANK), ("V", {0: 1, 1: 1, 3: 1, 4: 1}, (3, 4)),
          ("PM", times(2, SIX), ()), ("E1", *HALVES), ("GM", {6: 6, 7: 6}, ()), ("GV", {6: 1}, ()), ("GT", {6: 6, 7: 6}, ()),
          ("E2", *HALVES), ("C1", LN_MEAN, ()), ("T1", SIX, ()),
          ("XQ", *LINEAR), ("ATT", {0: 4, 1: 4, 2: 4, 3: 4, 4: 8, 5: 8, 6: 8, 7: 8}, ()),
          ("DEC", {0: 6, 1: 6, 2: 3, 3: 2, 4: 4, 5: 4, 6: 4, 7: 4}, tuple(range(8))), ("XO", *LINEAR), ("C2", LN_MEAN, ()),
          ("T2", SIX, ())]
for _g in range(FFG):
    STAGES += [(f"W1{_g}", *LINEAR), (f"W2{_g}", *LINEAR)]
STAGES += [("C3", LN_MEAN, ()), ("T3", SIX, ())]
FREED, FILLED = {}, {}
_n, _f = {b: 0 for b in range(8)}, {b: 0 for b in range(8)}
for _name, _uses, _silent in STAGES:
    FREED[_name], FILLED[_name] = dict(_n), dict(_f)
    for _b, _k in _uses.items():
        _n[_b] += _k
        _f[_b] += 0 if _b in _silent else _k


def decoder_step(nc, xT, memT, slabs, pool_w, params, consts, conv_state, pool_state, dec_kv,
                 yT, kT, v_out, conv_p, conv_s, pool_p, pool_s):
    f32, f32r = mybir.dt.float32, mybir.dt.float32r
    ALU = mybir.AluOpType
    ACT = mybir.ActivationFunctionType
    AX = mybir.AxisListType.X
    ctx = ExitStack()

    BASE = 16512
    O_XH = BASE
    O_XL = O_XH + NB * T * 4
    O_Q = O_XL + NB * T * 4
    O_W = O_Q + NB * BLK * 4
    O_KV = O_W + 6 * SLAB * 4
    O_S = O_KV + 32768
    O_PAR = O_S + 4 * T * 4
    O_CON = O_PAR + -(-NPAR // 8) * 32
    O_SMALL = O_CON + NCONST * 4

    def at(name, shape, dt, offset):
        return nc.alloc_sbuf_tensor_at(name, shape, dt, offset=offset)

    xh = at("x_high", [P, NB, T], f32r, O_XH)
    xl = at("x_low", [P, NB, T], f32r, O_XL)
    xf = at("x_full", [P, NB, T], f32, O_XL)
    q = at("mix", [P, NB, 2, T], f32r, O_Q)
    qf = at("mix_full", [P, NB, BLK], f32, O_Q)
    mem = at("mem", [P, 2, NB, NMEM], f32r, O_KV + 16384)
    memf = at("mem_full", [P, 2, NB, NMEM], f32, O_KV + 16384)
    raw = at("w_raw", [P, 2, SLAB], f32, O_W)
    raw_slots = [raw[:, b, :].rearrange("p (a n) -> p a n", a=2) for b in range(2)]
    raw_slots += [qf[:, b:b + 2, BLK - SLAB // 2:BLK] for b in (CB, CB + 2)]
    wh = at("w_high", [P, 2, SLAB], f32r, O_W + 2 * SLAB * 4)
    wl = at("w_low", [P, 2, SLAB], f32r, O_W + 4 * SLAB * 4)
    kh = at("k_high", [P, NB, NMEM], f32r, O_KV)
    kl = at("k_low", [P, NB, NMEM], f32r, O_KV + 8192)
    kf = at("k_full", [P, NB, NMEM], f32, O_KV + 8192)
    vh = at("v_high", [P, 2, D], f32r, O_KV + 16384)
    vl = at("v_low", [P, 2, D], f32r, O_KV + 24576)
    vf = at("v_full", [P, 2, D], f32, O_KV + 24576)
    s = at("scratch", [P, 4, T], f32, O_S)
    prob = at("prob", [P, 2, HEADS * NMEM], f32, O_S)
    pth = at("prob_t_high", [P, 2, 4, 2 * P], f32r, O_S + 8192)
    ptl = at("prob_t_low", [P, 2, 4, 2 * P], f32r, O_XH)
    qz = at("dec_q", [P, NB, SB, HEADS * ST], f32, O_XH + 2 * T * 4)
    dkv = at("dec_kv", [P, RING, D], f32, O_XH + 3 * T * 4)
    dprob = at("dec_prob", [HEADS * ST, SB, NMEM], f32, O_S)
    dpt = at("dec_prob_t", [P, SB, 2, HEADS * ST], f32, O_S + 8192)
    dout = at("dec_out", [P, 2, D], f32, O_XH)
    gsel = at("gn_select", [GROWS, GROWS, P // 2], f32, O_S + 2 * T * 4)
    acc = at("ffn_sum", [P, NB, T], f32, O_KV)
    relu = at("relu", [P, 2, T], f32, O_KV + NB * T * 4)
    s3 = at("ln3_scratch", [P, 4, T], f32, O_XH)
    par = at("params", [P, NPAR], f32, O_PAR)
    con = at("consts", [P, NCONST], f32, O_CON)
    small = at("small", [P, 80], f32, O_SMALL)
    ones = at("ones", [P, 1], f32, O_SMALL + 320)
    poolw = qf[:, CB - 1, BLK - PB * P:BLK]

    inv128, inv64, ident = con[:, 0:P], con[:, P:2 * P], con[:, 2 * P:3 * P]

    def col(name, i=0, n=1):
        c = COLS[name] + i
        return par[:, c:c + n] if isinstance(c, int) else par[:, bass.ds(c, n)]

    ps = [ctx.enter_context(nc.psum_tensor(f"bank{b}", [P, 512], f32)) for b in range(8)]

    sems = {}

    def sem(name):
        if name not in sems:
            sems[name] = ctx.enter_context(nc.semaphore(name))
        return sems[name]

    full = [sem(f"bank_full{b}") for b in range(8)]
    free = [sem(f"bank_free{b}") for b in range(8)]
    split_done, used = sem("split_done"), sem("slab_used")

    class Own:

        def __init__(self, eng, name):
            self.eng, self.sem, self.n = eng, sem(name), 0

        def done(self, ins):
            ins.then_inc(self.sem, 1)
            self.n += 1
            return self.n

        def wait(self, n=None):
            self.eng.wait_ge(self.sem, self.n if n is None else n)

        def link(self, ins):
            self.done(ins)
            self.wait()

    def conv_dec(i):
        return qf[:, i, EXT:EXT + SB * DEXT].rearrange("p (b n) -> p b n", b=SB)

    def pool_dec(g):
        return qf[:, CB + g, PEXT:PEXT + SB * DPEXT].rearrange("p (b n) -> p b n", b=SB)

    def by_request(ap):
        return ap.rearrange("p (b n) -> p b n", b=SB)

    def over_blocks(ap, n=NB):
        return ap.unsqueeze(1).broadcast_to([P, n, ap.shape[-1]])

    def slab_arrived(eng, stage, n, p, c, i, last=2):
        b = 3 * p + c
        if c == last:
            eng.wait_ge(used, n + 1)
        else:
            eng.wait_ge(full[b], FILLED[stage][b] + i + 1)
        return b

    def halves(w, p):
        return w[:, p, :].rearrange("p (a n) -> p a n", a=2)

    ctx.enter_context(nc.allow_non_contiguous_dma(reason="the state's rows are short"))
    block = ctx.enter_context(nc.Block())

    @block.sync
    def _(sp):
        def load(n, p):
            sp.dma_start(raw[:, p, :], slabs[bass.ds(n, 1)].rearrange("a p n -> p (a n)")).then_inc(sem(f"raw_in{p}"), 16)

        def load_once(out, in_, name):
            sp.dma_start(out, in_).then_inc(sem(name), 16)

        def load_x(i):
            f, a, z = PIECES[i]
            load_once(xf[:, f, a:z], xT[:, f, a:z], f"x_in{i}")

        load(0, 0)
        for i in range(4):
            load_x(i)
        load(1, 1)
        for i in range(4, len(PIECES)):
            load_x(i)
        load_once(par[:], params, "const_in")
        load_once(con[:], consts, "const_in")
        load_once(memf[:, 1], memT, "mem_in")
        for i in range(CB):
            load_once(conv_dec(i)[:, :, 0:CTX], conv_state[:, i], "conv_state_in")
        for g in range(PB):
            load_once(pool_dec(g)[:, :, 0:PCTX], pool_state[:, g], "pool_state_in")
        load_once(poolw, pool_w, "pool_w_in")
        def loads(lo, hi):
            with sp.Fori(lo // 2, hi // 2) as i:
                for p in range(2):
                    sp.wait_ge(split_done, 2 * i + p - 1)
                    load(2 * i + p, p)

        loads(2, S_K)
        for n in range(S_K, S_E1):
            k = (n - S_K) % 4
            if n < S_K + 2:
                sp.wait_ge(split_done, n - 1)
            elif n >= S_K + 4:
                sp.wait_ge(split_done, n - 3)
            sp.dma_start(raw_slots[k], slabs[n].rearrange("p (a n) -> p a n", a=2)).then_inc(sem(f"raw_in{k}"), 16)
        loads(S_E1, S_XO + 4)
        sp.wait_ge(sem("x_restored"), 2 * NB)
        for n in range(4 * SB):
            if n >= RING:
                sp.wait_ge(sem("dec_used"), n - RING + 1)
            sp.dma_start(dkv[:, n % RING, :], dec_kv[n]).then_inc(sem(f"dec_in{n % RING}"), 16)
        loads(S_XO + 4, NSLAB)
        for c, (a, z) in enumerate(CHUNKS):
            for h in range(2):
                sp.wait_ge(sem("x_norm"), NB * (6 + c) + 4 * (h + 1))
                f = slice(4 * h, 4 * h + 4)
                sp.dma_start(yT[:, f, a:z], xf[:, f, a:z]).then_inc(sem("y_out"), 16)
        sp.wait_ge(sem("y_out"), 96)
        sp.wait_ge(sem("k_out"), 16)
        sp.wait_ge(sem("v_out"), 16)
        for i in range(CB):
            sp.wait_ge(sem(f"conv_out{i}"), 32)
        for g in range(PB):
            sp.wait_ge(sem(f"pool_out{g}"), 32)

    @block.gpsimd
    def _(pool):
        high_done = sem("high_done")
        one = ones[:].broadcast_to([P, SLAB])
        pool.memset(ones[:], 1.0).then_inc(sem("one_set"), 1)
        pool.wait_ge(sem("one_set"), 1)

        def split(n, p, turn, others=0):
            pool.wait_ge(sem(f"raw_in{p}"), 16 * (turn + 1 - others // 4))
            if not (isinstance(n, int) and n < 2):
                pool.wait_ge(used, n - 1)
                pool.sem_inc(sem("slot_turned"), 1)
            pool.tensor_tensor(wh[:, p, :], raw[:, p, :], one, ALU.mult).then_inc(high_done, 1)
            pool.wait_ge(high_done, n + 1 - others)
            pool.tensor_tensor(wl[:, p, :], raw[:, p, :], wh[:, p, :].bitcast(f32), ALU.subtract).then_inc(split_done, 1)

        def splits(lo, hi):
            with pool.Fori(lo // 2, hi // 2) as i:
                for p in range(2):
                    split(2 * i + p, p, i, MEM_SLABS if lo >= S_E1 else 0)

        def restore(b):
            pool.tensor_tensor(xf[:, b, :], xh[:, b, :].bitcast(f32), xl[:, b, :].bitcast(f32), ALU.add)\
                .then_inc(sem("x_restored"), 1)

        def square_sum(n, *blocks):
            scr = s3 if n == 3 else s
            for j in blocks:
                pool.wait_ge(sem("ln_sq"), (NB - 1) * (n - 1) + j + 1)
                pool.tensor_tensor(scr[:, 1, :], scr[:, 1, :], scr[:, 3, :], ALU.add).then_inc(sem("ln_sq_used"), 1)

        def mix_low(b):
            pool.tensor_tensor(q[:, b, 1, :], qf[:, b, T:2 * T], q[:, b, 0, :].bitcast(f32), ALU.subtract)\
                .then_inc(sem("mix_low"), 1)

        split(0, 0, 0)
        split(1, 1, 0)
        pool.memset(qf[:, 0:CB, 0:CTX], 0.0).then_inc(sem("pad_done"), 1)
        pool.memset(qf[:, CB:NB, 0:PCTX], 0.0).then_inc(sem("pad_done"), 1)
        for i in range(CB):
            split(2 + 2 * i, 0, 1 + i)
            for b in range(6):
                pool.wait_ge(free[b], FREED["A"][b] + i + 1)
            pool.tensor_tensor(qf[:, i, CTX:EXT], s[:, 3, 0:TP], s[:, 2, 0:TP], ALU.mult).then_inc(sem("u_done"), 1)
            pool.tensor_tensor(conv_dec(i)[:, :, CTX:DEXT], by_request(s[:, 3, TP:T]), by_request(s[:, 2, TP:T]),
                               ALU.mult).then_inc(sem("u_done"), 1)
            split(3 + 2 * i, 1, 1 + i)
        splits(10, 12)
        with pool.Fori(0, MEM_SLABS // 4) as i:
            for k in range(4):
                p = k % 2
                for a in range(2):
                    pool.wait_ge(sem("mem_w_high"), 8 * i + 2 * k + a + 1)
                    pool.sem_inc(sem("slot_turned"), 1)
                    pool.tensor_tensor(halves(wl, p)[:, a], raw_slots[k][:, a], halves(wh, p)[:, a].bitcast(f32), ALU.subtract)\
                        .then_inc(split_done if a else sem("split_half"), 1)
        splits(28, 30)
        for g in range(PB):
            pool.wait_ge(sem("mix_high"), g + 1)
            mix_low(CB + g)
        for b in range(4):
            restore(b)
        split(30, 0, 15, MEM_SLABS)
        for b in range(4, NB):
            restore(b)
        split(31, 1, 15, MEM_SLABS)
        splits(32, 34)
        split(34, 0, 17, MEM_SLABS)
        pool.wait_ge(sem("gn_n"), CB)
        pool.memset(inv64, 1.0 / D).then_inc(sem("inv_d_set"), 1)
        square_sum(1, 1, 2)
        split(35, 1, 17, MEM_SLABS)
        square_sum(1, 3, 4, 5, 6)
        split(36, 0, 18, MEM_SLABS)
        split(37, 1, 18, MEM_SLABS)

        def ln_low(n):
            for c, (a, z) in enumerate(CHUNKS):
                for j in range(NB):
                    pool.wait_ge(sem("x_norm_high"), NB * (3 * (n - 1) + c) + j + 1)
                    pool.tensor_tensor(xl[:, j, a:z], xf[:, j, a:z], xh[:, j, a:z].bitcast(f32), ALU.subtract)\
                        .then_inc(sem("x_norm_low"), 1)

        ln_low(1)
        splits(38, 46)
        pool.wait_ge(used, S_XQ + 8)
        for b in range(NB):
            restore(b)
        pool.wait_ge(sem("x_restored"), NB + 3)
        pool.memset(qz[:], 0.0).then_inc(sem("dec_q_zero"), 1)
        pool.wait_ge(sem("dec_q_zero"), 1)
        pool.wait_ge(sem("q_low"), 24)
        for h in range(HEADS):
            part = [q[:, 2 * h:2 * h + 2, j, TP:T].bitcast(f32).rearrange("p f (n t) -> p f n t", n=SB) for j in range(2)]
            pool.tensor_tensor(qz[:, 2 * h:2 * h + 2, :, h * ST:(h + 1) * ST], part[0], part[1], ALU.add)\
                .then_inc(sem("dec_q"), 1)
        for b in (6, 7):
            pool.wait_ge(full[b], FILLED["ATT"][b] + 8)
        pool.memset(dout[:], 0.0).then_inc(sem("dec_zero"), 1)
        splits(46, 48)

        def splits_and_sums(n, n0, last):
            for j in range(2, 7):
                if n0 + 2 + j <= last:
                    split(n0 + 2 + j, j % 2, (n0 + 2 + j) // 2, MEM_SLABS)
                square_sum(n, *((1, 2) if j == 2 else (j,)))

        splits_and_sums(2, S_XO, S_FF)
        split(S_FF + 1, 1, S_FF // 2, MEM_SLABS)
        ln_low(2)
        splits(S_FF + 2, NSLAB - 4)
        splits_and_sums(3, NSLAB - NB, NSLAB - 1)
        for c, (a, z) in enumerate(CHUNKS):
            pool.wait_ge(sem("ln_mean_kept"), c + 1)
            pool.tensor_tensor(xf[:, 4:NB, a:z], xf[:, 4:NB, a:z], over_blocks(s3[:, 1, a:z], 4), ALU.subtract)\
                .then_inc(sem("ln_pool_centred"), 1)
            pool.wait_ge(sem("ln_pool_centred"), c + 1)
            pool.wait_ge(sem("ln_rstd"), c + 1)
            pool.tensor_tensor(xf[:, 6:NB, a:z], xf[:, 6:NB, a:z], over_blocks(s3[:, 2, a:z], 2), ALU.mult)\
                .then_inc(sem("ln_pool_scaled"), 1)

    @block.tensor
    def _(pe):
        def take(b, n):
            if not (isinstance(n, int) and n == 0):
                pe.wait_ge(free[b], n)

        def product(out, w_high, w_low, x_high, x_low, first, last):
            pe.matmul(out, w_high, x_high, start=first, stop=False)
            pe.matmul(out, w_high, x_low, start=False, stop=False)
            return pe.matmul(out, w_low, x_high, start=False, stop=last)

        def slab_chunk(stage, p, c, i, parts, a, z, ready, signal):
            b = 3 * p + c
            take(b, FREED[stage][b] + i)
            for k in range(NB):
                if ready:
                    ready(c, k)
                w = slice(k * P, (k + 1) * P)
                high, low = parts(k, a, z)
                last = product(ps[b][:, 0:z - a], wh[:, p, w], wl[:, p, w], high, low, k == 0, k == NB - 1)
            last.then_inc(signal, 1)

        def slab(stage, n, p, i, parts, ready=None, after=None):
            pe.wait_ge(split_done, n + 1)
            for c, (a, z) in enumerate(CHUNKS):
                slab_chunk(stage, p, c, i, parts, a, z, ready, used if c == 2 else full[3 * p + c])
                if after:
                    after(c)

        def pair_by_chunks(stage, n0, ready):
            for c, (a, z) in enumerate(CHUNKS):
                for p in range(2):
                    if c == 0:
                        pe.wait_ge(split_done, n0 + p + 1)
                    slab_chunk(stage, p, c, 0, x_parts, a, z, ready if p == 0 else None, used if c == 2 else full[3 * p + c])

        def last_pair(stage, n0, parts, n):
            slab(stage, n0, 0, 3, parts)
            slab(stage, n0 + 1, 1, 3, parts, after=lambda c: ln_stats(n, c - 1) if c else None)
            ln_stats(n, 2)

        def x_parts(k, a, z):
            return xh[:, k, a:z], xl[:, k, a:z]

        def q_parts(k, a, z):
            return q[:, k, 0, a:z], q[:, k, 1, a:z]

        def pairs(stage, n0, lo, hi, parts):
            with pe.Fori(lo, hi) as i:
                for p in range(2):
                    slab(stage, n0 + 2 * i + p, p, i, parts)

        def first_pair(stage, n0, parts, ready=None):
            for p in range(2):
                slab(stage, n0 + p, p, 0, parts, ready if p == 0 else None)

        def x_ready(c, k):
            for i, (f, a, _) in enumerate(PIECES):
                if (k, CHUNKS[c][0]) == (f.start, a):
                    pe.wait_ge(sem("x_low"), i + 1)

        first_pair("A", S_A, x_parts, ready=x_ready)
        pairs("A", S_A, 1, 4, x_parts)
        pairs("P", S_P, 0, 2, x_parts)

        pe.wait_ge(sem("mem_low"), 1)
        with pe.Fori(0, 4) as i:
            for p in range(2):
                pe.wait_ge(sem("split_half"), 2 * i + p + 1)
                take(3 * p, FREED["K"][3 * p] + i)
                for k in range(NB):
                    if k == 4:
                        pe.wait_ge(split_done, S_K + 2 * i + p + 1)
                    w = slice(k * P, (k + 1) * P)
                    last = product(ps[3 * p][:, 0:NMEM], wh[:, p, w], wl[:, p, w], mem[:, 0, k], mem[:, 1, k], k == 0, k == 7)
                last.then_inc(used, 1)

        for i in range(4):
            for p in range(2):
                pe.wait_ge(sem("split_half"), S_V - S_K + 2 * i + p + 1)
                for mt in range(2):
                    b = 3 * mt + i // 2
                    if p == 0 and i % 2 == 0:
                        take(b, FREED["V"][b])
                    m = slice(mt * P, (mt + 1) * P)
                    o = (i % 2) * 256
                    for k in range(4):
                        if mt == 0 and k == 2:
                            pe.wait_ge(split_done, S_V + 2 * i + p + 1)
                        w = slice(k * 256, (k + 1) * 256)
                        last = product(ps[b][:, o:o + 256], mem[:, 0, 4 * p + k, m], mem[:, 1, 4 * p + k, m],
                                       wh[:, p, w], wl[:, p, w], p == 0 and k == 0, p == 1 and k == 3)
                    if mt == 1:
                        last.then_inc(used, 1)
                    elif p == 1 and i % 2 == 1:
                        last.then_inc(full[b], 1)

        pe.wait_ge(sem("pool_w_in"), 16)
        for g in range(PB):
            pe.wait_ge(sem("delta_done"), 2 * (g + 1))
            for c, (a, z) in enumerate(CHUNKS):
                b = 3 * (g % 2) + c
                take(b, FREED["PM"][b] + g // 2)
                w = poolw[:, g * P:(g + 1) * P]
                zp = min(z, TP)
                last = pe.matmul(ps[b][:, 0:zp - a], w, qf[:, CB + g, PCTX + a:PCTX + zp], start=True, stop=True)
                if z > TP:
                    last = pe.matmul(ps[b][:, zp - a:z - a], w, pool_dec(g)[:, :, PCTX:DPEXT], start=True, stop=True)
                last.then_inc(full[b], 1)

        def half_slab(stage, n, p, turn, k0, after=None, blocks=(0, 1)):
            pe.wait_ge(split_done, n + 1)
            for m in blocks:
                for c, (a, z) in enumerate(CHUNKS):
                    b = 3 * m + c
                    take(b, FREED[stage][b] + turn)
                    for k in range(4):
                        w = slice((m * 4 + k) * P, (m * 4 + k + 1) * P)
                        last = product(ps[b][:, 0:z - a], wh[:, p, w], wl[:, p, w], *q_parts(k0 + k, a, z), k == 0, k == 3)
                    last.then_inc(used if b == 5 else full[b], 1)
                    if after and m == 1:
                        after(c)

        def gn_means(i):
            pe.wait_ge(sem("conv_kept"), i + 1)
            for c, (a, z) in enumerate(CHUNKS):
                u = 3 * i + c
                b = 6 + u % 2
                take(b, FREED["GM"][b] + u // 2)
                pe.matmul(ps[b][:, 0:z - a], inv64, qf[:, i, a:z], start=True, stop=True).then_inc(full[b], 1)

        def gn_variances(i):
            pe.wait_ge(sem("gn_sq"), i + 1)
            if i == 0:
                take(6, FREED["GV"][6])
            for c, (a, z) in enumerate(CHUNKS):
                row = 2 * (CB * c + i)
                w = col("half", GROWS - 2 - row, GROWS)
                last = pe.matmul(ps[6][0:GROWS, 0:z - a], w, qf[:, i, T + a:T + z], start=(i == 0 and c == 0),
                                 stop=(i == CB - 1 and c == 2))
            if i == CB - 1:
                last.then_inc(full[6], 1)

        def gn_spread(i):
            for c, (a, z) in enumerate(CHUNKS):
                u = 3 * i + c
                b = 6 + u % 2
                take(b, FREED["GT"][b] + u // 2)
                row = 2 * (CB * c + i)
                pe.matmul(ps[b][:, 0:z - a], gsel[:, row:row + 2, :], s[0:GROWS, 0, 0:z - a], start=True, stop=True).then_inc(full[b], 1)

        for i in range(CB - 1):
            gn_means(i)
        pe.wait_ge(sem("mix_low"), PB)
        half_slab("E1", S_E1, 0, 0, CB)
        half_slab("E1", S_E1 + 1, 1, 1, CB)
        half_slab("E1", S_E1 + 2, 0, 2, CB)
        gn_means(CB - 1)
        for i in range(CB):
            gn_variances(i)
        half_slab("E1", S_E1 + 3, 1, 3, CB, blocks=(0,))
        pe.wait_ge(sem("gn_select"), 1)
        pe.wait_ge(sem("gn_rstd"), 1)
        for i in range(CB):
            gn_spread(i)
        half_slab("E1", S_E1 + 3, 1, 3, CB, blocks=(1,))

        def ln_pivot(n):
            pe.wait_ge(sem("ln_y"), n)
            for c, (a, z) in enumerate(CHUNKS):
                b = 6 + c % 2
                take(b, FREED[f"C{n}"][b] + c // 2)
                pe.matmul(ps[b][:, 0:z - a], inv128, xf[:, 0, a:z], start=True, stop=True).then_inc(full[b], 1)

        def ln_stats(n, c):
            a, z = CHUNKS[c]
            src = s3 if n == 3 else s
            pe.wait_ge(sem("inv_d_set"), 1)
            pe.wait_ge(sem("ln_d7"), 3 * (n - 1) + c + 1)
            take(c, FREED[f"T{n}"][c])
            pe.matmul(ps[c][:, 0:z - a], inv64, src[:, 0, a:z], start=True, stop=False)
            pe.matmul(ps[c][:, 0:z - a], inv64, xf[:, NB - 1, a:z], start=False, stop=True).then_inc(full[c], 1)
            pe.wait_ge(sem("ln_sq7"), 3 * (n - 1) + c + 1)
            take(3 + c, FREED[f"T{n}"][3 + c])
            pe.matmul(ps[3 + c][:, 0:z - a], inv64, src[:, 1, a:z], start=True, stop=False)
            pe.matmul(ps[3 + c][:, 0:z - a], inv64, src[:, 3, a:z], start=False, stop=True).then_inc(full[3 + c], 1)

        pe.wait_ge(sem("mix_low"), PB + CB)
        half_slab("E2", S_E2, 0, 0, 0)
        ln_pivot(1)
        half_slab("E2", S_E2 + 1, 1, 1, 0)
        half_slab("E2", S_E2 + 2, 0, 2, 0)
        half_slab("E2", S_E2 + 3, 1, 3, 0, after=lambda c: ln_stats(1, c - 1) if c else None)
        ln_stats(1, 2)

        def x_normed(n):
            def ready(c, k):
                pe.wait_ge(sem("x_norm_low"), NB * (3 * (n - 1) + c) + k + 1)
            return ready

        pair_by_chunks("XQ", S_XQ, x_normed(1))
        pairs("XQ", S_XQ, 1, 4, x_parts)

        def scores(t):
            for h in range(HEADS):
                b = 2 * (t % 2) + h // 2
                if h % 2 == 0:
                    take(b, FREED["ATT"][b] + t // 2)
                o = (h % 2) * NMEM
                for k in range(2):
                    f = 2 * h + k
                    tok = slice(t * P, (t + 1) * P)
                    last = product(ps[b][:, o:o + NMEM], q[:, f, 0, tok], q[:, f, 1, tok], kh[:, f, :], kl[:, f, :],
                                   k == 0, k == 1)
                if h % 2 == 1:
                    last.then_inc(full[b], 1)

        def prob_transposes(i, hh):
            for t in range(2):
                pe.wait_ge(sem("prob_done"), 2 * i + t + 1)
                b = 4 + t
                take(b, FREED["ATT"][b] + 2 * i + hh)
                for j in range(4):
                    m = (4 * hh + j) * P
                    last = pe.transpose(ps[b][:, j * P:(j + 1) * P], prob[:, t, m:m + P], ident)
                last.then_inc(full[b], 1)

        def values(i, hh):
            pe.wait_ge(sem("prob_t_low"), 2 * (2 * i + hh) + 2)
            for f in range(4):
                b = 6 + f // 2
                if f % 2 == 0:
                    take(b, FREED["ATT"][b] + 2 * i + hh)
                for mt in range(2):
                    w = slice((4 * hh + f) * P, (4 * hh + f + 1) * P)
                    j = 2 * (f // 2) + mt
                    last = product(ps[b][:, (f % 2) * 2 * P:(f % 2 + 1) * 2 * P], vh[:, mt, w], vl[:, mt, w],
                                   pth[:, hh, j, :], ptl[:, hh, j, :], mt == 0, mt == 1)
                if f % 2 == 1:
                    last.then_inc(full[b], 1)

        pe.wait_ge(sem("q_low"), 24)
        pe.wait_ge(sem("kv_low"), 2)
        ROWS = HEADS * ST

        def dec_chunk(c):
            pe.wait_ge(sem(f"dec_in{c % RING}"), 16 * (c // RING + 1))
            return dkv[:, c % RING]

        def dec_scores(n):
            b = n % 4
            take(b, FREED["DEC"][b] + n // 4)
            for k in range(2):
                keys = dec_chunk(2 * n + k)
                for f in range(4):
                    last = pe.matmul(ps[b][0:ROWS, 0:NMEM], qz[:, 4 * k + f, n, :], keys[:, f * NMEM:(f + 1) * NMEM],
                                     start=(k == 0 and f == 0), stop=(k == 1 and f == 3))
                last.then_inc(sem("dec_used"), 1)

        def dec_transposes(n):
            b = 4 + n % 2
            take(b, FREED["DEC"][b] + n // 2)
            pe.wait_ge(sem("dec_prob"), n + 1)
            for mt in range(2):
                last = pe.transpose(ps[b][:, mt * ROWS:(mt + 1) * ROWS], dprob[:, n, mt * P:(mt + 1) * P],
                                    ident[0:ROWS, 0:ROWS])
            last.then_inc(sem("dec_pt_full"), 1)

        def dec_values(n):
            b = 0 if n % 2 else 6
            for j in range(2):
                take(b + j, FREED["DEC"][b + j] + n // 2 + (2 if n % 2 else 0))
            pe.wait_ge(sem("dec_pt"), n + 1)
            for mt in range(2):
                vals = dec_chunk(2 * SB + 2 * n + mt)
                for j in range(2):
                    last = pe.matmul(ps[b + j][0:ROWS, :], dpt[:, n, mt, :], vals[:, j * 512:(j + 1) * 512],
                                     start=(mt == 0), stop=(mt == 1))
                last.then_inc(sem("dec_used"), 1)

        def dec_pick(half):
            pe.wait_ge(sem("dec_o"), 8 * (half + 1))
            heads = ident.rearrange("p (n r) -> p n r", n=4)
            for f in range(NB):
                h = f // 2
                o = f * TS + half * TS // 2
                last = pe.matmul(ps[2][:, o:o + TS // 2], dout[:, half, f * P:(f + 1) * P],
                                 heads[:, :, h * ST:(h + 1) * ST], start=True, stop=True)
            last.then_inc(sem("dec_picked"), 1)

        scores(0)
        scores(1)
        for i in range(3):
            prob_transposes(i, 0)
            scores(2 * i + 2)
            prob_transposes(i, 1)
            values(i, 0)
            scores(2 * i + 3)
            values(i, 1)
        prob_transposes(3, 0)
        pe.wait_ge(sem("dec_q"), HEADS)
        dec_scores(0)
        prob_transposes(3, 1)
        values(3, 0)
        dec_scores(1)
        values(3, 1)
        for n in range(2, SB):
            dec_scores(n)
            dec_transposes(n - 2)
        dec_transposes(SB - 2)
        dec_values(0)
        dec_transposes(SB - 1)
        take(2, FREED["DEC"][2] + 2)
        for n in range(1, SB):
            dec_values(n)
            if n == SB // 2:
                dec_pick(0)
        dec_pick(1)

        pe.wait_ge(sem("o_low"), 2 * 8 + 1)
        first_pair("XO", S_XO, q_parts)
        ln_pivot(2)
        pairs("XO", S_XO, 1, 3, q_parts)
        last_pair("XO", S_XO + 6, q_parts, 2)

        for g in range(FFG):
            n0 = S_FF + g * 2 * GB
            if g == 0:
                pair_by_chunks("W10", n0, x_normed(2))
            else:
                first_pair(f"W1{g}", n0, x_parts)
            pairs(f"W1{g}", n0, 1, 4, x_parts)

            def hidden_ready(c, k, g=g):
                if k == 0:
                    pe.wait_ge(sem("hidden_low"), 24 * g + 21)
                if k == NB - 1:
                    pe.wait_ge(sem("hidden_low"), 24 * g + 21 + c + 1)

            first_pair(f"W2{g}", n0 + GB, q_parts, ready=hidden_ready)
            if g < FFG - 1:
                pairs(f"W2{g}", n0 + GB, 1, 4, q_parts)
            else:
                ln_pivot(3)
                pairs(f"W2{g}", n0 + GB, 1, 3, q_parts)
                last_pair(f"W2{g}", n0 + GB + 6, q_parts, 3)

    @block.scalar
    def _(act):
        own = Own(act, "act_own")

        for i, (f, a, z) in enumerate(PIECES):
            act.wait_ge(sem(f"x_in{i}"), 16)
            act.copy(xh[:, f, a:z], xf[:, f, a:z]).then_inc(sem("x_high"), 1)
        act.wait_ge(sem("mem_in"), 16)
        act.copy(mem[:, 0], memf[:, 1]).then_inc(sem("mem_high"), 1)

        def keep_conv(i):
            act.wait_ge(sem("conv_done"), i + 1)
            act.wait_ge(sem(f"conv_out{i}"), 32)
            act.copy(qf[:, i, 0:T], s[:, i % 2, :]).then_inc(sem("conv_kept"), 1)

        act.wait_ge(sem("const_in"), 32)
        for i in range(CB):
            if i >= 1:
                act.wait_ge(sem("u_done"), 2 * i)
            if i == CB - 1:
                keep_conv(0)
            for c, (a, z) in enumerate(CHUNKS):
                b = slab_arrived(act, "A", S_A + 2 * i, 0, c, i)
                act.activation(s[:, 3, a:z], ps[b][:, 0:z - a], ACT.Identity, bias=col("b_in", i)).then_inc(free[b], 1)
            for c, (a, z) in enumerate(CHUNKS):
                b = slab_arrived(act, "A", S_A + 2 * i + 1, 1, c, i)
                act.activation(s[:, 2, a:z], ps[b][:, 0:z - a], ACT.Sigmoid, bias=col("b_in", CB + i)).then_inc(free[b], 1)
            act.wait_ge(sem("u_done"), 2 * (i + 1))
            act.dma_start(conv_p[:, i], qf[:, i, EXT - CTX:EXT]).then_inc(sem(f"conv_out{i}"), 16)
            act.wait_ge(sem("conv_state_in"), 16 * CB)
            act.dma_start(conv_s[:, i], conv_dec(i)[:, :, ST:DEXT]).then_inc(sem(f"conv_out{i}"), 16)

        def pool_inputs(g):
            p, turn = g % 2, g // 2
            for c, (a, z) in enumerate(CHUNKS):
                b = slab_arrived(act, "P", S_P + g, p, c, turn)
                zp = min(z, TP)
                ins = act.activation(qf[:, CB + g, PCTX + a:PCTX + zp], ps[b][:, 0:zp - a], ACT.Identity,
                                     bias=col("b_in", 2 * CB + g))
                if z > TP:
                    own.done(ins)
                    ins = act.activation(pool_dec(g)[:, :, PCTX:DPEXT], by_request(ps[b][:, zp - a:z - a]),
                                         ACT.Identity, bias=col("b_in", 2 * CB + g))
                ins.then_inc(free[b], 1)
                if z > TP:
                    own.wait()
                    act.wait_ge(free[b], FREED["P"][b] + turn + 1)
            act.wait_ge(free[3 * p], FREED["P"][3 * p] + turn + 1)
            act.wait_ge(free[3 * p + 1], FREED["P"][3 * p + 1] + turn + 1)
            act.wait_ge(sem("pool_state_in"), 16 * PB)
            act.dma_start(pool_p[:, g], qf[:, CB + g, PEXT - PCTX:PEXT]).then_inc(sem(f"pool_out{g}"), 16)
            act.dma_start(pool_s[:, g], pool_dec(g)[:, :, ST:DPEXT]).then_inc(sem(f"pool_out{g}"), 16)

        def slab_high(n):
            p, k, turn = n % 2, (n - S_K) % 4, (n - S_K) // 4
            before = S_K // 2 if k < 2 else 0
            act.wait_ge(sem(f"raw_in{k}"), 16 * (before + turn + 1))
            act.wait_ge(used, n - 1)
            for a in range(2):
                act.copy(halves(wh, p)[:, a], raw_slots[k][:, a]).then_inc(sem("mem_w_high"), 1)

        for g in range(PB - 1):
            pool_inputs(g)
        slab_high(S_K)
        pool_inputs(PB - 1)
        slab_high(S_K + 1)
        for j in range(NB):
            slab_high(S_K + 2 + j)
            b = slab_arrived(act, "K", S_K + j, j % 2, 0, j // 2, last=0)
            act.copy(kf[:, j, :], ps[b][:, 0:NMEM]).then_inc(sem("k_full"), 1)
            act.copy(kh[:, j, :], ps[b][:, 0:NMEM]).then_inc(free[b], 1)
        act.wait_ge(sem("k_full"), NB)
        act.dma_start(kT, kf[:]).then_inc(sem("k_out"), 16)
        for n in range(S_V + 2, S_E1):
            slab_high(n)
            if n == S_V + 5:
                keep_conv(1)
        act.wait_ge(used, S_E1)
        for b in (0, 1, 3, 4):
            mt, i = divmod(b, 3)
            if mt == 0:
                act.wait_ge(full[b], FILLED["V"][b] + 1)
            w = slice(i * 512, (i + 1) * 512)
            act.copy(vf[:, mt, w], ps[b][:]).then_inc(sem("v_full"), 1)
            act.copy(vh[:, mt, w], ps[b][:]).then_inc(free[b], 1)
        act.wait_ge(sem("v_full"), 4)
        act.dma_start(v_out, vf[:]).then_inc(sem("v_out"), 16)
        keep_conv(2)

        for g in range(PB):
            banks = [3 * (g % 2) + c for c in range(3)]
            act.wait_ge(full[banks[2]], FILLED["PM"][banks[2]] + g // 2 + 1)
            for c, (a, z) in enumerate(CHUNKS):
                b = banks[c]
                act.wait_ge(full[b], FILLED["PM"][b] + g // 2 + 1)
                act.activation(qf[:, CB + g, T + a:T + z], ps[b][:, 0:z - a], ACT.Copy, scale=col("pool_scale", g))\
                    .then_inc(free[b], 1)
            for b in banks:
                act.wait_ge(free[b], FREED["PM"][b] + g // 2 + 1)
            act.copy(q[:, CB + g, 0, :], qf[:, CB + g, T:2 * T]).then_inc(sem("mix_high"), 1)

        act.copy(gsel[:], ident[0:GROWS, 0:GROWS].unsqueeze(2).broadcast_to([GROWS, GROWS, P // 2])).then_inc(sem("gn_select"), 1)
        for i in range(CB):
            if i == CB - 1:
                keep_conv(3)
            act.wait_ge(sem("gn_d"), 3 * (i + 1))
            act.activation(qf[:, i, T:2 * T], qf[:, i, 0:T], ACT.Square).then_inc(sem("gn_sq"), 1)
        act.wait_ge(full[6], FILLED["GV"][6] + 1)
        act.activation(s[0:GROWS, 0, 0:CHUNKS[0][1]], ps[6][0:GROWS, 0:CHUNKS[0][1]], ACT.Sqrt, bias=par[0:GROWS, COLS["eps"]:COLS["eps"] + 1])\
            .then_inc(free[6], 1)
        for i in range(CB):
            act.wait_ge(sem("gn_n"), i + 1)
            act.activation(qf[:, i, T:2 * T], qf[:, i, 0:T], ACT.Silu, scale=col("gn_g", i), bias=col("gn_b", i))\
                .then_inc(sem("gn_out"), 1)
            act.wait_ge(sem("gn_out"), i + 1)
            act.copy(q[:, i, 0, :], qf[:, i, T:2 * T]).then_inc(sem("mix_high"), 1)

        def ln(n, scr):
            for c, (a, z) in enumerate(CHUNKS):
                b = 6 + c % 2
                act.wait_ge(full[b], FILLED[f"C{n}"][b] + c // 2 + 1)
                act.copy(scr[:, 2, a:z], ps[b][:, 0:z - a]).then_inc(free[b], 1)
            for j in range(NB - 1):
                act.wait_ge(sem("ln_d"), (NB - 1) * (n - 1) + j + 1)
                if j >= 2:
                    act.wait_ge(sem("ln_sq_used"), (NB - 2) * (n - 1) + j - 1)
                act.activation(scr[:, 3 if j else 1, :], xf[:, j, :], ACT.Square).then_inc(sem("ln_sq"), 1)
            act.wait_ge(sem("ln_sq_used"), (NB - 2) * n)

            def square(c):
                a, z = CHUNKS[c]
                act.wait_ge(sem("ln_d7"), 3 * (n - 1) + c + 1)
                act.activation(scr[:, 3, a:z], xf[:, NB - 1, a:z], ACT.Square).then_inc(sem("ln_sq7"), 1)

            def mean_square(c):
                a, z = CHUNKS[c]
                act.wait_ge(full[c], FILLED[f"T{n}"][c] + 1)
                act.activation(scr[:, 0, a:z], ps[c][:, 0:z - a], ACT.Square).then_inc(sem("ln_mean_sq"), 1)
                if n == 3:
                    act.wait_ge(full[3 + c], FILLED["T3"][3 + c] + 1)
                    act.copy(scr[:, 1, a:z], ps[c][:, 0:z - a]).then_inc(sem("ln_mean_kept"), 1)

            def std(c):
                a, z = CHUNKS[c]
                act.wait_ge(sem("ln_var"), 3 * (n - 1) + c + 1)
                act.activation(scr[:, 2, a:z], scr[:, 2, a:z], ACT.Sqrt, bias=col("eps")).then_inc(sem("ln_std"), 1)

            def affine(c, half):
                a, z = CHUNKS[c]
                for j in range(4 * half, 4 * half + 5):
                    if j < 4 * half + 4:
                        if n == 3 and j == 6:
                            act.wait_ge(sem("ln_pool_scaled"), c + 1)
                        elif j % 2 == 0:
                            act.wait_ge(sem("ln_scaled"), (4 if n < 3 else 3) * c + 12 * (n - 1) + j // 2 + 1)
                        act.activation(xf[:, j, a:z], xf[:, j, a:z], ACT.Identity, scale=col(f"ln{n}_g", j),
                                       bias=col(f"ln{n}_b", j)).then_inc(sem("x_norm"), 1)
                    if j > 4 * half and n < 3:
                        act.wait_ge(sem("x_norm"), NB * (3 * (n - 1) + c) + j)
                        act.copy(xh[:, j - 1, a:z], xf[:, j - 1, a:z]).then_inc(sem("x_norm_high"), 1)

            square(0)
            square(1)
            mean_square(0)
            std(0)
            square(2)
            for c in range(3):
                if c < 2:
                    mean_square(c + 1)
                affine(c, 0)
                if c < 2:
                    std(c + 1)
                affine(c, 1)

        ln(1, s)

        with act.Fori(0, 4) as i:
            for p in range(2):
                for c, (a, z) in enumerate(CHUNKS):
                    b = slab_arrived(act, "XQ", S_XQ + 2 * i + p, p, c, i)
                    act.copy(q[:, bass.ds(2 * i + p, 1), 0, a:z], ps[b][:, 0:z - a].unsqueeze(1)).then_inc(sem("q_high"), 1)

        def prob_exp(t):
            for h in range(HEADS):
                if h % 2 == 0:
                    act.wait_ge(sem("neg_max"), 2 * t + h // 2 + 1)
                b = 2 * (t % 2) + h // 2
                if t >= 2 and h == 0:
                    f = 4 + t % 2
                    act.wait_ge(full[f], FILLED["ATT"][f] + 2 * (t // 2))
                ins = act.activation(prob[:, t % 2, h * NMEM:(h + 1) * NMEM], ps[b][:, (h % 2) * NMEM:(h % 2 + 1) * NMEM],
                                     ACT.Exp, bias=small[:, 8 * (t % 2) + h:8 * (t % 2) + h + 1], scale=SCALE,
                                     accum_out=small[:, 16 + 8 * (t % 2) + h:16 + 8 * (t % 2) + h + 1])
                ins.then_inc(sem("exp_done"), 1)
                if h % 2:
                    act.wait_ge(sem("exp_done"), 4 * t + h + 1)
                    act.sem_inc(free[b], 1)

        def prob_t_high(i, hh):
            for t in range(2):
                b = 4 + t
                act.wait_ge(full[b], FILLED["ATT"][b] + 2 * i + hh + 1)
                if i:
                    act.wait_ge(full[7], FILLED["ATT"][7] + 2 * i + hh - 1)
                act.copy(pth[:, hh, :, t * P:(t + 1) * P], ps[b][:].rearrange("p (j n) -> p j n", j=4))\
                    .then_inc(sem("prob_t_high"), 1)

        def o_high(i, hh):
            for j in range(2):
                b = 6 + j
                act.wait_ge(full[b], FILLED["ATT"][b] + 2 * i + hh + 1)
                f = 4 * hh + 2 * j
                act.copy(q[:, f:f + 2, 0, 2 * P * i:2 * P * (i + 1)], ps[b][:].rearrange("p (j n) -> p j n", j=2))\
                    .then_inc(sem("o_high"), 1)

        prob_exp(0)
        prob_exp(1)
        for i in range(4):
            prob_t_high(i, 0)
            prob_t_high(i, 1)
            if i < 3:
                prob_exp(2 * i + 2)
            o_high(i, 0)
            if i < 3:
                prob_exp(2 * i + 3)
            o_high(i, 1)

        R = HEADS * ST

        def dec_prob_t(n):
            act.wait_ge(sem("dec_pt_full"), n + 1)
            b = 4 + n % 2
            act.copy(dpt[:, n], ps[b][:, 0:2 * R].rearrange("p (m r) -> p m r", m=2)).then_inc(sem("dec_pt"), 1)
            act.wait_ge(sem("dec_pt"), n + 1)
            act.sem_inc(free[b], 1)

        def dec_out(n):
            if n == 0:
                act.wait_ge(sem("dec_zero"), 1)
            act.wait_ge(sem("dec_used"), 2 * SB + 2 * (n + 1))
            b = 0 if n % 2 else 6
            for j in range(2):
                row = 32 * (n % 4)
                act.copy(dout[row:row + R, n // 4, j * 512:(j + 1) * 512], ps[b + j][0:R, :]).then_inc(sem("dec_o"), 1)
            act.wait_ge(sem("dec_o"), 2 * (n + 1))
            for j in range(2):
                act.sem_inc(free[b + j], 1)

        for n in range(SB):
            act.wait_ge(sem("dec_max"), n + 1)
            act.activation(dprob[:, n, :], ps[n % 4][0:R, 0:NMEM], ACT.Exp, bias=small[0:R, 48 + n:49 + n], scale=SCALE,
                           accum_out=small[0:R, 56 + n:57 + n]).then_inc(free[n % 4], 1)
            if n >= 2:
                dec_prob_t(n - 2)
        dec_prob_t(SB - 2)
        dec_out(0)
        dec_prob_t(SB - 1)
        for n in range(1, SB):
            dec_out(n)
        act.wait_ge(sem("dec_picked"), 2)
        act.copy(q[:, :, 0, TP:T], ps[2][:, 0:NMEM].rearrange("p (f n) -> p f n", n=TS)).then_inc(sem("o_high"), 1)

        ln(2, s)

        for g in range(FFG):
            stage, n0 = f"W1{g}", S_FF + g * 2 * GB
            for i in range(GB // 2):
                for p in range(2):
                    j = 2 * i + p
                    for c, (a, z) in enumerate(CHUNKS):
                        done = 24 * g + 3 * j + c
                        b = slab_arrived(act, stage, n0 + j, p, c, i)
                        if done >= 6:
                            act.wait_ge(sem("square"), done - 5)
                        act.activation(relu[:, p, a:z], ps[b][:, 0:z - a], ACT.Relu, bias=col("b1", GB * g + j))\
                            .then_inc(free[b], 1)
                        act.wait_ge(sem("square"), done + 1)
                        act.copy(q[:, j, 0, a:z], qf[:, j, T + a:T + z]).then_inc(sem("hidden_high"), 1)
        ln(3, s3)

    @block.vector
    def _(dve):
        own = Own(dve, "dve_own")
        stt, tt, ts = dve.scalar_tensor_tensor, dve.tensor_tensor, dve.tensor_scalar

        for i, (f, a, z) in enumerate(PIECES):
            dve.wait_ge(sem("x_high"), i + 1)
            tt(xl[:, f, a:z], xf[:, f, a:z], xh[:, f, a:z].bitcast(f32), ALU.subtract).then_inc(sem("x_low"), 1)
        dve.wait_ge(sem("mem_high"), 1)
        tt(mem[:, 1], memf[:, 1], mem[:, 0].bitcast(f32), ALU.subtract).then_inc(sem("mem_low"), 1)
        dve.wait_ge(sem("const_in"), 32)
        dve.wait_ge(sem("pad_done"), 2)

        def tap(i, k):
            out = s[:, i % 2, 0:TP]
            if k:
                return stt(out, qf[:, i, k:k + TP], col("conv_w", TAPS * i + k), out, ALU.mult, ALU.add)
            dve.wait_ge(sem("u_done"), 2 * (i + 1))
            if i >= 2:
                dve.wait_ge(sem("conv_kept"), i - 1)
            return ts(out, qf[:, i, 0:TP], col("conv_w", TAPS * i), col("conv_b", i), ALU.mult, ALU.add)

        def sample_conv(i):
            dve.wait_ge(sem("conv_state_in"), 16 * CB)
            w = col("conv_w", TAPS * i, TAPS).unsqueeze(1).broadcast_to([P, SB, TAPS])
            tmp = qf[:, i, EXT + SB * DEXT:EXT + SB * DEXT + SB * TAPS].rearrange("p (b n) -> p b n", b=SB)
            dst = by_request(s[:, i % 2, TP:T])
            for t in range(ST):
                own.link(tt(tmp, conv_dec(i)[:, :, t:t + TAPS], w, ALU.mult))
                own.link(dve.tensor_reduce(dst[:, :, t:t + 1], tmp, AX, ALU.add))
            ts(s[:, i % 2, TP:T], s[:, i % 2, TP:T], col("conv_b", i), None, ALU.add).then_inc(sem("conv_done"), 1)

        def conv(i, lo=0, hi=TAPS):
            for k in range(lo, hi):
                own.link(tap(i, k))
            if hi == TAPS:
                sample_conv(i)

        def conv_two(i, j):
            done = {}
            for k in range(TAPS):
                for b in (i, j):
                    if k:
                        own.wait(done[b])
                    done[b] = own.done(tap(b, k))
            own.wait()
            sample_conv(i)
            sample_conv(j)

        def window(g):
            dve.wait_ge(sem("pool_out%d" % g), 32)
            src, sdec = qf[:, CB + g, 0:PEXT], pool_dec(g)
            n, nd, w = PEXT, DPEXT, 1
            cur, cdec = src, sdec
            base = CB + g
            while w < WINDOWS[g]:
                j = 2 + (w.bit_length() - 1) % 2
                n, nd = n - w, nd - w
                nxt = s[:, j, 0:n]
                o = 1200 + 160 * (j - 2)
                ndec = qf[:, base, o:o + SB * nd].rearrange("p (b n) -> p b n", b=SB)
                tt(nxt, cur[:, w:w + n], cur[:, 0:n], ALU.add).then_inc(own.sem, 1)
                tt(ndec, cdec[:, :, w:w + nd], cdec[:, :, 0:nd], ALU.add).then_inc(own.sem, 1)
                own.n += 2
                own.wait()
                cur, cdec, w = nxt, ndec, 2 * w
            wn = WINDOWS[g]
            tok = qf[:, base, PCTX:PEXT]
            lead = PCTX - (wn - 1)
            head = small[:, 64:80]
            own.link(tt(head, cur[:, lead:lead + 16], col("ramp", 16 * g, 16), ALU.mult))
            own.link(tt(head, head, tok[:, 0:16], ALU.subtract))
            own.link(stt(tok, cur[:, lead:lead + TP], 1.0 / wn, tok, ALU.mult, ALU.subtract))
            own.link(dve.tensor_copy(tok[:, 0:16], head))
            dve.sem_inc(sem("delta_done"), 1)
            stt(sdec[:, :, PCTX:DPEXT], cdec[:, :, lead:lead + ST], 1.0 / wn, sdec[:, :, PCTX:DPEXT],
                ALU.mult, ALU.subtract).then_inc(sem("delta_done"), 1)

        def e1_join(j):
            dve.wait_ge(sem("x_restored"), j + 1)
            m, turn = j % 2, j // 2
            for c, (a, z) in enumerate(CHUNKS):
                b = 3 * m + c
                if b == 5:
                    dve.wait_ge(used, S_E1 + turn + 1)
                else:
                    dve.wait_ge(full[b], FILLED["E1"][b] + turn + 1)
                stt(xf[:, j, a:z], xf[:, j, a:z], ALPHA, ps[b][:, 0:z - a], ALU.mult, ALU.add).then_inc(free[b], 1)

        conv(0)
        conv_two(1, 2)
        for g in range(PB):
            window(g)

        def gn_centre(i):
            for c, (a, z) in enumerate(CHUNKS):
                u = 3 * i + c
                b = 6 + u % 2
                dve.wait_ge(full[b], FILLED["GM"][b] + u // 2 + 1)
                tt(qf[:, i, a:z], qf[:, i, a:z], ps[b][:, 0:z - a], ALU.subtract).then_inc(free[b], 1)
                dve.wait_ge(free[b], FREED["GM"][b] + u // 2 + 1)
                dve.sem_inc(sem("gn_d"), 1)

        conv(3, 0, 8)
        for i in range(CB - 1):
            gn_centre(i)
        conv(3, 8, 17)
        e1_join(0)
        e1_join(1)
        conv(3, 17, 23)
        e1_join(2)
        e1_join(3)
        conv(3, 23)
        gn_centre(CB - 1)
        e1_join(4)
        e1_join(5)
        dve.wait_ge(free[6], FREED["GV"][6] + 1)
        dve.reciprocal(s[0:GROWS, 0, 0:CHUNKS[0][1]], s[0:GROWS, 0, 0:CHUNKS[0][1]]).then_inc(sem("gn_rstd"), 1)
        e1_join(6)
        for i in range(CB):
            for c, (a, z) in enumerate(CHUNKS):
                u = 3 * i + c
                b = 6 + u % 2
                dve.wait_ge(full[b], FILLED["GT"][b] + u // 2 + 1)
                tt(qf[:, i, a:z], qf[:, i, a:z], ps[b][:, 0:z - a], ALU.mult).then_inc(free[b], 1)
            for u in (3 * i + 1, 3 * i + 2):
                dve.wait_ge(free[6 + u % 2], FREED["GT"][6 + u % 2] + u // 2 + 1)
            dve.sem_inc(sem("gn_n"), 1)
        for i in range(CB):
            dve.wait_ge(sem("mix_high"), PB + i + 1)
            tt(q[:, i, 1, :], qf[:, i, T:2 * T], q[:, i, 0, :].bitcast(f32), ALU.subtract).then_inc(sem("mix_low"), 1)
        e1_join(7)
        dve.wait_ge(sem("k_out"), 16)
        tt(kl[:], kf[:], kh[:].bitcast(f32), ALU.subtract).then_inc(sem("kv_low"), 1)
        dve.wait_ge(sem("v_out"), 16)
        for b in (0, 1, 3, 4):
            dve.wait_ge(free[b], FREED["V"][b] + 1)
        tt(vl[:], vf[:], vh[:].bitcast(f32), ALU.subtract).then_inc(sem("kv_low"), 1)

        def ln_block(n, scr, j):
            k = (NB - 1) * (n - 1) + j + 1
            if j == 0:
                for b, uses in LN_MEAN.items():
                    dve.wait_ge(free[b], FREED[f"C{n}"][b] + uses)
            tt(xf[:, j, :], xf[:, j, :], scr[:, 2, :], ALU.subtract).then_inc(sem("ln_d"), 1)
            dve.wait_ge(sem("ln_d"), k)
            if j == 0:
                own.link(dve.tensor_copy(scr[:, 0, :], xf[:, j, :]))
            else:
                own.link(tt(scr[:, 0, :], scr[:, 0, :], xf[:, j, :], ALU.add))

        def ln_last(n, scr, join):
            i0 = 3 * (n - 1)

            def pivoted(c):
                a, z = CHUNKS[c]
                join(c, a, z)
                tt(xf[:, NB - 1, a:z], xf[:, NB - 1, a:z], scr[:, 2, a:z], ALU.subtract).then_inc(sem("ln_d7"), 1)

            def variance(c):
                a, z = CHUNKS[c]
                dve.wait_ge(full[3 + c], FILLED[f"T{n}"][3 + c] + 1)
                dve.wait_ge(sem("ln_mean_sq"), i0 + c + 1)
                dve.wait_ge(sem("ln_d7"), i0 + c + 1)
                if n == 3:
                    dve.wait_ge(sem("ln_mean_kept"), c + 1)
                tt(scr[:, 2, a:z], ps[3 + c][:, 0:z - a], scr[:, 0, a:z], ALU.subtract).then_inc(free[3 + c], 1)
                dve.wait_ge(free[3 + c], FREED[f"T{n}"][3 + c] + 1)
                dve.sem_inc(sem("ln_var"), 1)

            def centre(c, h):
                a, z = CHUNKS[c]
                dve.wait_ge(full[c], FILLED[f"T{n}"][c] + 1)
                x4 = xf[:, 4 * h:4 * h + 4, a:z]
                ins = tt(x4, x4, over_blocks(ps[c][:, 0:z - a], 4), ALU.subtract)
                if h == 0:
                    own.done(ins)
                else:
                    ins.then_inc(free[c], 1)
                    dve.wait_ge(free[c], FREED[f"T{n}"][c] + 1)

            def scale(c, h):
                a, z = CHUNKS[c]
                for j in (4 * h, 4 * h + 2)[:1 if n == 3 and h == 1 else 2]:
                    x2 = xf[:, j:j + 2, a:z]
                    tt(x2, x2, over_blocks(scr[:, 2, a:z], 2), ALU.mult).then_inc(sem("ln_scaled"), 1)

            pivoted(0)
            pivoted(1)
            for c, (a, z) in enumerate(CHUNKS):
                variance(c)
                centre(c, 0)
                if c and n < 3:
                    centre(c, 1)
                if c == 0:
                    pivoted(2)
                dve.wait_ge(sem("ln_std"), i0 + c + 1)
                own.link(dve.reciprocal(scr[:, 2, a:z], scr[:, 2, a:z]))
                if n == 3:
                    own.wait()
                    dve.sem_inc(sem("ln_rstd"), 1)
                scale(c, 0)
                if c == 0 and n < 3:
                    centre(c, 1)
                if n == 3:
                    dve.wait_ge(sem("ln_pool_centred"), c + 1)
                scale(c, 1)

        def joins(arrived, freed, n, scr, add):
            def join(j, c, a, z):
                b = arrived(j, c)
                add(j, c, a, z, ps[b][:, 0:z - a]).then_inc(free[b], 1)
                return b

            for j in range(NB - 1):
                for c, (a, z) in enumerate(CHUNKS):
                    join(j, c, a, z)
                for c in range(3):
                    b = 3 * (j % 2) + c
                    dve.wait_ge(free[b], freed[b] + j // 2 + 1)
                if j == 0:
                    dve.sem_inc(sem("ln_y"), 1)
                if j == 2:
                    ln_block(n, scr, 0)
                    ln_block(n, scr, 1)
                if j >= 2:
                    ln_block(n, scr, j)

            def join_last(c, a, z):
                b = join(NB - 1, c, a, z)
                dve.wait_ge(free[b], freed[b] + (NB - 1) // 2 + 1)

            ln_last(n, scr, join_last)

        def e2_arrived(j, c):
            b = 3 * (j % 2) + c
            if b == 5:
                dve.wait_ge(used, S_E2 + j // 2 + 1)
            else:
                dve.wait_ge(full[b], FILLED["E2"][b] + j // 2 + 1)
            return b

        joins(e2_arrived, FREED["E2"], 1, s, lambda j, c, a, z, y: tt(xf[:, j, a:z], xf[:, j, a:z], y, ALU.add))

        with dve.Fori(0, 4) as i:
            for p in range(2):
                for c, (a, z) in enumerate(CHUNKS):
                    b = 3 * p + c
                    dve.wait_ge(sem("q_high"), 6 * i + 3 * p + c + 1)
                    f = bass.ds(2 * i + p, 1)
                    tt(q[:, f, 1, a:z], ps[b][:, 0:z - a].unsqueeze(1), q[:, f, 0, a:z].bitcast(f32), ALU.subtract)\
                        .then_inc(free[b], 1)
        for b in range(6):
            dve.wait_ge(free[b], FREED["XQ"][b] + 4)
        dve.sem_inc(sem("q_low"), 24)

        def maxes(t):
            if t >= 2:
                dve.wait_ge(sem("exp_done"), 4 * (t - 1))
            for j in range(2):
                b = 2 * (t % 2) + j
                dve.wait_ge(full[b], FILLED["ATT"][b] + t // 2 + 1)
                top = small[:, 8 * (t % 2) + 2 * j:8 * (t % 2) + 2 * j + 2]
                own.link(dve.reduce_max(top, ps[b][:].rearrange("p (h m) -> p h m", h=2), AX))
                ts(top, top, -SCALE, None, ALU.mult).then_inc(sem("neg_max"), 1)

        def normalise(t):
            for j in range(2):
                dve.wait_ge(sem("exp_done"), 4 * t + 2 * j + 2)
                o = 8 * (t % 2) + 2 * j
                own.link(dve.reciprocal(small[:, 32 + o:34 + o], small[:, 16 + o:18 + o]))
                for h in (2 * j, 2 * j + 1):
                    head = prob[:, t % 2, h * NMEM:(h + 1) * NMEM]
                    own.done(ts(head, head, small[:, 32 + o + h % 2:33 + o + h % 2], None, ALU.mult))
            own.wait()
            dve.sem_inc(sem("prob_done"), 1)

        def prob_t_low(i, hh):
            for t in range(2):
                b = 4 + t
                dve.wait_ge(sem("prob_t_high"), 2 * (2 * i + hh) + t + 1)
                tt(ptl[:, hh, :, t * P:(t + 1) * P], ps[b][:].rearrange("p (j n) -> p j n", j=4),
                   pth[:, hh, :, t * P:(t + 1) * P].bitcast(f32), ALU.subtract).then_inc(free[b], 1)
                dve.wait_ge(free[b], FREED["ATT"][b] + 2 * i + hh + 1)
                dve.sem_inc(sem("prob_t_low"), 1)

        def o_low(i, hh):
            for j in range(2):
                b = 6 + j
                dve.wait_ge(sem("o_high"), 2 * (2 * i + hh) + j + 1)
                f, tok = 4 * hh + 2 * j, slice(2 * P * i, 2 * P * (i + 1))
                tt(q[:, f:f + 2, 1, tok], ps[b][:].rearrange("p (j n) -> p j n", j=2),
                   q[:, f:f + 2, 0, tok].bitcast(f32), ALU.subtract).then_inc(free[b], 1)
                dve.wait_ge(free[b], FREED["ATT"][b] + 2 * i + hh + 1)
                dve.sem_inc(sem("o_low"), 1)

        maxes(0)
        maxes(1)
        normalise(0)
        normalise(1)
        dve.wait_ge(sem("x_restored"), NB + 2)
        for i in range(4):
            prob_t_low(i, 0)
            if i < 3:
                maxes(2 * i + 2)
            prob_t_low(i, 1)
            if i < 3:
                normalise(2 * i + 2)
            o_low(i, 0)
            if i < 3:
                maxes(2 * i + 3)
                normalise(2 * i + 3)
            o_low(i, 1)

        R = HEADS * ST

        def dec_max(n):
            dve.wait_ge(sem("dec_used"), 2 * (n + 1))
            c = small[0:R, 48 + n:49 + n]
            own.link(dve.reduce_max(c, ps[n % 4][0:R, 0:NMEM], AX))
            ts(c, c, -SCALE, None, ALU.mult).then_inc(sem("dec_max"), 1)

        def dec_norm(n):
            b = n % 4
            dve.wait_ge(free[b], FREED["DEC"][b] + n // 4 + 1)
            own.link(dve.reciprocal(small[0:R, 64 + n:65 + n], small[0:R, 56 + n:57 + n]))
            ts(dprob[:, n, :], dprob[:, n, :], small[0:R, 64 + n:65 + n], None, ALU.mult).then_inc(sem("dec_prob"), 1)

        for n in range(SB):
            dec_max(n)
            if n:
                dec_norm(n - 1)
        dec_norm(SB - 1)
        dve.wait_ge(sem("o_high"), 17)
        tt(q[:, :, 1, TP:T], ps[2][:, 0:NMEM].rearrange("p (f n) -> p f n", n=TS), q[:, :, 0, TP:T].bitcast(f32),
           ALU.subtract).then_inc(free[2], 1)
        dve.wait_ge(free[2], FREED["DEC"][2] + 3)
        dve.sem_inc(sem("o_low"), 1)

        joins(lambda j, c: slab_arrived(dve, "XO", S_XO + j, j % 2, c, j // 2), FREED["XO"], 2, s,
              lambda j, c, a, z, y: stt(xf[:, j, a:z], xf[:, j, a:z], ALPHA, y, ALU.mult, ALU.add))

        for g in range(FFG):
            n0 = S_FF + g * 2 * GB
            for j in range(GB):
                p = j % 2
                for c, (a, z) in enumerate(CHUNKS):
                    done = 24 * g + 3 * j + c
                    dve.wait_ge(free[3 * p + c], FREED[f"W1{g}"][3 * p + c] + j // 2 + 1)
                    full_part = qf[:, j, T + a:T + z]
                    tt(full_part, relu[:, p, a:z], relu[:, p, a:z], ALU.mult).then_inc(sem("square"), 1)
                    dve.wait_ge(sem("hidden_high"), done + 1)
                    tt(q[:, j, 1, a:z], full_part, q[:, j, 0, a:z].bitcast(f32), ALU.subtract).then_inc(sem("hidden_low"), 1)
                if g == 0:
                    own.link(ts(acc[:, j, :], xh[:, j, :].bitcast(f32), ALPHA, col("b2", j), ALU.mult, ALU.add))
                    own.link(stt(acc[:, j, :], xl[:, j, :].bitcast(f32), ALPHA, acc[:, j, :], ALU.mult, ALU.add))
            if g < FFG - 1:
                for j in range(NB):
                    p, i = j % 2, j // 2
                    for c, (a, z) in enumerate(CHUNKS):
                        b = slab_arrived(dve, f"W2{g}", n0 + GB + j, p, c, i)
                        tt(acc[:, j, a:z], acc[:, j, a:z], ps[b][:, 0:z - a], ALU.add).then_inc(free[b], 1)
                for b in range(6):
                    dve.wait_ge(free[b], FREED[f"W2{g}"][b] + 4)
            else:
                joins(lambda j, c: slab_arrived(dve, f"W2{g}", n0 + GB + j, j % 2, c, j // 2), FREED[f"W2{g}"], 3, s3,
                      lambda j, c, a, z, y: tt(xf[:, j, a:z], acc[:, j, a:z], y, ALU.add))

    ctx.close()


def kernel(x_prompt, x_sample, mem_prompt, cache_mem_k, cache_mem_v, state_conv, state_pool,
           w_in, b_in, conv_w, conv_b, gn_g, gn_b, pool_w, pool_scale, w_out,
           ln1_g, ln1_b, xq_w, xk_w, xv_w, xo_w, ln2_g, ln2_b, w1, b1, w2, b2, ln3_g, ln3_b):
    import numpy as np
    import concourse.bacc as bacc
    from concourse import mybir as mb
    from concourse.bass_utils import run_bass_kernel_spmd as run

    def feature_major(a):
        a = np.asarray(a)
        return a.reshape(a.shape[0], -1, P).transpose(2, 1, 0)

    def blocks(w, k=NB):
        w = np.asarray(w)
        return w.reshape(k, P, -1, P).transpose(2, 1, 0, 3).reshape(-1, P, k * P)

    def paired(w):
        return blocks(w, 4).reshape(4, 2, P, 4 * P).transpose(0, 2, 1, 3).reshape(4, P, SLAB)

    x = np.concatenate([np.asarray(x_prompt).reshape(TP, D), np.asarray(x_sample).reshape(TS, D)])
    win = blocks(w_in[0])
    order = [n for i in range(CB) for n in (i, CB + i)]
    ff = []
    up, down = blocks(w1[0]), np.asarray(w2[0]).reshape(FFG, D, D)
    for g in range(FFG):
        ff += [up[g * GB:(g + 1) * GB], blocks(down[g])]
    wo = np.asarray(w_out[0])
    wv = np.asarray(xv_w[0]).reshape(2, 4, P, 4, 256).transpose(3, 0, 2, 1, 4).reshape(NB, P, SLAB)
    slabs = np.concatenate([win[order], win[8:12], blocks(xk_w[0]), wv,
                            paired(wo[D_CONV:]), paired(wo[:D_CONV]), blocks(xq_w[0]), blocks(xo_w[0])] + ff)
    cols = [np.asarray(conv_w[0]).reshape(TAPS, CB, P).transpose(2, 1, 0).reshape(P, -1)]
    for v in (b_in, conv_b, gn_g, gn_b, pool_scale, ln1_g, ln1_b, ln2_g, ln2_b, ln3_g, ln3_b, b1, b2):
        cols.append(np.asarray(v[0]).reshape(-1, P).T)
    ramp = np.array([[1.0 / min(t + 1, w) for t in range(16)] for w in WINDOWS], np.float32).reshape(1, -1)
    fixed = [np.repeat(ramp, P, 0), np.full((P, 1), EPS, np.float32),
             np.pad(np.repeat(np.eye(2, dtype=np.float32) / 64, 64, 0), ((0, 0), (GROWS - 2, GROWS - 2)))]
    params = np.concatenate(cols + fixed, axis=1)
    consts = np.concatenate([np.full((P, P), 1.0 / P, np.float32),
                             np.kron(np.eye(2, dtype=np.float32), np.full((64, 64), 1.0 / 64, np.float32)),
                             np.eye(P, dtype=np.float32)], axis=1)
    ck = np.asarray(cache_mem_k[0]).transpose(0, 2, 3, 1).reshape(SB, 2, 4, P, NMEM).transpose(0, 1, 3, 2, 4).reshape(-1, P, D)
    cv = np.asarray(cache_mem_v[0]).reshape(-1, P, D)
    state = lambda a, n: np.asarray(a[0]).transpose(2, 0, 1).reshape(-1, P, SB, n).transpose(1, 0, 2, 3)
    arrays = {
        "xT": feature_major(x), "memT": feature_major(np.asarray(mem_prompt)[0]), "slabs": slabs,
        "pool_w": np.asarray(pool_w[0]).transpose(1, 0, 2).reshape(P, -1), "params": params, "consts": consts,
        "conv_state": state(state_conv, CTX), "pool_state": state(state_pool, PCTX),
        "dec_kv": np.concatenate([ck, cv]),
    }
    outs = {"yT": (P, NB, T), "kT": (P, NB, NMEM), "v_out": (P, 2, D), "conv_p": (P, CB, CTX),
            "conv_s": (P, CB, SB, CTX), "pool_p": (P, PB, PCTX), "pool_s": (P, PB, SB, PCTX)}
    nc = bacc.Bacc("TRN2", target_bir_lowering=False, num_devices=1)
    args, fed = {}, {}
    for name, a in arrays.items():
        fed[name + "_in"] = np.ascontiguousarray(a)
        args[name] = nc.dram_tensor(name + "_in", a.shape, mb.dt.float32, kind="ExternalInput").ap()
    for name, shape in outs.items():
        args[name] = nc.dram_tensor(name + "_res", shape, mb.dt.float32, kind="ExternalOutput").ap()
    decoder_step(nc, **args)
    r = run(nc, [fed], core_ids=[0]).results[0]
    got = {name: np.asarray(r[name + "_res"]) for name in outs}

    y = got["yT"].transpose(2, 1, 0).reshape(T, D)
    k = got["kT"].transpose(2, 1, 0).reshape(1, 1, NMEM, HEADS, D // HEADS)
    v = got["v_out"].transpose(1, 0, 2).reshape(1, 1, NMEM, HEADS, D // HEADS)
    cp = got["conv_p"].transpose(2, 1, 0).reshape(1, 1, CTX, D_CONV)
    cs = got["conv_s"].transpose(2, 3, 1, 0).reshape(1, SB, CTX, D_CONV)
    pp = got["pool_p"].transpose(2, 1, 0).reshape(1, 1, PCTX, D - D_CONV)
    pss = got["pool_s"].transpose(2, 3, 1, 0).reshape(1, SB, PCTX, D - D_CONV)
    return (y[:TP].reshape(1, TP, D), y[TP:].reshape(SB, ST, D), k, v, cp, cs, pp, pss)
```
